# Optimizing a Trainium2 kernel written in Bass

```python
import math
import jax
import jax.numpy as jnp
from jax import lax
import numpy as np

D_MODEL = 1024
BATCH = 1
SEQ = 1024
DEPTH = 2
DEC_BATCH = 1
DEC_SEQ = 32
PAST_LEN = 1024

CHUNK = 64
Q_BLOCK = 128
N_EVEN = (DEPTH + 1) // 2
N_ODD = DEPTH // 2

MLA_HEADS = 8
MLA_Q_LORA = 256
MLA_KV_LORA = 128
MLA_NOPE = 64
MLA_ROPE = 32
MLA_V = 64
ROPE_THETA = 10000.0
MLA_SCALE = (MLA_NOPE + MLA_ROPE) ** -0.5

SWA_HEADS = 8
SWA_KV_HEADS = 2
SWA_HD = 64
WINDOW = 128
WINDOW_CHUNKS = WINDOW // CHUNK
SWA_SCALE = SWA_HD ** -0.5

DSA_HEADS = 8
DSA_KV_HEADS = 2
DSA_HD = 128
IDX_HEADS = 8
IDX_DIM = 64
TOPK_MAX = 256
DSA_SCALE = DSA_HD ** -0.5
IDX_W_SCALE = (IDX_HEADS * IDX_DIM) ** -0.5

EVEN_IN = MLA_Q_LORA + MLA_KV_LORA + MLA_ROPE + (SWA_HEADS + 2 * SWA_KV_HEADS) * SWA_HD
EVEN_OUT = MLA_HEADS * MLA_V + SWA_HEADS * SWA_HD
ODD_IN = (DSA_HEADS + 2 * DSA_KV_HEADS) * DSA_HD + IDX_HEADS * IDX_DIM + IDX_DIM + IDX_HEADS
ODD_OUT = DSA_HEADS * DSA_HD

D_FF = 2816
CONV_W = 3

REL_BUCKETS = 32
REL_MAX_DIST = 1024
REL_HEADS = 8

DN_ALPHA = (2.0 * DEPTH) ** 0.25
DN_BETA = (8.0 * DEPTH) ** -0.25
LN_EPS = 1e-5
RMS_EPS = 1e-6
NEG_INF = -1e30
F32 = jnp.float32

kernel_name = 'hybrid_streaming_encoder_step'

def split_cols(z, sizes):
    return jnp.split(z, np.cumsum(sizes)[:-1].tolist(), axis=-1)

def layer_norm(x, g, b):
    xf = x.astype(F32)
    mu = jnp.mean(xf, -1, keepdims=True)
    var = jnp.mean(jnp.square(xf - mu), -1, keepdims=True)
    return ((xf - mu) * lax.rsqrt(var + LN_EPS) * g.astype(F32) + b.astype(F32)).astype(x.dtype)

def rms_norm(x, g):
    xf = x.astype(F32)
    return (xf * lax.rsqrt(jnp.mean(jnp.square(xf), -1, keepdims=True) + RMS_EPS) * g.astype(F32)).astype(x.dtype)

def apply_rope(x, pos):
    half = x.shape[-1] // 2
    inv = jnp.power(ROPE_THETA, -jnp.arange(half, dtype=F32) / half)
    ang = pos.astype(F32)[:, None] * inv[None, :]
    cos, sin = jnp.cos(ang)[:, None, :], jnp.sin(ang)[:, None, :]
    xf = x.astype(F32)
    x1, x2 = xf[..., :half], xf[..., half:]
    return jnp.concatenate([x1 * cos - x2 * sin, x1 * sin + x2 * cos], -1).astype(x.dtype)

def rel_bucket(rel):
    nb = REL_BUCKETS // 2
    max_exact = nb // 2
    n = jnp.abs(rel)
    nf = jnp.maximum(n, 1).astype(F32)
    large = max_exact + (jnp.log(nf / max_exact) / math.log(REL_MAX_DIST / max_exact) * (nb - max_exact)).astype(jnp.int32)
    large = jnp.minimum(large, nb - 1)
    return jnp.where(rel > 0, nb, 0) + jnp.where(n < max_exact, n, large)

def sink_softmax(s, sink):
    m = jnp.maximum(jnp.max(s, -1, keepdims=True), sink)
    e = jnp.exp(s - m)
    return e / (jnp.sum(e, -1, keepdims=True) + jnp.exp(sink - m))

def over_query_blocks(fn, n_q):
    starts = jnp.arange(n_q // Q_BLOCK, dtype=jnp.int32) * Q_BLOCK
    out = jnp.swapaxes(lax.map(fn, starts), 0, 1)
    return out.reshape((out.shape[0], n_q) + out.shape[3:])

def dense_chunk_attn(q, k, v, q_pos, k_pos, scale):
    s = jnp.einsum('bqhd,bkhd->bhqk', q, k, preferred_element_type=F32) * scale
    vis = (k_pos[None, :] // CHUNK) <= (q_pos[:, None] // CHUNK)
    p = jax.nn.softmax(jnp.where(vis, s, NEG_INF), axis=-1)
    return jnp.einsum('bhqk,bkhd->bqhd', p.astype(v.dtype), v)

def swa_banded(q, k, v, sinks, rel_bias):
    B, S, Hq, hd = q.shape
    Hk = k.shape[2]
    G = Hq // Hk
    nc = S // CHUNK
    back = WINDOW_CHUNKS * CHUNK
    KB = back + CHUNK

    def band(t):
        tp = jnp.pad(t, ((0, 0), (back, 0), (0, 0), (0, 0))).reshape(B, nc + WINDOW_CHUNKS, CHUNK, Hk, hd)
        return jnp.concatenate([tp[:, j:j + nc] for j in range(WINDOW_CHUNKS + 1)], axis=2)

    kb, vb = band(k), band(v)
    qb = q.reshape(B, nc, CHUNK, Hk, G, hd)
    qi = jnp.arange(CHUNK, dtype=jnp.int32)
    kj = jnp.arange(KB, dtype=jnp.int32)
    rel = (kj[None, :] - back) - qi[:, None]
    bias = rel_bias[rel_bucket(rel)].astype(F32).reshape(CHUNK, KB, Hk, G).transpose(2, 3, 0, 1)
    kpos = jnp.arange(nc, dtype=jnp.int32)[:, None] * CHUNK - back + kj[None, :]
    s = jnp.einsum('bcqngd,bcjnd->bcngqj', qb, kb, preferred_element_type=F32) * SWA_SCALE + bias
    s = jnp.where((kpos >= 0)[None, :, None, None, None, :], s, NEG_INF)
    p = sink_softmax(s, sinks.astype(F32).reshape(Hk, G)[..., None, None])
    o = jnp.einsum('bcngqj,bcjnd->bcqngd', p.astype(v.dtype), vb)
    return o.reshape(B, S, Hq * hd)

def swa_dense(q, k, v, q_pos, k_pos, sinks, rel_bias):
    B, T, Hq, hd = q.shape
    Hk = k.shape[2]
    G = Hq // Hk
    L = k.shape[1]
    qc, kc = q_pos // CHUNK, k_pos // CHUNK
    vis = (kc[None, :] <= qc[:, None]) & (kc[None, :] >= qc[:, None] - WINDOW_CHUNKS) & (k_pos[None, :] >= 0)
    bias = rel_bias[rel_bucket(k_pos[None, :] - q_pos[:, None])].astype(F32).reshape(T, L, Hk, G).transpose(2, 3, 0, 1)
    s = jnp.einsum('bqngd,bjnd->bngqj', q.reshape(B, T, Hk, G, hd), k, preferred_element_type=F32) * SWA_SCALE + bias
    s = jnp.where(vis, s, NEG_INF)
    p = sink_softmax(s, sinks.astype(F32).reshape(Hk, G)[..., None, None])
    o = jnp.einsum('bngqj,bjnd->bqngd', p.astype(v.dtype), v)
    return o.reshape(B, T, Hq * hd)

def dsa_attend(q, qi, wi, k, v, ki, q_pos, k_pos, topk, rel_bias):
    B, Tq, Hq, hd = q.shape
    Hk = k.shape[2]
    G = Hq // Hk
    dots = jnp.einsum('bqhd,bkd->bqhk', qi, ki, preferred_element_type=F32)
    score = jnp.einsum('bqhk,bqh->bqk', jax.nn.relu(dots), wi.astype(F32))
    adm = (k_pos[None, :] // CHUNK) <= (q_pos[:, None] // CHUNK)
    score = jnp.where(adm[None], score, NEG_INF)
    _, idx = lax.top_k(score, topk)
    sel_pos = k_pos[idx]
    valid = (sel_pos // CHUNK) <= (q_pos[None, :, None] // CHUNK)
    kg = jax.vmap(lambda t, ii: t[ii])(k, idx)
    vg = jax.vmap(lambda t, ii: t[ii])(v, idx)
    bias = rel_bias[rel_bucket(sel_pos - q_pos[None, :, None])].astype(F32)
    bias = bias.reshape(B, Tq, topk, Hk, G).transpose(0, 3, 4, 1, 2)
    s = jnp.einsum('bqngd,bqjnd->bngqj', q.reshape(B, Tq, Hk, G, hd), kg, preferred_element_type=F32) * DSA_SCALE + bias
    s = jnp.where(valid[:, None, None], s, NEG_INF)
    p = jax.nn.softmax(s, axis=-1)
    o = jnp.einsum('bngqj,bqjnd->bqngd', p.astype(v.dtype), vg)
    return o.reshape(B, Tq, Hq * hd)

def conv_ffn(h, prev, w_in, conv_w, conv_b, w_out):
    T = h.shape[1]
    u = h @ w_in
    ue = jnp.concatenate([prev.astype(u.dtype), u], axis=1)
    y = conv_b
    for j in range(CONV_W):
        y = y + ue[:, j:j + T] * conv_w[j]
    a, g = jnp.split(y, 2, axis=-1)
    return (jax.nn.silu(g) * a) @ w_out, ue[:, ue.shape[1] - (CONV_W - 1):]

def mix_even(h, pos, past, past_len, i, W):
    B, T, _ = h.shape
    z = h @ W['w_in_even'][i]
    cq, ckv, kr, qs, ks, vs = split_cols(z, [MLA_Q_LORA, MLA_KV_LORA, MLA_ROPE, SWA_HEADS * SWA_HD,
                                             SWA_KV_HEADS * SWA_HD, SWA_KV_HEADS * SWA_HD])
    qa = (rms_norm(cq, W['g_q_lora'][i]) @ W['w_uq'][i]).reshape(B, T, MLA_HEADS, MLA_NOPE + MLA_ROPE)
    qa = jnp.concatenate([qa[..., :MLA_NOPE], apply_rope(qa[..., MLA_NOPE:], pos)], axis=-1)
    lat = rms_norm(ckv, W['g_kv_lora'][i])
    kpe = apply_rope(kr[:, :, None, :], pos)[:, :, 0, :]
    if past is None:
        lat_all, kpe_all, kpos = lat, kpe, pos
    else:
        lat_all = jnp.concatenate([past['mla_lat'][i], lat], axis=1)
        kpe_all = jnp.concatenate([past['mla_kpe'][i], kpe], axis=1)
        kpos = jnp.arange(lat_all.shape[1], dtype=jnp.int32)
    L = lat_all.shape[1]
    kv = (lat_all @ W['w_ukv'][i]).reshape(B, L, MLA_HEADS, MLA_NOPE + MLA_V)
    ka = jnp.concatenate([kv[..., :MLA_NOPE],
                          jnp.broadcast_to(kpe_all[:, :, None, :], (B, L, MLA_HEADS, MLA_ROPE))], axis=-1)
    va = kv[..., MLA_NOPE:]
    if past is None:
        def blk(s):
            return dense_chunk_attn(lax.dynamic_slice_in_dim(qa, s, Q_BLOCK, 1), ka, va,
                                    lax.dynamic_slice_in_dim(pos, s, Q_BLOCK), kpos, MLA_SCALE)
        oa = over_query_blocks(blk, T)
    else:
        oa = dense_chunk_attn(qa, ka, va, pos, kpos, MLA_SCALE)
    oa = oa.reshape(B, T, MLA_HEADS * MLA_V)
    qb = qs.reshape(B, T, SWA_HEADS, SWA_HD)
    kb = ks.reshape(B, T, SWA_KV_HEADS, SWA_HD)
    vb = vs.reshape(B, T, SWA_KV_HEADS, SWA_HD)
    sinks = W['swa_sinks'][i]
    if past is None:
        ob = swa_banded(qb, kb, vb, sinks, W['rel_bias'])
        keep = min(WINDOW, T)
        new_k, new_v = kb[:, T - keep:], vb[:, T - keep:]
    else:
        keep = past['swa_k'][i].shape[1]
        k_all = jnp.concatenate([past['swa_k'][i], kb], axis=1)
        v_all = jnp.concatenate([past['swa_v'][i], vb], axis=1)
        kp = jnp.arange(past_len - keep, past_len + T, dtype=jnp.int32)
        ob = swa_dense(qb, k_all, v_all, pos, kp, sinks, W['rel_bias'])
        new_k, new_v = k_all[:, T:], v_all[:, T:]
    out = jnp.concatenate([oa, ob], axis=-1) @ W['w_out_even'][i]
    return out, lat, kpe, new_k, new_v

def mix_odd(h, pos, past, j, W):
    B, T, _ = h.shape
    z = h @ W['w_in_odd'][j]
    q, k, v, qi, ki, wi = split_cols(z, [DSA_HEADS * DSA_HD, DSA_KV_HEADS * DSA_HD, DSA_KV_HEADS * DSA_HD,
                                         IDX_HEADS * IDX_DIM, IDX_DIM, IDX_HEADS])
    q = q.reshape(B, T, DSA_HEADS, DSA_HD)
    k = k.reshape(B, T, DSA_KV_HEADS, DSA_HD)
    v = v.reshape(B, T, DSA_KV_HEADS, DSA_HD)
    qi = qi.reshape(B, T, IDX_HEADS, IDX_DIM)
    wi = wi * IDX_W_SCALE
    if past is None:
        k_all, v_all, ki_all, kpos = k, v, ki, pos
    else:
        k_all = jnp.concatenate([past['dsa_k'][j], k], axis=1)
        v_all = jnp.concatenate([past['dsa_v'][j], v], axis=1)
        ki_all = jnp.concatenate([past['dsa_idx'][j], ki], axis=1)
        kpos = jnp.arange(k_all.shape[1], dtype=jnp.int32)
    topk = min(TOPK_MAX, k_all.shape[1] // 4)
    if past is None:
        def blk(s):
            sl = lambda t: lax.dynamic_slice_in_dim(t, s, Q_BLOCK, 1)
            return dsa_attend(sl(q), sl(qi), sl(wi), k_all, v_all, ki_all,
                              lax.dynamic_slice_in_dim(pos, s, Q_BLOCK), kpos, topk, W['rel_bias'])
        o = over_query_blocks(blk, T)
    else:
        o = dsa_attend(q, qi, wi, k_all, v_all, ki_all, pos, kpos, topk, W['rel_bias'])
    return o @ W['w_out_odd'][j], k, v, ki

def trunk(x, c, past, W):
    B, T, _ = x.shape
    past_len = 0 if past is None else past['mla_lat'].shape[2]
    pos = jnp.arange(T, dtype=jnp.int32) + past_len
    lats, kpes, sks, svs, dks, dvs, dis, convs = [], [], [], [], [], [], [], []
    for l in range(DEPTH):
        mod = (jax.nn.silu(c) @ W['w_ada'][l] + W['b_ada'][l])[:, None, :]
        sh_m, sc_m, g_m, sh_f, sc_f, g_f = jnp.split(mod, 6, axis=-1)
        h = x * (1 + sc_m) + sh_m
        if l % 2 == 0:
            out, lat, kpe, sk, sv = mix_even(h, pos, past, past_len, l // 2, W)
            lats.append(lat); kpes.append(kpe); sks.append(sk); svs.append(sv)
        else:
            out, dk, dv, di = mix_odd(h, pos, past, l // 2, W)
            dks.append(dk); dvs.append(dv); dis.append(di)
        x = layer_norm(DN_ALPHA * x + g_m * out, W['ln_mix_g'][l], W['ln_mix_b'][l])
        h = x * (1 + sc_f) + sh_f
        prev = jnp.zeros((B, CONV_W - 1, 2 * D_FF), x.dtype) if past is None else past['ffn_conv'][l]
        out, cs = conv_ffn(h, prev, W['ffn_w_in'][l], W['ffn_conv_w'][l], W['ffn_conv_b'][l], W['ffn_w_out'][l])
        convs.append(cs)
        x = layer_norm(DN_ALPHA * x + g_f * out, W['ln_ffn_g'][l], W['ln_ffn_b'][l])
    st = jnp.stack
    return x, st(lats), st(kpes), st(sks), st(svs), st(dks), st(dvs), st(dis), st(convs)

def setup_inputs(seed: int = 0) -> dict:
    key = jax.random.key(seed)
    keys = iter(jax.random.split(key, 48))
    nrm = lambda shape, scale: scale * jax.random.normal(next(keys), shape, F32)
    D = D_MODEL
    swa_keep = min(WINDOW, PAST_LEN)
    return {
        'x_prompt': nrm((BATCH, SEQ, D), 1.0),
        'x_sample': nrm((DEC_BATCH, DEC_SEQ, D), 1.0),
        'cache_mla_latent': nrm((N_EVEN, DEC_BATCH, PAST_LEN, MLA_KV_LORA), 1.0),
        'cache_mla_kpe': nrm((N_EVEN, DEC_BATCH, PAST_LEN, MLA_ROPE), 1.0),
        'cache_swa_k': nrm((N_EVEN, DEC_BATCH, swa_keep, SWA_KV_HEADS, SWA_HD), 1.0),
        'cache_swa_v': nrm((N_EVEN, DEC_BATCH, swa_keep, SWA_KV_HEADS, SWA_HD), 1.0),
        'cache_dsa_k': nrm((N_ODD, DEC_BATCH, PAST_LEN, DSA_KV_HEADS, DSA_HD), 1.0),
        'cache_dsa_v': nrm((N_ODD, DEC_BATCH, PAST_LEN, DSA_KV_HEADS, DSA_HD), 1.0),
        'cache_dsa_idx_k': nrm((N_ODD, DEC_BATCH, PAST_LEN, IDX_DIM), 1.0),
        'state_ffn_conv': nrm((DEPTH, DEC_BATCH, CONV_W - 1, 2 * D_FF), 1.0),
        'c_prompt': nrm((BATCH, D), 1.0),
        'c_sample': nrm((DEC_BATCH, D), 1.0),
        'rel_bias': nrm((REL_BUCKETS, REL_HEADS), 0.5),
        'w_ada': nrm((DEPTH, D, 6 * D), 0.5 * D ** -0.5),
        'b_ada': nrm((DEPTH, 6 * D), 0.02),
        'ln_mix_g': 1.0 + nrm((DEPTH, D), 0.05),
        'ln_mix_b': nrm((DEPTH, D), 0.02),
        'ln_ffn_g': 1.0 + nrm((DEPTH, D), 0.05),
        'ln_ffn_b': nrm((DEPTH, D), 0.02),
        'w_in_even': nrm((N_EVEN, D, EVEN_IN), D ** -0.5),
        'g_q_lora': 1.0 + nrm((N_EVEN, MLA_Q_LORA), 0.05),
        'g_kv_lora': 1.0 + nrm((N_EVEN, MLA_KV_LORA), 0.05),
        'w_uq': nrm((N_EVEN, MLA_Q_LORA, MLA_HEADS * (MLA_NOPE + MLA_ROPE)), MLA_Q_LORA ** -0.5),
        'w_ukv': nrm((N_EVEN, MLA_KV_LORA, MLA_HEADS * (MLA_NOPE + MLA_V)), MLA_KV_LORA ** -0.5),
        'swa_sinks': nrm((N_EVEN, SWA_HEADS), 1.0),
        'w_out_even': nrm((N_EVEN, EVEN_OUT, D), DN_BETA * EVEN_OUT ** -0.5),
        'w_in_odd': nrm((N_ODD, D, ODD_IN), D ** -0.5),
        'w_out_odd': nrm((N_ODD, ODD_OUT, D), DN_BETA * ODD_OUT ** -0.5),
        'ffn_w_in': nrm((DEPTH, D, 2 * D_FF), D ** -0.5),
        'ffn_conv_w': nrm((DEPTH, CONV_W, 2 * D_FF), CONV_W ** -0.5),
        'ffn_conv_b': nrm((DEPTH, 2 * D_FF), 0.02),
        'ffn_w_out': nrm((DEPTH, D_FF, D), DN_BETA * D_FF ** -0.5),
    }

def reference(x_prompt, x_sample, cache_mla_latent, cache_mla_kpe, cache_swa_k, cache_swa_v,
              cache_dsa_k, cache_dsa_v, cache_dsa_idx_k, state_ffn_conv, c_prompt, c_sample,
              rel_bias, w_ada, b_ada, ln_mix_g, ln_mix_b, ln_ffn_g, ln_ffn_b,
              w_in_even, g_q_lora, g_kv_lora, w_uq, w_ukv, swa_sinks, w_out_even,
              w_in_odd, w_out_odd, ffn_w_in, ffn_conv_w, ffn_conv_b, ffn_w_out):
    W = dict(rel_bias=rel_bias, w_ada=w_ada, b_ada=b_ada, ln_mix_g=ln_mix_g, ln_mix_b=ln_mix_b,
             ln_ffn_g=ln_ffn_g, ln_ffn_b=ln_ffn_b, w_in_even=w_in_even, g_q_lora=g_q_lora,
             g_kv_lora=g_kv_lora, w_uq=w_uq, w_ukv=w_ukv, swa_sinks=swa_sinks, w_out_even=w_out_even,
             w_in_odd=w_in_odd, w_out_odd=w_out_odd, ffn_w_in=ffn_w_in, ffn_conv_w=ffn_conv_w,
             ffn_conv_b=ffn_conv_b, ffn_w_out=ffn_w_out)
    past = dict(mla_lat=cache_mla_latent, mla_kpe=cache_mla_kpe, swa_k=cache_swa_k, swa_v=cache_swa_v,
                dsa_k=cache_dsa_k, dsa_v=cache_dsa_v, dsa_idx=cache_dsa_idx_k, ffn_conv=state_ffn_conv)
    y_prompt, p_lat, p_kpe, p_sk, p_sv, p_dk, p_dv, p_di, p_conv = trunk(x_prompt, c_prompt, None, W)
    y_sample, s_lat, s_kpe, s_sk, s_sv, s_dk, s_dv, s_di, s_conv = trunk(x_sample, c_sample, past, W)
    return (y_prompt, y_sample, p_lat, p_kpe, p_sk, p_sv, p_dk, p_dv, p_di, p_conv,
            s_lat, s_kpe, s_sk, s_sv, s_dk, s_dv, s_di, s_conv)


_drawn_inputs = setup_inputs


def setup_inputs(seed=0):
    import zlib

    import numpy as np

    out = dict(_drawn_inputs(seed))
    spreads = {}
    factors = {'cache_mla_latent': 8.0,
     'cache_mla_kpe': 8.0,
     'cache_dsa_k': 5.579,
     'cache_dsa_v': 4.521,
     'cache_dsa_idx_k': 5.136,
     'state_ffn_conv': 2.961,
     'rel_bias': 6.539,
     'g_q_lora': 8.0,
     'w_uq': 7.3,
     'swa_sinks': 25.294,
     'ffn_conv_b': 8.0}
    for name, (base, spread) in spreads.items():
        noise = np.random.default_rng([zlib.crc32(name.encode()), seed]).standard_normal(out[name].shape)
        drawn = base * np.exp(spread * noise) if base else spread * noise
        out[name] = jnp.asarray(drawn.astype(out[name].dtype))
    for name, factor in factors.items():
        out[name] = (out[name] * factor).astype(out[name].dtype)
    return out
```

```python
from contextlib import ExitStack, contextmanager

import numpy as np

import concourse.bass as bass
from concourse import mybir

F32 = mybir.dt.float32
ALU = mybir.AluOpType
ACT = mybir.ActivationFunctionType
AX = mybir.AxisListType

P = 128
D = 1024
KT = D // P
TP, TS = 1024, 32
N = TP + TS
NTOK = 3
NT = N // NTOK
PAST = 1024
CHUNK = 64
NEG = -1e30
TAKEN = -3e38
LN_EPS, RMS_EPS = 1e-5, 1e-6
ALPHA = float(np.float32(4.0 ** 0.25))
FF = 2816
FT = FF // P
HEADS = 8
MLA_SCALE = 96 ** -0.5
SWA_SCALE = 64 ** -0.5
DSA_SCALE = 128 ** -0.5
IDX_W_SCALE = (8 * 64) ** -0.5
TOPK = 256
NKEYS = TP + PAST + TS
SWA_COLS = TP + P + TS
REL_LEN = 1281
REL_BASE = 1151
BIAS_W = TP + P
EVEN_W = 1216
ODD_TILES = 15
VW = 256 + 8
SEQS = ((0, TP), (TP, N))


class Chain:

    def __init__(self, eng, sem):
        self.eng, self.sem, self.n, self.extra = eng, sem, 0, 0

    def link(self, ins, standing=None):
        ins.then_inc(self.sem, 1)
        self.n += 1
        self.eng.wait_ge(self.sem, self.extra + self.n)
        if standing:
            self.eng.sem_inc(standing, 1)

    @contextmanager
    def loop(self, rounds, per, first=0):
        with self.eng.Fori(first, rounds) as i:
            start = self.n
            self.extra = (i - first) * per if first else i * per
            yield i
            assert self.n == start + per, (self.n - start, per)
            self.extra = 0
        self.n = start + per * (rounds - first)


class Machine:

    def __init__(self, nc, ctx, dram):
        self.nc, self.ctx, self.d, self.held = nc, ctx, dram, []
        sb = self.sb
        self.xT = sb("xT", [P, KT, N])
        self.hT = sb("hT", [P, KT, N])
        self.mods = sb("mods", [P, 96, 2])
        self.lnp = sb("lnp", [P, 2, 4, KT])
        self.ones = sb("ones", [P, P])
        self.ident = sb("ident", [P, P])
        self.convp = sb("convp", [P, 2, FT, 8])
        self.convs = sb("convs", [P, 2, FT, 4])
        self.convo = sb("convo", [P, 2, FT, 8])
        self.sinks = sb("sinks", [P, HEADS])
        self.gq = sb("gq", [P, 3])
        self.negs = sb("negs", [P, 1])
        self.ps = ctx.enter_context(nc.psum_tensor("ps", [P, 8, 512], F32))
        self.biasd = nc.dram_tensor("rel_scratch", [HEADS, P, REL_LEN], F32, kind="Internal").ap()

    def sb(self, name, shape, ctx=None):
        return (ctx or self.ctx).enter_context(self.nc.sbuf_tensor("t_" + name, shape, F32))

    def sem(self, name):
        self.held.append(self.nc.alloc_semaphore(name=name))
        return self.held[-1]

    def recycle(self):
        self.nc.clear_and_free_semaphores(self.held)
        self.nc.all_engine_barrier()
        self.held = []


def spread(ap, k):
    return ap.unsqueeze(1).broadcast_to([ap.shape[0], k, ap.shape[1]])


def segments(t):
    out = []
    for s, (a, b) in enumerate(SEQS):
        lo, hi = max(a, t * NT), min(b, (t + 1) * NT)
        if lo < hi:
            out.append((s, lo - t * NT, hi - lo))
    return out


def toeplitz(m, j0, width):
    return bass.AP(m.biasd.tensor, REL_BASE - TP + j0,
                   [[REL_LEN - 1, P], [P * REL_LEN, HEADS], [1, width]])


def start_stage(m):
    nc, d, ps = m.nc, m.d, m.ps
    with ExitStack() as c:
        NB = 4
        G = 4
        ROUNDS = 96 // (G * NB)
        w = m.sb("wada", [P, NB, G, KT, P], c)
        bada = m.sb("bada", [P, 96, 2], c)
        cT = m.sb("cT", [P, KT, 2], c)
        csT = m.sb("csT", [P, KT, 2], c)
        onehot = m.sb("onehot", [32, REL_LEN], c)
        rel = m.sb("rel", [32, HEADS], c)
        relrow = m.sb("relrow", [HEADS, REL_LEN], c)
        par = m.sem("par_loaded")
        rel_in = m.sem("rel_loaded")
        x_in = m.sem("x_loaded")
        wl = [m.sem(f"wada_loaded{i}") for i in range(NB)]
        mod_done, mod_out = m.sem("mod_done"), m.sem("mod_out")
        silu = m.sem("c_silu")
        rel_mm, rel_ev, rel_st = m.sem("rel_mm"), m.sem("rel_ev"), m.sem("rel_stored")
        ch, modded = m.sem("start_chain"), m.sem("first_h")
        params = [(cT, "cT"), (bada, "bada"), (m.lnp, "lnp"), (m.ident, "ident"), (m.convp, "convp"),
                  (m.convs, "convs"), (m.sinks, "sinks"), (m.gq, "gq"), (m.ones, "ones")]
        with nc.Block() as block:
            @block.sync
            def _(sp):
                for tile, name in params:
                    sp.dma_start(tile[:], d[name]).then_inc(par, 16)
                for u in range(NB):
                    sp.dma_start(w[:, u], d["wada"][u]).then_inc(wl[u], 16)
                with sp.Fori(1, ROUNDS) as i:
                    for u in range(NB):
                        sp.wait_ge(mod_done, i * NB + (u - NB + 1))
                        sp.dma_start(w[:, u], d["wada"][bass.ds(i * NB + u, 1)]
                                     .rearrange("a p g k m -> (a p) g k m")).then_inc(wl[u], 16)

            @block.scalar
            def _(act):
                act.dma_start(onehot[:], d["onehot"]).then_inc(rel_in, 16)
                act.dma_start(rel[:], d["rel_bias"]).then_inc(rel_in, 16)
                act.dma_start(m.xT[:], d["xT"]).then_inc(x_in, 16)
                act.wait_ge(par, 16 * len(params))
                nc.scalar.activation(csT[:], cT[:], ACT.Silu).then_inc(silu, 1)
                act.wait_ge(rel_ev, 1)
                act.dma_start(m.biasd, spread(relrow[:], P)).then_inc(rel_st, 16)
                act.wait_ge(rel_st, 16)

            @block.tensor
            def _(pe):
                pe.wait_ge(rel_in, 32)
                for q in range(3):
                    n0, n1 = q * 512, min(REL_LEN, (q + 1) * 512)
                    mm = nc.tensor.matmul(ps[0:HEADS, 4 + q, 0:n1 - n0], rel[:], onehot[:, n0:n1],
                                          start=True, stop=True)
                mm.then_inc(rel_mm, 1)
                pe.wait_ge(silu, 1)

                def group(i, first):
                    for u in range(NB):
                        pe.wait_ge(wl[u], i * 16 + 16)
                        if not first:
                            pe.wait_ge(mod_out, i * NB + (u - NB + 1))
                        for g in range(G):
                            for k in range(KT):
                                mm = nc.tensor.matmul(ps[:, u, 2 * g:2 * g + 2], w[:, u, g, k], csT[:, k],
                                                      start=k == 0, stop=k == KT - 1)
                        mm.then_inc(mod_done, 1)
                group(0, True)
                with pe.Fori(1, ROUNDS) as i:
                    group(i, False)

            @block.vector
            def _(dve):
                nc.vector.memset(m.negs[:], TAKEN)
                dve.wait_ge(rel_mm, 1)
                flat = ps[0:HEADS, 4:7, :].rearrange("p a b -> p (a b)")
                nc.vector.tensor_copy(relrow[:], flat[:, 0:REL_LEN]).then_inc(rel_ev, 1)
                dve.wait_ge(par, 16 * len(params))
                with dve.Fori(0, ROUNDS) as i:
                    for u in range(NB):
                        dve.wait_ge(mod_done, i * NB + (u + 1))
                        at = bass.ds(i * (NB * G) + u * G, G)
                        ins = nc.vector.tensor_tensor(m.mods[:, at], ps[:, u, 0:2 * G].rearrange("p (g s) -> p g s", s=2),
                                                      bada[:, at], ALU.add)
                        ins.then_inc(mod_out, 1)
                dve.wait_ge(mod_out, ROUNDS * NB)
                for l in range(2):
                    for t0 in (8, 32):
                        at = m.mods[:, 48 * l + t0:48 * l + t0 + KT]
                        ins = nc.vector.tensor_scalar(at, at, 1.0, None, ALU.add)
                ins.then_inc(ch, 1)
                dve.wait_ge(ch, 1)
                dve.wait_ge(x_in, 16)
                modulate(m, nc.vector, 0, 0)
    return


def modulate(m, eng, layer, part, only=None):
    base = 48 * layer + 24 * part
    ins = None
    for k in range(KT) if only is None else [only]:
        for s, (a, b) in enumerate(SEQS):
            ins = eng.tensor_scalar(m.hT[:, k, a:b], m.xT[:, k, a:b], m.mods[:, base + 8 + k, s:s + 1],
                                    m.mods[:, base + k, s:s + 1], ALU.mult, ALU.add)
    return ins


def down_stage(m, tag, wd, rhs, kt, layer, part, ctx):
    nc, ps = m.nc, m.ps
    w = m.sb("wd" + tag, [P, 2, kt, P], ctx)
    wl = [m.sem(f"wd{tag}_loaded{u}") for u in range(2)]
    ready, added, scaled = m.sem(f"down{tag}_ready"), m.sem(f"down{tag}_added"), m.sem(f"down{tag}_scaled")
    gate = 48 * layer + 24 * part + 16
    BANKS = 2 * NTOK
    with nc.Block() as block:
        @block.sync
        def _(sp):
            for u in range(2):
                sp.dma_start(w[:, u], wd[u]).then_inc(wl[u], 16)
            with sp.Fori(1, KT // 2) as i:
                for u in range(2):
                    sp.wait_ge(ready, i * BANKS + (u - 1) * NTOK)
                    sp.dma_start(w[:, u], wd[bass.ds(i * 2 + u, 1)]
                                 .rearrange("a p k m -> (a p) k m")).then_inc(wl[u], 16)

        @block.tensor
        def _(pe):
            def tiles(i, first):
                for u in range(2):
                    pe.wait_ge(wl[u], i * 16 + 16)
                    for t in range(NTOK):
                        bank = u * NTOK + t
                        if not first:
                            pe.wait_ge(added, i * BANKS + (bank - BANKS + 1))
                        for k in range(kt):
                            mm = nc.tensor.matmul(ps[:, bank, 0:NT], w[:, u, k], rhs[:, k, t * NT:(t + 1) * NT],
                                                  start=k == 0, stop=k == kt - 1)
                        mm.then_inc(ready, 1)
            tiles(0, True)
            with pe.Fori(1, KT // 2) as i:
                tiles(i, False)

        @block.gpsimd
        def _(pool):
            for k in range(KT):
                nc.gpsimd.tensor_scalar(m.xT[:, k], m.xT[:, k], ALPHA, None, ALU.mult).then_inc(scaled, 1)

        @block.vector
        def _(dve):
            with dve.Fori(0, KT // 2) as i:
                for u in range(2):
                    dve.wait_ge(scaled, i * 2 + (u + 1))
                    for t in range(NTOK):
                        bank = u * NTOK + t
                        dve.wait_ge(ready, i * BANKS + (bank + 1))
                        for s, c0, cn in segments(t):
                            x = m.xT[:, bass.ds(i * 2 + u, 1), t * NT + c0:t * NT + c0 + cn] \
                                .rearrange("p a n -> p (a n)")
                            g = m.mods[:, bass.ds(i * 2 + (gate + u), 1), s:s + 1].rearrange("p a n -> p (a n)")
                            ins = nc.vector.scalar_tensor_tensor(x, ps[:, bank, c0:c0 + cn], g, x, ALU.mult, ALU.add)
                        ins.then_inc(added, 1)


def norm_stage(m, layer, part, final=False):
    nc, ps = m.nc, m.ps
    tag = f"{layer}{part}"
    centred, squared, summed = m.sem(f"ln{tag}_centred"), m.sem(f"ln{tag}_squared"), m.sem(f"ln{tag}_summed")
    mean, inv, root = m.sem(f"ln{tag}_mean"), m.sem(f"ln{tag}_inv"), m.sem(f"ln{tag}_root")
    ch, done, out = m.sem(f"ln{tag}_chain"), m.sem(f"ln{tag}_done"), m.sem(f"ln{tag}_stored")
    with ExitStack() as c:
        rs = m.sb("rs" + tag, [P, N], c)
        cols = [slice(t * NT, (t + 1) * NT) for t in range(NTOK)]
        with nc.Block() as block:
            @block.tensor
            def _(pe):
                for t in range(NTOK):
                    for k in range(KT):
                        mm = nc.tensor.matmul(ps[:, t, 0:NT], m.ones[:], m.xT[:, k, cols[t]],
                                              start=k == 0, stop=k == KT - 1)
                    mm.then_inc(mean, 1)
                for t in range(NTOK):
                    pe.wait_ge(squared, t + 1)
                    for k in range(KT):
                        mm = nc.tensor.matmul(ps[:, NTOK + t, 0:NT], m.ones[:], m.hT[:, k, cols[t]],
                                              start=k == 0, stop=k == KT - 1)
                    mm.then_inc(summed, 1)

            @block.scalar
            def _(act):
                for t in range(NTOK):
                    act.wait_ge(centred, t + 1)
                    nc.scalar.activation(m.hT[:, :, cols[t]], m.xT[:, :, cols[t]], ACT.Square).then_inc(squared, 1)
                for t in range(NTOK):
                    act.wait_ge(inv, t + 1)
                    nc.scalar.activation(rs[:, cols[t]], rs[:, cols[t]], ACT.Sqrt).then_inc(root, 1)
                if final:
                    for k in range(KT):
                        act.wait_ge(done, k + 1)
                        act.dma_start(m.d["yT"][:, k], m.xT[:, k]).then_inc(out, 16)
                    act.wait_ge(out, 16 * KT)

            @block.vector
            def _(dve):
                chain = Chain(dve, ch)
                for t in range(NTOK):
                    dve.wait_ge(mean, t + 1)
                    x = m.xT[:, :, cols[t]]
                    nc.vector.tensor_tensor(x, x, spread(ps[:, t, 0:NT], KT), ALU.subtract).then_inc(centred, 1)
                for t in range(NTOK):
                    dve.wait_ge(summed, t + 1)
                    chain.link(nc.vector.tensor_scalar(rs[:, cols[t]], ps[:, NTOK + t, 0:NT], LN_EPS, None, ALU.add))
                    nc.vector.reciprocal(rs[:, cols[t]], rs[:, cols[t]]).then_inc(inv, 1)
                dve.wait_ge(centred, NTOK)
                for t in range(NTOK):
                    dve.wait_ge(root, t + 1)
                    x = m.xT[:, :, cols[t]]
                    ins = nc.vector.tensor_tensor(x, x, spread(rs[:, cols[t]], KT), ALU.mult)
                chain.link(ins)
                for k in range(KT):
                    g, b = (m.lnp[:, layer, 2 * part + j, k:k + 1] for j in range(2))
                    ins = nc.vector.tensor_scalar(m.xT[:, k], m.xT[:, k], g, b, ALU.mult, ALU.add)
                    ins.then_inc(done, 1)
                if not final:
                    dve.wait_ge(done, KT)
                    modulate(m, nc.vector, layer + part, 1 - part)


def ffn_stage(m, layer):
    nc, ps, d = m.nc, m.ps, m.d
    PAD = 2
    UW = N + 2 * PAD
    S0 = TP + 2 * PAD
    YW = UW - PAD
    with ExitStack() as c:
        sT = m.sb(f"sT{layer}", [P, FT, N], c)
        with ExitStack() as ci:
            w = m.sb(f"wi{layer}", [P, 2, 2, KT, P], ci)
            u_ = m.sb(f"u{layer}", [P, 2, 2, UW], ci)
            y = m.sb(f"y{layer}", [P, 2, YW], ci)
            cp = m.sb(f"cp{layer}", [P, 2, 8], ci)
            wl = [m.sem(f"wi{layer}_loaded{b}") for b in range(2)]
            ready, moved, staged = m.sem(f"u{layer}_ready"), m.sem(f"u{layer}_moved"), m.sem(f"conv{layer}_staged")
            tap0, tap2, gated, used = (m.sem(f"{n}{layer}") for n in ("tap0_", "tap2_", "gated_", "u_used_"))
            kept, zeroed, ch, silu = (m.sem(f"{n}{layer}") for n in ("kept_", "zeroed_", "ffn_chain_", "silu_"))
            ROUNDS = FT // 2
            UNITS = 2 * NTOK
            with nc.Block() as block:
                @block.sync
                def _(sp):
                    for b in range(2):
                        sp.dma_start(w[:, b], d["wfi"][layer, b]).then_inc(wl[b], 16)
                    with sp.Fori(1, ROUNDS) as i:
                        for b in range(2):
                            sp.wait_ge(ready, i * (2 * UNITS) + (b - 1) * UNITS)
                            sp.dma_start(w[:, b], d["wfi"][layer, bass.ds(i * 2 + b, 1)]
                                         .rearrange("a p h k m -> (a p) h k m")).then_inc(wl[b], 16)

                @block.tensor
                def _(pe):
                    def pair(i, first, b):
                        pe.wait_ge(wl[b], i * 16 + 16)
                        for q in range(UNITS):
                            half, t = divmod(q, NTOK)
                            if not first:
                                pe.wait_ge(moved, i * (2 * UNITS) + (b - 1) * UNITS + (q + 1))
                            for k in range(KT):
                                mm = nc.tensor.matmul(ps[:, q, 0:NT], w[:, b, half, k],
                                                      m.hT[:, k, t * NT:(t + 1) * NT],
                                                      start=k == 0, stop=k == KT - 1)
                            mm.then_inc(ready, 1)
                    pair(0, True, 0)
                    pair(0, False, 1)
                    with pe.Fori(1, ROUNDS) as i:
                        pair(i, False, 0)
                        pair(i, False, 1)

                @block.gpsimd
                def _(pool):
                    for b in range(2):
                        nc.gpsimd.memset(u_[:, b, :, 0:PAD], 0.0).then_inc(zeroed, 1)

                    def stage(i, first, b):
                        j = i * 2 + b
                        if not first:
                            pool.wait_ge(gated, i * 2 + (b - 1))
                            pool.wait_ge(kept, i * 2 + (b - 1))
                        pick = (lambda t: t[:, layer, j]) if first else \
                            (lambda t: t[:, layer, bass.ds(j, 1)].rearrange("p a n -> p (a n)"))
                        nc.gpsimd.tensor_copy(cp[:, b], pick(m.convp))
                        nc.gpsimd.tensor_copy(u_[:, b, :, TP + PAD:S0],
                                              pick(m.convs).rearrange("p (h c) -> p h c", h=2)).then_inc(staged, 1)

                    def keep(i, first, b):
                        j = i * 2 + b
                        pool.wait_ge(moved, (j + 1) * UNITS if first else i * (2 * UNITS) + (b + 1) * UNITS)
                        pick = (lambda c0: m.convo[:, layer, j, c0:c0 + 4]) if first else \
                            (lambda c0: m.convo[:, layer, bass.ds(j, 1), c0:c0 + 4].rearrange("p a n -> p (a n)"))
                        for s, c0 in enumerate((TP, UW - PAD)):
                            ins = nc.gpsimd.tensor_copy(pick(4 * s).rearrange("p (h c) -> p h c", h=2),
                                                        u_[:, b, :, c0:c0 + PAD])
                        ins.then_inc(kept, 1)
                    for b in range(2):
                        stage(0, True, b)
                    for b in range(2):
                        keep(0, True, b)
                    with pool.Fori(1, ROUNDS) as i:
                        for b in range(2):
                            stage(i, False, b)
                        for b in range(2):
                            keep(i, False, b)

                @block.scalar
                def _(act):
                    act.wait_ge(zeroed, 2)

                    def pair(i, first, b):
                        act.wait_ge(staged, i * 2 + (b + 1))
                        for q in range(UNITS):
                            half, t = divmod(q, NTOK)
                            act.wait_ge(ready, i * (2 * UNITS) + b * UNITS + (q + 1))
                            for s, c0, cn in segments(t):
                                to = t * NT + c0 + PAD * (s + 1)
                                ins = nc.scalar.activation(u_[:, b, half, to:to + cn], ps[:, q, c0:c0 + cn], ACT.Copy)
                            ins.then_inc(moved, 1)
                        act.wait_ge(moved, i * (2 * UNITS) + (b + 1) * UNITS)
                        if not (first and b == 0):
                            act.wait_ge(gated, i * 2 + b)
                        for half in range(2):
                            nc.scalar.activation(y[:, half], u_[:, b, half, 0:YW], ACT.Identity,
                                                 bias=cp[:, b, 4 * half + 3:4 * half + 4],
                                                 scale=cp[:, b, 4 * half:4 * half + 1]).then_inc(tap0, 1)
                        act.wait_ge(tap2, i * 2 + (b + 1))
                        nc.scalar.activation(y[:, 1], y[:, 1], ACT.Silu).then_inc(silu, 1)
                    pair(0, True, 0)
                    pair(0, True, 1)
                    with act.Fori(1, ROUNDS) as i:
                        pair(i, False, 0)
                        pair(i, False, 1)

                @block.vector
                def _(dve):
                    chain = Chain(dve, ch)

                    def pair(i, first, b):
                        dve.wait_ge(tap0, i * 4 + 2 * (b + 1))
                        for tap in (1, 2):
                            for half in (1, 0):
                                ins = nc.vector.scalar_tensor_tensor(
                                    y[:, half], u_[:, b, half, tap:tap + YW], cp[:, b, 4 * half + tap:4 * half + tap + 1],
                                    y[:, half], ALU.mult, ALU.add)
                                if (tap, half) == (2, 1):
                                    ins.then_inc(tap2, 1)
                                else:
                                    chain.link(ins)
                        dve.wait_ge(silu, i * 2 + (b + 1))
                        for s, (a, e) in enumerate(SEQS):
                            to = sT[:, bass.ds(i * 2 + b, 1), a:e].rearrange("p a n -> p (a n)")
                            ins = nc.vector.tensor_tensor(to, y[:, 0, a + PAD * s:e + PAD * s],
                                                          y[:, 1, a + PAD * s:e + PAD * s], ALU.mult)
                        ins.then_inc(gated, 1)
                    with chain.loop(ROUNDS, 6) as i:
                        pair(i, False, 0)
                        pair(i, False, 1)
        down_stage(m, f"f{layer}", d["wfo"][layer], sT, FT, layer, 1, c)


class Keys:

    def __init__(self, q0, nq, key_tiles, single=False):
        self.q0, self.nq, self.tiles = q0, nq, key_tiles
        self.nk = sum(t[1] for t in key_tiles)
        self.single = single
        self.s_bank = (0, 3) if single else (0, 2)
        self.t_banks = (6,) if single else (4, 5)
        self.o_banks = (7, 7) if single else (6, 7)
        self.per = 16 if single else 4
        self.groups = -(-len(key_tiles) // self.per)

    def offsets(self):
        at, out = 0, []
        for col, size, v in self.tiles:
            out.append((at, size, v))
            at += size
        return out

    def bank(self, ps, u, width=None):
        b = self.s_bank[u]
        return ps[0:self.nq, b:b + 3 if self.single else b + 2, :].rearrange("p a b -> p (a b)")[:, 0:self.nk]


def attention_stage(m, tag, blocks, kind, q_of, k_of, v_of, dv, rows, out_tile, bias_w=0, bias_of=None,
                    sink=False, select=None, out=None):
    nc, ps = m.nc, m.ps
    out = m.hT if out is None else out
    names = ("q_staged", "s_ready", "s_free", "max_ready", "p_ready", "t_ready", "t_moved", "o_ready", "o_moved",
             "inv_ready", "chain") + ("pchain", "turns", "pool_turns") * bool(bias_w) + \
        ("mask_ready", "idx_ready", "relu_ready", "relu_free") * bool(select)
    S = {n: m.sem(f"{tag}_{n}") for n in names}
    c = ExitStack()
    with c:
        qst = m.sb(tag + "qst", [P, 2, P], c)
        prob = m.sb(tag + "prob", [P, 2, max(kb.nk for kb, _ in blocks)], c)
        probT = m.sb(tag + "probT", [P, 2, max(len(kb.tiles) * kb.nq for kb, _ in blocks)], c)
        osb = m.sb(tag + "osb", [P, HEADS * dv], c)
        stat = m.sb(tag + "stat", [P, 2, 8], c)
        bm = m.sb(tag + "bm", [P, 2, bias_w], c) if bias_w else None
        if select:
            score = m.sb(tag + "score", [P, N], c)
            work = m.sb(tag + "work", [P, N], c)
            relu = prob
            best = m.sb(tag + "best", [P, 8], c)
        OT = HEADS * dv // P
        first_block = blocks[0][0] is not None

        plan, g, sel_n = [], 0, 0
        for n, (kb, b) in enumerate(blocks):
            og = -(-OT // 4)
            sel = select and kb.nk > TOPK
            plan.append(dict(kb=kb, b=b, pair=8 * n, group=g, og=og, n=n, sel=sel, sel_n=sel_n,
                             fresh=n == 0 or kb.single != blocks[n - 1][0].single))
            g += 8 * kb.groups + og
            sel_n += bool(sel)

        def rounds(eng, p, body, chain=None, per=0):
            if p["kb"].single:
                for t in range(4):
                    body(t, t == 0)
            elif p["n"] == 0:
                body(0, True)
                if chain:
                    with chain.loop(4, per, 1) as t:
                        body(t, False)
                else:
                    with eng.Fori(1, 4) as t:
                        body(t, False)
            elif chain:
                with chain.loop(4, per) as t:
                    body(t, False)
            else:
                with eng.Fori(0, 4) as t:
                    body(t, False)

        with nc.Block() as block:
            @block.gpsimd
            def _(pool):
                chain = Chain(pool, S["pchain"]) if bias_w else None
                for p in plan:
                    kb, b = p["kb"], p["b"]
                    nq = kb.nq
                    if select:
                        if p["n"]:
                            pool.wait_ge(S["s_ready"], p["pair"])
                            pool.wait_ge(S["s_free"], p["pair"])

                    def body(t, first):
                        for u in range(2):
                            h = t + 4 * u
                            if not (first and p["n"] == 0):
                                pool.wait_ge(S["s_ready"], p["pair"] + t * 2 + (u - 1))
                            r = rows(u)
                            src = q_of(t, u, kb)
                            if bias_w:
                                if not (first and p["n"] == 0):
                                    pool.wait_ge(S["s_free"], p["pair"] + t * 2 + (u - 1))
                                bt = bias_of(h, kb, first)
                                to = bm[0:nq, u, 0:kb.nk]
                                if select and p["sel"]:
                                    if u == 0:
                                        pool.wait_ge(S["mask_ready"], p["sel_n"] + 1)
                                    chain.link(nc.gpsimd.tensor_tensor(to, bt, score[0:nq, 0:kb.nk], ALU.add))
                                else:
                                    standing = S["pool_turns"]
                                    chain.link(nc.gpsimd.tensor_copy(to, bt), standing)
                                    if not kb.single:
                                        chain.link(nc.gpsimd.memset(bm[0:CHUNK, u, kb.nk - CHUNK:kb.nk], NEG), standing)
                                        if kind == "swa" and b > 0:
                                            chain.link(nc.gpsimd.memset(bm[CHUNK:P, u, 0:CHUNK], NEG))
                            nc.gpsimd.tensor_copy(qst[r, u, 0:nq], src).then_inc(S["q_staged"], 1)
                            if kind == "swa":
                                pool.wait_ge(S["q_staged"], p["pair"] + t * 2 + (u + 1))
                    per = 0
                    if bias_w:
                        per = 1
                        if not (select and p["sel"]) and not kb.single:
                            per += 1 + (kind == "swa" and b > 0)
                        per *= 2
                    rounds(pool, p, body, chain, per)

            @block.tensor
            def _(pe):
                qi_n = 0
                for p in plan:
                    kb = p["kb"]
                    nq, G = kb.nq, kb.groups
                    if p["fresh"] and p["n"]:
                        pe.wait_ge(S["s_free"], p["pair"])
                        pe.wait_ge(S["t_moved"], p["group"])
                        pe.wait_ge(S["o_moved"], p["pair"])
                    if p["sel"]:
                        for h in range(8):
                            if h >= 2:
                                pe.wait_ge(S["relu_ready"], 8 * p["sel_n"] + h - 1)
                            elif p["n"]:
                                pe.wait_ge(S["s_free"], p["pair"])
                            r = slice(64 * (h % 2), 64 * (h % 2) + 64)
                            s = kb.bank(ps, h % 2)
                            lhs = select["q"][r, h // 2, kb.q0:kb.q0 + nq]
                            for n0 in range(0, kb.nk, 512):
                                n1 = min(kb.nk, n0 + 512)
                                k0 = kb.tiles[0][0]
                                mm = nc.tensor.matmul(s[:, n0:n1], lhs, select["k"][r, k0 + n0:k0 + n1],
                                                      start=True, stop=True)
                            mm.then_inc(S["idx_ready"], 1)
                        pe.wait_ge(S["relu_ready"], 8 * p["sel_n"] + 8)

                    def body(t, first):
                        for u in range(2):
                            pe.wait_ge(S["q_staged"], p["pair"] + t * 2 + (u + 1))
                            if not (first and p["n"] == 0):
                                pe.wait_ge(S["s_free"], p["pair"] + t * 2 + (u - 1))
                            s = kb.bank(ps, u)
                            for n0 in range(0, kb.nk, 512):
                                n1 = min(kb.nk, n0 + 512)
                                mm = nc.tensor.matmul(s[:, n0:n1], qst[rows(u), u, 0:nq], k_of(t, u, kb, n0, n1),
                                                      start=True, stop=True)
                            mm.then_inc(S["s_ready"], 1)
                        for u in range(2):
                            pe.wait_ge(S["p_ready"], p["pair"] + t * 2 + (u + 1))
                            offs = kb.offsets()
                            for g in range(G):
                                gi = u * G + g
                                if not (first and p["n"] == 0 and gi < len(kb.t_banks)):
                                    pe.wait_ge(S["t_moved"], p["group"] + t * (2 * G) + (gi - len(kb.t_banks) + 1))
                                bank = kb.t_banks[(p["group"] + gi) % len(kb.t_banks)]
                                for j, (at, size, _) in enumerate(offs[g * kb.per:(g + 1) * kb.per]):
                                    mm = nc.tensor.transpose(ps[0:size, bank, j * nq:(j + 1) * nq],
                                                             prob[0:nq, u, at:at + size], m.ident[0:nq, 0:nq])
                                mm.then_inc(S["t_ready"], 1)
                            pe.wait_ge(S["t_moved"], p["group"] + t * (2 * G) + (u + 1) * G)
                            if not (first and p["n"] == 0) or (kb.single and u):
                                back = 0 if kb.single else 1
                                pe.wait_ge(S["o_moved"], p["pair"] + t * 2 + (u - back))
                            for j, (at, size, v) in enumerate(offs):
                                mm = nc.tensor.matmul(ps[0:nq, kb.o_banks[u], 0:dv], probT[0:size, u, j * nq:(j + 1) * nq],
                                                      v_of(t, u, v, size), start=j == 0, stop=j == len(offs) - 1)
                            mm.then_inc(S["o_ready"], 1)
                    rounds(pe, p, body)
                    pe.wait_ge(S["o_moved"], p["pair"] + 8)
                    for g in range(p["og"]):
                        gi = p["group"] + 8 * G + g
                        pe.wait_ge(S["t_moved"], gi - len(kb.t_banks) + 1)
                        bank = kb.t_banks[gi % len(kb.t_banks)]
                        for j in range(min(4, OT - 4 * g)):
                            mm = nc.tensor.transpose(ps[:, bank, j * nq:(j + 1) * nq],
                                                     osb[0:nq, (4 * g + j) * P:(4 * g + j + 1) * P], m.ident[0:nq, 0:nq])
                        mm.then_inc(S["t_ready"], 1)

            @block.scalar
            def _(act):
                for p in plan:
                    kb = p["kb"]
                    nq, G = kb.nq, kb.groups
                    if p["sel"]:
                        for h in range(8):
                            act.wait_ge(S["idx_ready"], 8 * p["sel_n"] + h + 1)
                            k = 8 * p["sel_n"] + h
                            if k >= 2:
                                act.wait_ge(S["relu_free"], k - 1)
                            nc.scalar.activation(relu[0:nq, h % 2, 0:kb.nk], kb.bank(ps, h % 2), ACT.Relu) \
                                .then_inc(S["relu_ready"], 1)

                    def body(t, first):
                        for u in range(2):
                            act.wait_ge(S["max_ready"], p["pair"] + t * 2 + (u + 1))
                            if not (first and p["n"] == 0):
                                act.wait_ge(S["o_ready"], p["pair"] + t * 2 + (u - 1))
                                act.wait_ge(S["inv_ready"], p["pair"] + t * 2 + (u - 1))
                            src = prob[0:nq, u, 0:kb.nk] if bias_w else kb.bank(ps, u)
                            ins = nc.scalar.activation(prob[0:nq, u, 0:kb.nk], src, ACT.Exp, bias=stat[0:nq, u, 1:2],
                                                       accum_out=stat[0:nq, u, 2:3])
                            if not bias_w:
                                ins.then_inc(S["p_ready"], 1)
                                act.wait_ge(S["p_ready"], p["pair"] + t * 2 + (u + 1))
                                nc.scalar.activation(stat[0:nq, u, 4:5], stat[0:nq, u, 1:2], ACT.Copy).then_inc(S["s_free"], 1)
                            else:
                                if sink:
                                    nc.scalar.activation(stat[0:nq, u, 4:5], stat[0:nq, u, 5:6], ACT.Exp,
                                                         bias=stat[0:nq, u, 1:2]).then_inc(S["p_ready"], 1)
                                else:
                                    ins.then_inc(S["p_ready"], 1)
                        offs = kb.offsets()
                        for u in range(2):
                            for g in range(G):
                                gi = u * G + g
                                act.wait_ge(S["t_ready"], p["group"] + t * (2 * G) + (gi + 1))
                                bank = kb.t_banks[(p["group"] + gi) % len(kb.t_banks)]
                                part = offs[g * kb.per:(g + 1) * kb.per]
                                at = g * kb.per * nq
                                full = sum(size == P for _, size, _ in part)
                                if full:
                                    ins = nc.scalar.activation(probT[:, u, at:at + full * nq],
                                                               ps[:, bank, 0:full * nq], ACT.Copy)
                                if full < len(part):
                                    ins = nc.scalar.activation(probT[0:TS, u, at + full * nq:at + (full + 1) * nq],
                                                               ps[0:TS, bank, full * nq:(full + 1) * nq], ACT.Copy)
                                ins.then_inc(S["t_moved"], 1)
                            act.wait_ge(S["o_ready"], p["pair"] + t * 2 + (u + 1))
                            act.wait_ge(S["inv_ready"], p["pair"] + t * 2 + (u + 1))
                            to = osb[0:nq, bass.ds((t + 4 * u) * dv, dv)]
                            nc.scalar.activation(to, ps[0:nq, kb.o_banks[u], 0:dv], ACT.Copy,
                                                 scale=stat[0:nq, u, 3:4]).then_inc(S["o_moved"], 1)
                    rounds(act, p, body)
                    for g in range(p["og"]):
                        gi = p["group"] + 8 * G + g
                        act.wait_ge(S["t_ready"], gi + 1)
                        bank = kb.t_banks[gi % len(kb.t_banks)]
                        k = min(4, OT - 4 * g)
                        nc.scalar.activation(out[:, out_tile + 4 * g:out_tile + 4 * g + k, kb.q0:kb.q0 + nq],
                                             ps[:, bank, 0:k * nq].rearrange("p (a n) -> p a n", a=k),
                                             ACT.Copy).then_inc(S["t_moved"], 1)

            @block.vector
            def _(dve):
                chain = Chain(dve, S["chain"])
                for p in plan:
                    kb, b = p["kb"], p["b"]
                    nq, nk = kb.nq, kb.nk
                    if p["sel"]:
                        sc, wk = score[0:nq, 0:nk], work[0:nq, 0:nk]
                        if p["n"]:
                            dve.wait_ge(S["s_free"], p["pair"])
                            dve.wait_ge(S["q_staged"], p["pair"])
                        for h in range(8):
                            k = 8 * p["sel_n"] + h
                            dve.wait_ge(S["relu_ready"], k + 1)
                            wi = select["w"][0:nq, kb.q0 // P, h:h + 1]
                            src = relu[0:nq, h % 2, 0:nk]
                            if h == 0:
                                ins = nc.vector.tensor_scalar(sc, src, wi, None, ALU.mult)
                            else:
                                dve.wait_ge(S["relu_free"], k)
                                ins = nc.vector.scalar_tensor_tensor(sc, src, wi, sc, ALU.mult, ALU.add)
                            ins.then_inc(S["relu_free"], 1)
                        dve.wait_ge(S["relu_free"], 8 * p["sel_n"] + 8)
                        hidden = score[0:CHUNK, nk - CHUNK:nk]
                        if not kb.single:
                            chain.link(nc.vector.memset(hidden, NEG))
                        chain.link(nc.vector.max(best[0:nq], sc))
                        chain.link(nc.vector.match_replace(wk, best[0:nq], sc, TAKEN))
                        with chain.loop(TOPK // 8 - 1, 2) as _:
                            chain.link(nc.vector.max(best[0:nq], wk), S["turns"])
                            chain.link(nc.vector.match_replace(wk, best[0:nq], wk, TAKEN))
                        ins = nc.vector.tensor_scalar(sc, wk, TAKEN / 2, NEG, ALU.is_gt, ALU.mult)
                        if not kb.single:
                            chain.link(ins)
                            ins = nc.vector.memset(hidden, NEG)
                        ins.then_inc(S["mask_ready"], 1)

                    def body(t, first):
                        for u in range(2):
                            dve.wait_ge(S["s_ready"], p["pair"] + t * 2 + (u + 1))
                            s = kb.bank(ps, u)
                            if sink:
                                src = m.sinks[0:nq, bass.ds(t + 4 * u, 1)]
                                if not (first and p["n"] == 0):
                                    dve.wait_ge(S["p_ready"], p["pair"] + t * 2 + (u - 1))
                                chain.link(nc.vector.tensor_copy(stat[0:nq, u, 5:6], src))
                            if bias_w:
                                if not (first and p["n"] == 0):
                                    dve.wait_ge(S["o_ready"], p["pair"] + t * 2 + (u - 1))
                                dve.sem_inc(S["turns"], 1)
                                init = stat[0:nq, u, 5:6] if sink else m.negs[0:nq]
                                ins = nc.vector.tensor_tensor_reduce(
                                    out=prob[0:nq, u, 0:nk], in0=s, in1=bm[0:nq, u, 0:nk], scale=1.0,
                                    scalar=init, op0=ALU.add, op1=ALU.max, accum_out=stat[0:nq, u, 0:1])
                                chain.link(ins)
                                nc.vector.tensor_scalar(stat[0:nq, u, 6:7], stat[0:nq, u, 0:1], 0.0, None, ALU.mult) \
                                    .then_inc(S["s_free"], 1)
                            else:
                                if not kb.single:
                                    chain.link(nc.vector.memset(s[0:CHUNK, nk - CHUNK:nk], NEG))
                                chain.link(nc.vector.tensor_reduce(stat[0:nq, u, 0:1], s, AX.X, ALU.max))
                            if not (first and p["n"] == 0):
                                dve.wait_ge(S["p_ready"], p["pair"] + t * 2 + (u - 1))
                                if not bias_w:
                                    dve.wait_ge(S["s_free"], p["pair"] + t * 2 + (u - 1))
                            nc.vector.tensor_scalar(stat[0:nq, u, 1:2], stat[0:nq, u, 0:1], -1.0, None, ALU.mult) \
                                .then_inc(S["max_ready"], 1)
                        for u in range(2):
                            dve.wait_ge(S["p_ready"], p["pair"] + t * 2 + (u + 1))
                            if not (first and p["n"] == 0):
                                dve.wait_ge(S["o_moved"], p["pair"] + t * 2 + (u - 1))
                            if sink:
                                chain.link(nc.vector.tensor_tensor(stat[0:nq, u, 2:3], stat[0:nq, u, 2:3],
                                                                   stat[0:nq, u, 4:5], ALU.add))
                            nc.vector.reciprocal(stat[0:nq, u, 3:4], stat[0:nq, u, 2:3]).then_inc(S["inv_ready"], 1)
                    per = 1 + 2 * sink + (not bias_w and not kb.single)
                    rounds(dve, p, body, chain, 2 * per)


def rms_scale(m, tag, src, sq, rs, tiles, factor, gains, ctx):
    pass


def even_mixer(m):
    nc, ps, d = m.nc, m.ps, m.d
    with ExitStack() as outer:
        lat = m.sb("lat", [P, NKEYS], outer)
        kpe = m.sb("kpe", [P, NKEYS], outer)
        cq = m.sb("cq", [P, 2, N], outer)
        rope = m.sb("rope", [P, 2, N], outer)
        R = slice(64, 96)
        with ExitStack() as mid:
            qs = m.sb("qs", [P, 4, N], mid)
            ks = m.sb("ks", [P, SWA_COLS], mid)
            vs = m.sb("vs", [P, 10, P], mid)
            with ExitStack() as c:
                w = m.sb("we", [P, KT, EVEN_W], c)
                sq = m.sb("sqe", [P, 3, N], c)
                rs = m.sb("rse", [P, 2, N], c)
                rot = m.sb("rot", [P, N], c)
                names = ("we_loaded", "ec_loaded", "e_ready", "e_moved", "e_roped", "e_squared", "e_summed", "e_chain",
                         "e_inv", "e_root", "e_normed", "e_out", "e_kpe")
                S = {n: m.sem(n) for n in names}
                units = [("cq", 0, 0), ("cq", 1, 128), ("lat", 0, 256), ("ks", 0, 384)] + \
                        [("qs", t, 512 + P * t) for t in range(4)]
                flat = [(n, i, c0, t) for n, i, c0 in units for t in range(NTOK)]
                vbase = len(flat)
                rbase = vbase + 9
                with nc.Block() as block:
                    @block.sync
                    def _(sp):
                        for k in range(KT):
                            sp.dma_start(w[:, k], d["we"][:, k]).then_inc(S["we_loaded"], 16)
                        sp.wait_ge(S["e_kpe"], 1)
                        sp.wait_ge(S["e_normed"], 1)
                        sp.wait_ge(S["e_moved"], rbase)
                        outs = [(d["latT"][:, 0:TP], lat[:, 0:TP]), (d["latT"][:, TP:N], lat[:, TP + PAST:NKEYS]),
                                (d["kpeT"][:, 0:TP], kpe[R, 0:TP]), (d["kpeT"][:, TP:N], kpe[R, TP + PAST:NKEYS]),
                                (d["swakT"][:, 0:P], ks[:, TP - P:TP]),
                                (d["swakT"][:, P:2 * P], ks[:, TP + TS:SWA_COLS]),
                                (d["swav"][0], vs[:, 7]), (d["swav"][1, 0:P - TS], vs[TS:P, 8]),
                                (d["swav"][1, P - TS:P], vs[0:TS, 9])]
                        for to, src in outs:
                            sp.dma_start(to, src).then_inc(S["e_out"], 16)
                        sp.wait_ge(S["e_out"], 16 * len(outs))

                    @block.scalar
                    def _(act):
                        ins = [(lat[:, TP:TP + PAST], "c_lat"), (kpe[R, TP:TP + PAST], "c_kpe"),
                               (ks[:, TP:TP + P], "c_swak"), (vs[:, 8], "c_swav"), (rope[R], "rope")]
                        for tile, name in ins:
                            act.dma_start(tile, d[name]).then_inc(S["ec_loaded"], 16)
                        dest = {"cq": lambda i, t: [(cq[:, i, t * NT:(t + 1) * NT], 0, NT)],
                                "qs": lambda i, t: [(qs[:, i, t * NT:(t + 1) * NT], 0, NT)]}
                        for q, (name, i, _, t) in enumerate(flat):
                            act.wait_ge(S["e_ready"], q + 1)
                            bank = q % 8
                            if name in dest:
                                pieces = dest[name](i, t)
                            else:
                                tile, start = (lat, TP + PAST) if name == "lat" else (ks, TP + P)
                                pieces = [(tile[:, t * NT + c0:t * NT + c0 + cn] if s == 0 else tile[:, start:start + cn], c0, cn)
                                          for s, c0, cn in segments(t)]
                            for to, c0, cn in pieces:
                                ins = nc.scalar.activation(to, ps[:, bank, c0:c0 + cn], ACT.Copy,
                                                           scale=SWA_SCALE if name == "qs" else 1.0)
                            ins.then_inc(S["e_moved"], 1)
                        for i in range(9):
                            q = vbase + i
                            act.wait_ge(S["e_ready"], q + 1)
                            rows = P if i < 8 else TS
                            nc.scalar.activation(vs[0:rows, i if i < 8 else 9], ps[0:rows, q % 8, 0:P], ACT.Copy) \
                                .then_inc(S["e_moved"], 1)
                        act.wait_ge(S["e_moved"], vbase)
                        for i in range(2):
                            nc.scalar.activation(sq[:, i], cq[:, i], ACT.Square).then_inc(S["e_squared"], 1)
                        nc.scalar.activation(sq[:, 2, 0:TP], lat[:, 0:TP], ACT.Square)
                        nc.scalar.activation(sq[:, 2, TP:N], lat[:, TP + PAST:NKEYS], ACT.Square).then_inc(S["e_squared"], 1)
                        for i in range(2):
                            act.wait_ge(S["e_inv"], i + 1)
                            nc.scalar.activation(rs[:, i], rs[:, i], ACT.Sqrt).then_inc(S["e_root"], 1)

                    @block.tensor
                    def _(pe):
                        pe.wait_ge(S["we_loaded"], 16 * KT)
                        for q, (name, i, c0, t) in enumerate(flat):
                            if q >= 8:
                                pe.wait_ge(S["e_moved"], q - 7)
                            for k in range(KT):
                                mm = nc.tensor.matmul(ps[:, q % 8, 0:NT], w[:, k, c0:c0 + P],
                                                      m.hT[:, k, t * NT:(t + 1) * NT], start=k == 0, stop=k == KT - 1)
                            mm.then_inc(S["e_ready"], 1)
                        for i in range(9):
                            q = vbase + i
                            pe.wait_ge(S["e_moved"], q - 7)
                            rows = P if i < 8 else TS
                            for k in range(KT):
                                mm = nc.tensor.matmul(ps[0:rows, q % 8, 0:P], m.hT[:, k, i * P:i * P + rows],
                                                      w[:, k, 1024:1024 + P], start=k == 0, stop=k == KT - 1)
                            mm.then_inc(S["e_ready"], 1)
                        for j in range(2):
                            for t in range(NTOK):
                                q = rbase + j * NTOK + t
                                pe.wait_ge(S["e_moved"], q - 7)
                                for k in range(KT):
                                    mm = nc.tensor.matmul(ps[R, q % 8, 0:NT], w[:, k, 1152 + 32 * j:1184 + 32 * j],
                                                          m.hT[:, k, t * NT:(t + 1) * NT], start=k == 0, stop=k == KT - 1)
                                mm.then_inc(S["e_ready"], 1)
                        pe.wait_ge(S["e_moved"], rbase)
                        pe.wait_ge(S["e_roped"], 6)
                        pe.wait_ge(S["e_squared"], 3)
                        for t in range(NTOK):
                            for i in range(2):
                                nc.tensor.matmul(ps[:, t, 0:NT], m.ones[:], sq[:, i, t * NT:(t + 1) * NT],
                                                 start=i == 0, stop=i == 1)
                            mm = nc.tensor.matmul(ps[:, NTOK + t, 0:NT], m.ones[:], sq[:, 2, t * NT:(t + 1) * NT],
                                                  start=True, stop=True)
                        mm.then_inc(S["e_summed"], 1)

                    @block.vector
                    def _(dve):
                        chain = Chain(dve, S["e_chain"])
                        dve.wait_ge(S["ec_loaded"], 16 * 5)
                        for j in range(2):
                            for t in range(NTOK):
                                q = rbase + j * NTOK + t
                                dve.wait_ge(S["e_ready"], q + 1)
                                if j == 0:
                                    for s, c0, cn in segments(t):
                                        to = t * NT + c0 if s == 0 else TP + PAST
                                        src = slice(t * NT + c0, t * NT + c0 + cn)
                                        ins = nc.vector.tensor_tensor(kpe[R, to:to + cn], ps[R, q % 8, c0:c0 + cn],
                                                                      rope[R, 0, src], ALU.mult)
                                else:
                                    src = slice(t * NT, (t + 1) * NT)
                                    ins = nc.vector.tensor_tensor(rot[R, src], ps[R, q % 8, 0:NT], rope[R, 1, src], ALU.mult)
                                ins.then_inc(S["e_roped"], 1)
                        dve.wait_ge(S["e_roped"], 6)
                        nc.vector.tensor_tensor(kpe[R, 0:TP], kpe[R, 0:TP], rot[R, 0:TP], ALU.add)
                        new = kpe[R, TP + PAST:NKEYS]
                        nc.vector.tensor_tensor(new, new, rot[R, TP:N], ALU.add).then_inc(S["e_kpe"], 1)
                        dve.wait_ge(S["e_summed"], 1)
                        for i, factor in enumerate((D / 256, D / 128)):
                            for t in range(NTOK):
                                ins = nc.vector.tensor_scalar(rs[:, i, t * NT:(t + 1) * NT], ps[:, i * NTOK + t, 0:NT],
                                                              factor, RMS_EPS, ALU.mult, ALU.add)
                            chain.link(ins)
                            nc.vector.reciprocal(rs[:, i], rs[:, i]).then_inc(S["e_inv"], 1)
                        chain.link(nc.vector.tensor_scalar(m.gq[:, 0:2], m.gq[:, 0:2], MLA_SCALE, None, ALU.mult))
                        dve.wait_ge(S["e_root"], 2)
                        for i in range(2):
                            nc.vector.scalar_tensor_tensor(cq[:, i], cq[:, i], m.gq[:, i:i + 1], rs[:, 0], ALU.mult, ALU.mult)
                        for a, b, r0 in ((0, TP, 0), (TP + PAST, NKEYS, TP)):
                            ins = nc.vector.scalar_tensor_tensor(lat[:, a:b], lat[:, a:b], m.gq[:, 2:3],
                                                                 rs[:, 1, r0:r0 + b - a], ALU.mult, ALU.mult)
                        ins.then_inc(S["e_normed"], 1)

            with ExitStack() as c:
                btile = m.sb("bswa", [P, HEADS, 256], c)
                bl = m.sem("bswa_loaded")
                with nc.Block() as block:
                    @block.sync
                    def _(sp):
                        src = toeplitz(m, TP - P, 256)
                        sp.dma_start(btile[:], src).then_inc(bl, 16)
                        sp.wait_ge(bl, 16)
                blocks = [(Keys(b * P, P, [(c0 * P, P, c0) for c0 in range(max(0, b - 1), b + 1)]), b) for b in range(8)]
                blocks.append((Keys(TP, TS, [(TP, P, 8), (TP + P, TS, 9)], single=True), 8))

                def rows(u):
                    return slice(64 * u, 64 * u + 64)

                def q_of(t, u, kb):
                    at = t if isinstance(t, int) else bass.ds(t, 1)
                    ap = qs[rows(u), at, kb.q0:kb.q0 + kb.nq]
                    return ap if isinstance(t, int) else ap.rearrange("p a n -> p (a n)")

                def bias_of(h, kb, first):
                    j0 = 0 if kb.single or kb.nk == 256 else P
                    ap = btile[0:kb.nq, h if isinstance(h, int) else bass.ds(h, 1), j0:j0 + kb.nk]
                    return ap if isinstance(h, int) else ap.rearrange("p a n -> p (a n)")
                attention_stage(m, "swa", blocks, "swa", q_of,
                                lambda t, u, kb, n0, n1: ks[rows(u), kb.tiles[0][0] + n0:kb.tiles[0][0] + n1],
                                lambda t, u, v, size: vs[0:size, v, 64 * u:64 * u + 64],
                                64, rows, 4, bias_w=256, bias_of=bias_of, sink=True)

        with ExitStack() as c:
            q = m.sb("qmla", [96, HEADS, N], c)
            kT = m.sb("kmla", [96, HEADS, N], c)
            v = m.sb("vmla", [P, 9, 512], c)
            for part in range(2):
                with ExitStack() as cc:
                    rot = m.sb(f"rotq{part}", [P, 2, NT], cc)
                    wq = m.sb("wuq", [P, 2, HEADS, P], cc) if part == 0 else None
                    wkv = m.sb(f"wukv{part}", [P, 2, 512], cc)
                    mla_up(m, part, q, kT, v, wq, wkv, cq, lat, kpe, rope, rot, R)
                nk0 = 0 if part == 0 else TP
                if part == 0:
                    blocks = [(Keys(b * P, P, [(i * P, P, i) for i in range(b + 1)]), b) for b in range(8)]
                else:
                    blocks = [(Keys(TP, TS, [(i * P, P, i) for i in range(8)] + [(TP, TS, 8)], single=True), 8)]

                def q_of(t, u, kb):
                    if isinstance(t, int):
                        return q[:, t + 4 * u, kb.q0:kb.q0 + kb.nq]
                    return q[:, bass.ds(t + 4 * u, 1), kb.q0:kb.q0 + kb.nq].rearrange("p a n -> p (a n)")

                def k_of(t, u, kb, n0, n1):
                    if isinstance(t, int):
                        return kT[:, t + 4 * u, n0:n1]
                    return kT[:, bass.ds(t + 4 * u, 1), n0:n1].rearrange("p a n -> p (a n)")
                attention_stage(m, f"mla{part}", blocks, "mla", q_of, k_of,
                                lambda t, u, i, size: v[0:size, i, bass.ds((t + 4 * u) * 64, 64)],
                                64, lambda u: slice(0, 96), 0)
    with ExitStack() as c:
        down_stage(m, "e", d["woe"], m.hT, KT, 0, 0, c)


def mla_up(m, part, q, kT, v, wq, wkv, cq, lat, kpe, rope, rot, R):
    nc, ps, d = m.nc, m.ps, m.d
    names = ("w_loaded", "q_ready", "q_moved", "q_rot", "chain", "k_ready", "k_moved")
    S = {n: m.sem(f"up{part}_{n}") for n in names}
    l0, nk = (0, TP) if part == 0 else (TP, N)
    chunks = [(a, min(nk, a + 512)) for a in range(0, nk, 512)]
    vt = 8 if part == 0 else 9
    nunits = HEADS * NTOK if part == 0 else 0
    kunits = HEADS * len(chunks)
    with nc.Block() as block:
        @block.sync
        def _(sp):
            sp.dma_start(wkv[:], d["wukv"]).then_inc(S["w_loaded"], 16)
            if part == 0:
                sp.dma_start(wq[:], d["wuq"]).then_inc(S["w_loaded"], 16)

        @block.tensor
        def _(pe):
            pe.wait_ge(S["w_loaded"], 32 if part == 0 else 16)
            for n in range(nunits):
                h, t = divmod(n, NTOK)
                cols = slice(t * NT, (t + 1) * NT)
                if n >= 2:
                    pe.wait_ge(S["q_moved"], n - 1)
                    pe.wait_ge(S["q_rot"], n - 1)
                for j, (r, w0, w1) in enumerate(((slice(0, 96), 0, 96), (R, 96, 128))):
                    for k in range(2):
                        mm = nc.tensor.matmul(ps[r, 2 * (n % 2) + j, 0:NT], wq[:, k, h, w0:w1], cq[:, k, cols],
                                              start=k == 0, stop=k == 1)
                mm.then_inc(S["q_ready"], 1)
            for n in range(kunits + vt):
                if n >= 4:
                    pe.wait_ge(S["k_moved"], n - 3)
                bank = 4 + n % 4
                if n < kunits:
                    h, ci = divmod(n, len(chunks))
                    a, b = chunks[ci]
                    mm = nc.tensor.matmul(ps[0:64, bank, 0:b - a], wkv[:, 0, 64 * h:64 * h + 64],
                                          lat[:, l0 + a:l0 + b], start=True, stop=True)
                else:
                    i = n - kunits
                    rows = min(P, nk - i * P)
                    mm = nc.tensor.matmul(ps[0:rows, bank, :], lat[:, l0 + i * P:l0 + i * P + rows], wkv[:, 1],
                                          start=True, stop=True)
                mm.then_inc(S["k_ready"], 1)

        @block.scalar
        def _(act):
            for n in range(nunits):
                h, t = divmod(n, NTOK)
                act.wait_ge(S["q_ready"], n + 1)
                act.wait_ge(S["q_rot"], n + 1)
                nc.scalar.activation(q[0:64, h, t * NT:(t + 1) * NT], ps[0:64, 2 * (n % 2), 0:NT], ACT.Copy) \
                    .then_inc(S["q_moved"], 1)
            for n in range(kunits + vt):
                act.wait_ge(S["k_ready"], n + 1)
                bank = 4 + n % 4
                if n < kunits:
                    h, ci = divmod(n, len(chunks))
                    a, b = chunks[ci]
                    ins = nc.scalar.activation(kT[0:64, h, a:b], ps[0:64, bank, 0:b - a], ACT.Copy)
                else:
                    i = n - kunits
                    rows = min(P, nk - i * P)
                    ins = nc.scalar.activation(v[0:rows, i], ps[0:rows, bank, :], ACT.Copy)
                ins.then_inc(S["k_moved"], 1)

        @block.gpsimd
        def _(pool):
            nc.gpsimd.tensor_copy(kT[R, :, 0:nk], spread(kpe[R, l0:l0 + nk], HEADS))

        @block.vector
        def _(dve):
            chain = Chain(dve, S["chain"])
            for n in range(nunits):
                h, t = divmod(n, NTOK)
                cols = slice(t * NT, (t + 1) * NT)
                dve.wait_ge(S["q_ready"], n + 1)
                nc.vector.tensor_tensor(rot[R, 0], ps[R, 2 * (n % 2), 0:NT], rope[R, 0, cols], ALU.mult)
                chain.link(nc.vector.tensor_tensor(rot[R, 1], ps[R, 2 * (n % 2) + 1, 0:NT], rope[R, 1, cols], ALU.mult))
                nc.vector.tensor_tensor(q[R, h, cols], rot[R, 0], rot[R, 1], ALU.add).then_inc(S["q_rot"], 1)
                dve.wait_ge(S["q_rot"], n + 1)


def odd_mixer(m):
    nc, ps, d = m.nc, m.ps, m.d
    with ExitStack() as outer:
        qd = m.sb("qd", [P, HEADS, N], outer)
        kd = m.sb("kd", [P, 2, NKEYS], outer)
        ki = m.sb("ki", [P, NKEYS], outer)
        qi = m.sb("qi", [P, 4, N], outer)
        v = m.sb("vd", [P, 17, 256], outer)
        wi = m.sb("wi", [P, 9, HEADS], outer)
        with ExitStack() as c:
            w = m.sb("wo", [P, 3, KT, P], c)
            wv = m.sb("wov", [P, KT, VW], c)
            names = ("ready", "moved", "v_loaded", "c_loaded", "out", "v_ready", "v_moved", "w_chain")
            S = {n: m.sem("o_" + n) for n in names}
            wl = [m.sem(f"wo_loaded{u}") for u in range(3)]
            with nc.Block() as block:
                @block.sync
                def _(sp):
                    for j in range(ODD_TILES):
                        if j >= 3:
                            sp.wait_ge(S["ready"], 3 * (j - 2))
                        sp.dma_start(w[:, j % 3], d["wo"][j]).then_inc(wl[j % 3], 16)
                        if j == 2:
                            sp.dma_start(wv[:], d["wov"]).then_inc(S["v_loaded"], 16)
                    sp.wait_ge(S["moved"], 3 * ODD_TILES)
                    sp.wait_ge(S["v_moved"], 18)
                    outs = [(d["dsakT"][:, :, 0:TP], kd[:, :, 0:TP]), (d["dsakT"][:, :, TP:N], kd[:, :, TP + PAST:NKEYS]),
                            (d["idxT"][:, 0:TP], ki[0:64, 0:TP]), (d["idxT"][:, TP:N], ki[0:64, TP + PAST:NKEYS]),
                            (d["dsav"][:, 0:8], v[:, 0:8]), (d["dsav"][0:TS, 8], v[0:TS, 16])]
                    for to, src in outs:
                        sp.dma_start(to, src).then_inc(S["out"], 16)
                    sp.wait_ge(S["out"], 16 * len(outs))

                @block.tensor
                def _(pe):
                    for j in range(ODD_TILES):
                        pe.wait_ge(wl[j % 3], 16 * (j // 3 + 1))
                        for t in range(NTOK):
                            n = NTOK * j + t
                            if n >= 6:
                                pe.wait_ge(S["moved"], n - 5)
                            for k in range(KT):
                                mm = nc.tensor.matmul(ps[:, n % 6, 0:NT], w[:, j % 3, k], m.hT[:, k, t * NT:(t + 1) * NT],
                                                      start=k == 0, stop=k == KT - 1)
                            mm.then_inc(S["ready"], 1)
                    pe.wait_ge(S["v_loaded"], 16)
                    for i in range(9):
                        if i >= 2:
                            pe.wait_ge(S["v_moved"], 2 * (i - 1))
                        rows = P if i < 8 else TS
                        for k in range(KT):
                            mm = nc.tensor.matmul(ps[0:rows, 6 + i % 2, 0:VW], m.hT[:, k, i * P:i * P + rows], wv[:, k],
                                                  start=k == 0, stop=k == KT - 1)
                        mm.then_inc(S["v_ready"], 1)

                @block.scalar
                def _(act):
                    for to, name in ((kd[:, :, TP:TP + PAST], "c_dsak"), (v[:, 8:16], "c_dsav"),
                                     (ki[0:64, TP:TP + PAST], "c_idx"), (ki[64:P, TP:TP + PAST], "c_idx")):
                        act.dma_start(to, d[name]).then_inc(S["c_loaded"], 16)
                    for j in range(ODD_TILES):
                        for t in range(NTOK):
                            n = NTOK * j + t
                            act.wait_ge(S["ready"], n + 1)
                            cols = slice(t * NT, (t + 1) * NT)
                            if j < 8 or j > 10:
                                to = qd[:, j, cols] if j < 8 else qi[:, j - 11, cols]
                                pieces = [(to, 0, NT)]
                            else:
                                tile = kd[:, j - 8] if j < 10 else ki[:]
                                pieces = [(tile[:, t * NT + c0:t * NT + c0 + cn] if s == 0 else tile[:, TP + PAST:NKEYS], c0, cn)
                                          for s, c0, cn in segments(t)]
                            for to, c0, cn in pieces:
                                ins = nc.scalar.activation(to, ps[:, n % 6, c0:c0 + cn], ACT.Copy,
                                                           scale=DSA_SCALE if j < 8 else 1.0)
                            ins.then_inc(S["moved"], 1)
                    for i in range(9):
                        rows = P if i < 8 else TS
                        act.wait_ge(S["v_ready"], i + 1)
                        nc.scalar.activation(v[0:rows, i if i < 8 else 16], ps[0:rows, 6 + i % 2, 0:256], ACT.Copy) \
                            .then_inc(S["v_moved"], 1)
                        nc.scalar.activation(wi[0:rows, i], ps[0:rows, 6 + i % 2, 256:VW], ACT.Copy, scale=IDX_W_SCALE) \
                            .then_inc(S["v_moved"], 1)
                    act.wait_ge(S["c_loaded"], 64)

        btile = m.hT
        for part in range(2):
            bl = m.sem(f"bdsa_loaded{part}")
            width, j0 = (TP, P) if part == 0 else (N, 0)
            with nc.Block() as block:
                @block.sync
                def _(sp):
                    src = toeplitz(m, j0, width)
                    sp.dma_start(btile[:, :, 0:width], src).then_inc(bl, 16)
                    sp.wait_ge(bl, 16)
            if part == 0:
                blocks = [(Keys(b * P, P, [(i * P, P, i) for i in range(b + 1)]), b) for b in range(8)]
            else:
                blocks = [(Keys(TP, TS, [(TP + i * P, P, 8 + i) for i in range(8)] + [(TP + PAST, TS, 16)],
                                single=True), 8)]

            def q_of(t, u, kb):
                if isinstance(t, int):
                    return qd[:, t + 4 * u, kb.q0:kb.q0 + kb.nq]
                return qd[:, bass.ds(t + 4 * u, 1), kb.q0:kb.q0 + kb.nq].rearrange("p a n -> p (a n)")

            def bias_of(h, kb, first):
                b0 = 0 if kb.single else 7 * P - kb.q0
                ap = btile[0:kb.nq, h if isinstance(h, int) else bass.ds(h, 1), b0:b0 + kb.nk]
                return ap if isinstance(h, int) else ap.rearrange("p a n -> p (a n)")
            attention_stage(m, f"dsa{part}", blocks, "dsa", q_of,
                            lambda t, u, kb, n0, n1: kd[:, u, kb.tiles[0][0] + n0:kb.tiles[0][0] + n1],
                            lambda t, u, i, size: v[0:size, i, P * u:P * u + P],
                            P, lambda u: slice(0, P), 0, bias_w=TP if part == 0 else N, bias_of=bias_of,
                            select=dict(q=qi, k=ki, w=wi), out=qd)
        down_stage(m, "o", d["woo"], qd, KT, 1, 0, outer)


def build_program(nc, dram):
    with ExitStack() as ctx:
        m = Machine(nc, ctx, dram)
        start_stage(m)
        even_mixer(m)
        norm_stage(m, 0, 0)
        m.recycle()
        ffn_stage(m, 0)
        norm_stage(m, 0, 1)
        m.recycle()
        odd_mixer(m)
        norm_stage(m, 1, 0)
        m.recycle()
        ffn_stage(m, 1)
        norm_stage(m, 1, 1, final=True)
        stored = m.sem("conv_stored")
        with nc.Block() as block:
            @block.sync
            def _(sp):
                sp.dma_start(dram["convo"], m.convo[:]).then_inc(stored, 16)
                sp.wait_ge(stored, 16)


def shape_constants():
    pos = np.arange(N, dtype=np.float32)
    half = np.arange(16, dtype=np.float32)
    inv = np.power(np.float64(10000.0), -(half / np.float32(16)).astype(np.float64)).astype(np.float32)
    ang = (pos[None, :] * inv[:, None]).astype(np.float32).astype(np.float64)
    cos, sin = np.cos(ang).astype(np.float32), np.sin(ang).astype(np.float32)
    rope = np.stack([np.concatenate([cos, cos]), np.concatenate([-sin, sin])], axis=1)
    rel = np.arange(REL_LEN) - REL_BASE
    n = np.abs(rel)
    large = 8 + (np.log(np.maximum(n, 1).astype(np.float32) / np.float32(8)) / np.float32(np.log(128.0))
                 * np.float32(8)).astype(np.int32)
    bucket = np.where(rel > 0, 16, 0) + np.where(n < 8, n, np.minimum(large, 15))
    onehot = (np.arange(32)[:, None] == bucket[None, :]).astype(np.float32)
    return dict(rope=rope, onehot=onehot, ident=np.eye(P, dtype=np.float32),
                ones=np.full((P, P), 1.0 / D, np.float32))


def tiles_of(w, columns):
    w = w[:, columns]
    rows, cols = w.shape
    return np.ascontiguousarray(w.reshape(rows // P, P, cols // P, P).transpose(2, 1, 0, 3))


def by_partition(a):
    return np.moveaxis(a.reshape(a.shape[:-1] + (-1, P)), -1, 0)


def kernel(**inputs):
    import concourse.bacc as bacc
    from concourse.bass_utils import run_bass_kernel_spmd

    i = {k: np.asarray(v) for k, v in inputs.items()}
    a = dict(shape_constants())
    a["xT"] = np.concatenate([i["x_prompt"][0], i["x_sample"][0]]).T.reshape(KT, P, N).transpose(1, 0, 2)
    a["cT"] = np.stack([i["c_prompt"][0], i["c_sample"][0]]).T.reshape(KT, P, 2).transpose(1, 0, 2)
    wada = np.stack([tiles_of(i["w_ada"][l], slice(None)) for l in range(2)]).reshape(24, 4, P, KT, P)
    a["wada"] = wada.transpose(0, 2, 1, 3, 4)
    a["bada"] = np.repeat(by_partition(i["b_ada"]).reshape(P, 96, 1), 2, axis=2)
    a["lnp"] = np.stack([by_partition(i[n]) for n in ("ln_mix_g", "ln_mix_b", "ln_ffn_g", "ln_ffn_b")], axis=2)
    a["rel_bias"] = i["rel_bias"]
    a["sinks"] = np.broadcast_to(i["swa_sinks"][0], (P, HEADS))
    a["gq"] = np.concatenate([i["g_q_lora"][0].reshape(2, P), i["g_kv_lora"][0].reshape(1, P)]).T

    kr = np.arange(384, 416)
    qs = 416 + np.concatenate([np.r_[t * 64:t * 64 + 64, (t + 4) * 64:(t + 4) * 64 + 64] for t in range(4)])
    cols = np.concatenate([np.arange(384), np.arange(928, 1056), qs, np.arange(1056, 1184), kr, np.roll(kr, 16)])
    a["we"] = i["w_in_even"][0][:, cols].reshape(KT, P, EVEN_W).transpose(1, 0, 2)
    uq = i["w_uq"][0].reshape(2, P, HEADS, 96)
    a["wuq"] = np.concatenate([uq, np.roll(uq[..., 64:], 16, axis=-1)], axis=-1).transpose(1, 0, 2, 3)
    ukv = i["w_ukv"][0].reshape(P, HEADS, 2, 64)
    a["wukv"] = ukv.transpose(0, 2, 1, 3).reshape(P, 2, 512)
    a["woe"] = tiles_of(i["w_out_even"][0], slice(None))

    cols = np.concatenate([np.arange(1280), np.arange(2048, 2112), np.arange(2048, 2112), np.arange(1536, 2048)])
    a["wo"] = tiles_of(i["w_in_odd"][0], cols)
    a["wov"] = i["w_in_odd"][0][:, np.r_[1280:1536, 2112:2120]].reshape(KT, P, VW).transpose(1, 0, 2)
    a["woo"] = tiles_of(i["w_out_odd"][0], slice(None))

    wfi = np.stack([tiles_of(i["ffn_w_in"][l], slice(None)) for l in range(2)])
    a["wfi"] = wfi.reshape(2, 2, FT, P, KT, P).transpose(0, 2, 3, 1, 4, 5)
    a["wfo"] = np.stack([tiles_of(i["ffn_w_out"][l], slice(None)) for l in range(2)])
    taps = np.concatenate([i["ffn_conv_w"], i["ffn_conv_b"][:, None]], axis=1)
    a["convp"] = taps.reshape(2, 4, 2, FT, P).transpose(4, 0, 3, 2, 1).reshape(P, 2, FT, 8)
    state = i["state_ffn_conv"][:, 0]
    a["convs"] = state.reshape(2, 2, 2, FT, P).transpose(4, 0, 3, 2, 1).reshape(P, 2, FT, 4)

    a["c_lat"] = i["cache_mla_latent"][0, 0].T
    a["c_kpe"] = i["cache_mla_kpe"][0, 0].T
    a["c_swak"] = i["cache_swa_k"][0, 0].reshape(P, P).T
    a["c_swav"] = i["cache_swa_v"][0, 0].reshape(P, P)
    a["c_dsak"] = i["cache_dsa_k"][0, 0].transpose(2, 1, 0)
    a["c_dsav"] = i["cache_dsa_v"][0, 0].reshape(8, P, 256).transpose(1, 0, 2)
    a["c_idx"] = i["cache_dsa_idx_k"][0, 0].T
    a = {k: np.ascontiguousarray(v) for k, v in a.items()}

    outs = dict(yT=(P, KT, N), latT=(P, N), kpeT=(32, N), swakT=(P, 2 * P), swav=(2, P, P), dsakT=(P, 2, N),
                dsav=(P, 9, 256), idxT=(64, N), convo=(P, 2, FT, 8))
    nc = bacc.Bacc("TRN2", target_bir_lowering=False, num_devices=1)
    dram = {k: nc.dram_tensor(f"in_{k}", v.shape, F32, kind="ExternalInput").ap() for k, v in a.items()}
    for k, shape in outs.items():
        dram[k] = nc.dram_tensor(f"out_{k}", shape, F32, kind="ExternalOutput").ap()
    build_program(nc, dram)
    r = run_bass_kernel_spmd(nc, [{f"in_{k}": v for k, v in a.items()}], core_ids=[0]).results[0]
    o = {k: np.asarray(r[f"out_{k}"]) for k in outs}

    y = o["yT"].transpose(2, 1, 0).reshape(N, D)
    lat, kpe = o["latT"].T, o["kpeT"].T
    swak = o["swakT"].T.reshape(2, 1, 1, P, 2, 64)
    swav = o["swav"].reshape(2, 1, 1, P, 2, 64)
    dk = o["dsakT"].transpose(2, 1, 0)
    dv = o["dsav"].transpose(1, 0, 2).reshape(9 * P, 2, P)[:N]
    di = o["idxT"].T
    cv = o["convo"].reshape(P, 2, FT, 2, 2, 2).transpose(3, 1, 5, 4, 2, 0).reshape(2, 2, 1, 2, 2 * FF)
    both = [slice(0, TP), slice(TP, N)]
    group = [[lat[s][None, None], kpe[s][None, None], swak[n], swav[n], dk[s][None, None], dv[s][None, None],
              di[s][None, None], cv[n]] for n, s in enumerate(both)]
    return tuple(np.ascontiguousarray(x) for x in [y[both[0]][None], y[both[1]][None], *group[0], *group[1]])
```

```python
from contextlib import ExitStack, contextmanager

import numpy as np

import concourse.bass as bass
from concourse import mybir

F32 = mybir.dt.float32
F32R = mybir.dt.float32r
ALU = mybir.AluOpType
ACT = mybir.ActivationFunctionType
AX = mybir.AxisListType

P = 128
D = 1024
KT = D // P
TP, TS = 1024, 32
N = TP + TS
NTOK = 3
NT = N // NTOK
PAST = 1024
CHUNK = 64
NEG = -1e30
TAKEN = -3e38
LN_EPS, RMS_EPS = 1e-5, 1e-6
ALPHA = float(np.float32(4.0 ** 0.25))
FF = 2816
FT = FF // P
HEADS = 8
MLA_SCALE = 96 ** -0.5
SWA_SCALE = 64 ** -0.5
DSA_SCALE = 128 ** -0.5
IDX_W_SCALE = (8 * 64) ** -0.5
TOPK = 256
NKEYS = TP + PAST + TS
SWA_COLS = TP + P + TS
REL_LEN = 1281
REL_BASE = 1151
BIAS_W = TP + P
EVEN_W = 1216
ODD_TILES = 15
VW = 256 + 8
SEQS = ((0, TP), (TP, N))


class Chain:

    def __init__(self, eng, sem):
        self.eng, self.sem, self.n, self.extra = eng, sem, 0, 0

    def link(self, ins, standing=None):
        ins.then_inc(self.sem, 1)
        self.n += 1
        self.eng.wait_ge(self.sem, self.extra + self.n)
        if standing:
            self.eng.sem_inc(standing, 1)

    @contextmanager
    def loop(self, rounds, per, first=0):
        with self.eng.Fori(first, rounds) as i:
            start = self.n
            self.extra = (i - first) * per if first else i * per
            yield i
            assert self.n == start + per, (self.n - start, per)
            self.extra = 0
        self.n = start + per * (rounds - first)


class Machine:

    def __init__(self, nc, ctx, dram):
        self.nc, self.ctx, self.d, self.held = nc, ctx, dram, []
        sb = self.sb
        self.xT = sb("xT", [P, KT, N])
        self.hT = None
        self.mods = sb("mods", [P, 96, 2])
        self.lnp = sb("lnp", [P, 2, 4, KT])
        self.ones = sb("ones", [P, P])
        self.ident = sb("ident", [P, P])
        self.convp = sb("convp", [P, 2, FT, 8])
        self.convs = sb("convs", [P, 2, FT, 4])
        self.convo = sb("convo", [P, 2, FT, 8])
        self.sinks = sb("sinks", [P, HEADS])
        self.gq = sb("gq", [P, 3])
        self.negs = sb("negs", [P, 1])
        self.ps = ctx.enter_context(nc.psum_tensor("ps", [P, 8, 512], F32))
        self.biasd = nc.dram_tensor("rel_scratch", [HEADS, P, REL_LEN], F32, kind="Internal").ap()

    def sb(self, name, shape, ctx=None, dtype=F32):
        return (ctx or self.ctx).enter_context(self.nc.sbuf_tensor("t_" + name, shape, dtype))

    def sem(self, name):
        self.held.append(self.nc.alloc_semaphore(name=name))
        return self.held[-1]

    def recycle(self):
        self.nc.clear_and_free_semaphores(self.held)
        self.nc.all_engine_barrier()
        self.held = []


def spread(ap, k):
    return ap.unsqueeze(1).broadcast_to([ap.shape[0], k, ap.shape[1]])


def segments(t):
    out = []
    for s, (a, b) in enumerate(SEQS):
        lo, hi = max(a, t * NT), min(b, (t + 1) * NT)
        if lo < hi:
            out.append((s, lo - t * NT, hi - lo))
    return out


def toeplitz(m, j0, width):
    return bass.AP(m.biasd.tensor, REL_BASE - TP + j0,
                   [[REL_LEN - 1, P], [P * REL_LEN, HEADS], [1, width]])


def start_stage(m):
    nc, d, ps = m.nc, m.d, m.ps
    with ExitStack() as c:
        NB = 6
        CW = 512
        ROUNDS = 96 * P // (CW * NB)
        TILES = CW // P
        w = m.sb("wada", [P, NB, KT, CW], c)
        rows = m.sb("modrows", [P, 2, CW], c)
        bada = m.sb("bada", [P, 96, 2], c)
        cT = m.sb("cT", [P, KT, 2], c)
        csT = m.sb("csT", [P, KT, 2], c)
        onehot = m.sb("onehot", [32, REL_LEN], c)
        rel = m.sb("rel", [32, HEADS], c)
        relrow = m.sb("relrow", [HEADS, REL_LEN], c)
        wl = [m.sem(f"wada_loaded{i}") for i in range(NB)]
        names = ("par_loaded", "c_loaded", "rel_loaded", "x_loaded", "c_silu", "multiplied", "rowed", "turned", "mods_out",
                 "rows_zeroed", "rel_mm", "rel_ev", "rel_stored", "start_chain")
        S = {n: m.sem(n) for n in names}
        params = [(bada, "bada"), (m.lnp, "lnp"), (m.ident, "ident"), (m.convp, "convp"),
                  (m.convs, "convs"), (m.sinks, "sinks"), (m.gq, "gq"), (m.ones, "ones")]
        with nc.Block() as block:
            @block.sync
            def _(sp):
                for u in range(NB):
                    sp.dma_start(w[:, u], d["wada"][u]).then_inc(wl[u], 16)
                with sp.Fori(1, ROUNDS) as i:
                    for u in range(NB):
                        sp.wait_ge(S["multiplied"], i * NB + (u - NB + 1))
                        sp.dma_start(w[:, u], d["wada"][bass.ds(i * NB + u, 1)]
                                     .rearrange("a p k m -> (a p) k m")).then_inc(wl[u], 16)

            @block.scalar
            def _(act):
                act.dma_start(cT[:], d["cT"]).then_inc(S["c_loaded"], 16)
                act.dma_start(onehot[:], d["onehot"]).then_inc(S["rel_loaded"], 16)
                act.dma_start(rel[:], d["rel_bias"]).then_inc(S["rel_loaded"], 16)
                for tile, name in params:
                    act.dma_start(tile[:], d[name]).then_inc(S["par_loaded"], 16)
                act.dma_start(m.xT[:], d["xT"]).then_inc(S["x_loaded"], 16)
                act.wait_ge(S["c_loaded"], 16)
                nc.scalar.activation(csT[:], cT[:], ACT.Silu).then_inc(S["c_silu"], 1)
                act.wait_ge(S["rel_ev"], 1)
                act.dma_start(m.biasd, spread(relrow[:], P)).then_inc(S["rel_stored"], 16)
                act.wait_ge(S["rows_zeroed"], 1)

                def move(i, first):
                    for u in range(NB):
                        g, q = divmod(u, 3)
                        if not first:
                            act.wait_ge(S["turned"], i * 2 + (g - 1))
                        act.wait_ge(S["multiplied"], i * NB + (u + 1))
                        at = slice(32 * q, 32 * q + 2)
                        nc.scalar.activation(rows[at, g], ps[at, u], ACT.Copy).then_inc(S["rowed"], 1)
                move(0, True)
                with act.Fori(1, ROUNDS) as i:
                    move(i, False)
                act.wait_ge(S["rel_stored"], 16)

            @block.tensor
            def _(pe):
                pe.wait_ge(S["rel_loaded"], 32)
                for q in range(3):
                    n0, n1 = q * 512, min(REL_LEN, (q + 1) * 512)
                    mm = nc.tensor.matmul(ps[0:HEADS, 4 + q, 0:n1 - n0], rel[:], onehot[:, n0:n1],
                                          start=True, stop=True)
                mm.then_inc(S["rel_mm"], 1)
                pe.wait_ge(S["c_silu"], 1)

                def chunk(i, first, u):
                    pe.wait_ge(wl[u], i * 16 + 16)
                    if not first:
                        pe.wait_ge(S["rowed"], i * NB + (u - NB + 1))
                    q = u % 3
                    for k in range(KT):
                        mm = nc.tensor.matmul(ps[32 * q:32 * q + 2, u], csT[:, k], w[:, u, k],
                                              start=k == 0, stop=k == KT - 1)
                    mm.then_inc(S["multiplied"], 1)

                def turn(i, first, g):
                    pe.wait_ge(S["rowed"], i * NB + (3 * g + 3))
                    if not first:
                        pe.wait_ge(S["mods_out"], i * 2 + (g - 1))
                    for j in range(TILES):
                        mm = nc.tensor.matmul(ps[:, 6 + g, P * j:P * (j + 1)], rows[:, g, P * j:P * (j + 1)], m.ident[:],
                                              start=True, stop=True)
                    mm.then_inc(S["turned"], 1)

                def round(i, first):
                    for u in range(NB):
                        if first and u == 4:
                            pe.wait_ge(S["rel_ev"], 1)
                        chunk(i, first, u)
                        if u == 0 and not first:
                            turn(i - 1, isinstance(i, int) and i == 1, 1)
                        if u == 3:
                            turn(i, first, 0)
                pe.wait_ge(S["par_loaded"], 16 * len(params))
                round(0, True)
                round(1, False)
                with pe.Fori(2, ROUNDS) as i:
                    round(i, False)
                turn(ROUNDS - 1, False, 1)

            @block.vector
            def _(dve):
                nc.vector.memset(rows[:], 0.0).then_inc(S["rows_zeroed"], 1)
                nc.vector.memset(m.negs[:], TAKEN)
                dve.wait_ge(S["rel_mm"], 1)
                flat = ps[0:HEADS, 4:7, :].rearrange("p a b -> p (a b)")
                nc.vector.tensor_copy(relrow[:], flat[:, 0:REL_LEN]).then_inc(S["rel_ev"], 1)
                dve.wait_ge(S["par_loaded"], 16 * len(params))
                with dve.Fori(0, ROUNDS) as i:
                    for g in range(2):
                        dve.wait_ge(S["turned"], i * 2 + (g + 1))
                        for q in range(3):
                            at = bass.ds(i * (NB * TILES) + (3 * g + q) * TILES, TILES)
                            src = ps[:, 6 + g].rearrange("p (j s) -> p j s", j=TILES)[:, :, 32 * q:32 * q + 2]
                            ins = nc.vector.tensor_tensor(m.mods[:, at], src, bada[:, at], ALU.add)
                        ins.then_inc(S["mods_out"], 1)
                dve.wait_ge(S["mods_out"], ROUNDS * 2)
                for l in range(2):
                    for t0 in (8, 32):
                        at = m.mods[:, 48 * l + t0:48 * l + t0 + KT]
                        ins = nc.vector.tensor_scalar(at, at, 1.0, None, ALU.add)
                ins.then_inc(S["start_chain"], 1)
                dve.wait_ge(S["start_chain"], 1)
                dve.wait_ge(S["x_loaded"], 16)
                modulate(m, nc.vector, 0, 0)


def modulate(m, eng, layer, part, only=None):
    base = 48 * layer + 24 * part
    ins = None
    for k in range(KT) if only is None else [only]:
        for s, (a, b) in enumerate(SEQS):
            ins = eng.tensor_scalar(m.hT[:, k, a:b], m.xT[:, k, a:b], m.mods[:, base + 8 + k, s:s + 1],
                                    m.mods[:, base + k, s:s + 1], ALU.mult, ALU.add)
    return ins


def down_stage(m, tag, wd, rhs, kt, layer, part, ctx):
    nc, ps = m.nc, m.ps
    w = m.sb("wd" + tag, [P, 2, kt, P], ctx)
    wl = [m.sem(f"wd{tag}_loaded{u}") for u in range(2)]
    ready, added, scaled = m.sem(f"down{tag}_ready"), m.sem(f"down{tag}_added"), m.sem(f"down{tag}_scaled")
    gate = 48 * layer + 24 * part + 16
    BANKS = 2 * NTOK
    with nc.Block() as block:
        @block.sync
        def _(sp):
            for u in range(2):
                sp.dma_start(w[:, u], wd[u]).then_inc(wl[u], 16)
            with sp.Fori(1, KT // 2) as i:
                for u in range(2):
                    sp.wait_ge(ready, i * BANKS + (u - 1) * NTOK)
                    sp.dma_start(w[:, u], wd[bass.ds(i * 2 + u, 1)]
                                 .rearrange("a p k m -> (a p) k m")).then_inc(wl[u], 16)

        @block.tensor
        def _(pe):
            def tiles(i, first):
                for u in range(2):
                    pe.wait_ge(wl[u], i * 16 + 16)
                    for t in range(NTOK):
                        bank = u * NTOK + t
                        if not first:
                            pe.wait_ge(added, i * BANKS + (bank - BANKS + 1))
                        for k in range(kt):
                            mm = nc.tensor.matmul(ps[:, bank, 0:NT], w[:, u, k], rhs[:, k, t * NT:(t + 1) * NT],
                                                  start=k == 0, stop=k == kt - 1)
                        mm.then_inc(ready, 1)
            tiles(0, True)
            with pe.Fori(1, KT // 2) as i:
                tiles(i, False)

        @block.gpsimd
        def _(pool):
            for k in range(KT):
                nc.gpsimd.tensor_scalar(m.xT[:, k], m.xT[:, k], ALPHA, None, ALU.mult).then_inc(scaled, 1)

        @block.vector
        def _(dve):
            with dve.Fori(0, KT // 2) as i:
                for u in range(2):
                    dve.wait_ge(scaled, i * 2 + (u + 1))
                    for t in range(NTOK):
                        bank = u * NTOK + t
                        dve.wait_ge(ready, i * BANKS + (bank + 1))
                        for s, c0, cn in segments(t):
                            x = m.xT[:, bass.ds(i * 2 + u, 1), t * NT + c0:t * NT + c0 + cn] \
                                .rearrange("p a n -> p (a n)")
                            g = m.mods[:, bass.ds(i * 2 + (gate + u), 1), s:s + 1].rearrange("p a n -> p (a n)")
                            ins = nc.vector.scalar_tensor_tensor(x, ps[:, bank, c0:c0 + cn], g, x, ALU.mult, ALU.add)
                        ins.then_inc(added, 1)


def norm_stage(m, layer, part, split=None, final=False):
    nc, ps = m.nc, m.ps
    tag = f"{layer}{part}"
    names = ("centred", "squared", "summed", "mean", "inv", "root", "chain", "scaled", "shifted", "h", "stored")
    S = {n: m.sem(f"ln{tag}_{n}") for n in names}
    base = 48 * (layer + part) + 24 * (1 - part)
    with ExitStack() as c:
        rs = m.sb("rs" + tag, [P, N], c)
        cols = [slice(t * NT, (t + 1) * NT) for t in range(NTOK)]
        with nc.Block() as block:
            @block.tensor
            def _(pe):
                for t in range(NTOK):
                    for k in range(KT):
                        mm = nc.tensor.matmul(ps[:, t, 0:NT], m.ones[:], m.xT[:, k, cols[t]],
                                              start=k == 0, stop=k == KT - 1)
                    mm.then_inc(S["mean"], 1)
                for t in range(NTOK):
                    pe.wait_ge(S["squared"], t + 1)
                    for k in range(KT):
                        mm = nc.tensor.matmul(ps[:, NTOK + t, 0:NT], m.ones[:], m.hT[:, k, cols[t]],
                                              start=k == 0, stop=k == KT - 1)
                    mm.then_inc(S["summed"], 1)

            @block.scalar
            def _(act):
                def modulate_tile(k):
                    act.wait_ge(S["shifted"], k + 1)
                    for s, (a, b) in enumerate(SEQS):
                        ins = nc.scalar.activation(m.hT[:, k, a:b], m.xT[:, k, a:b], ACT.Identity,
                                                   bias=m.mods[:, base + k, s:s + 1], scale=m.mods[:, base + 8 + k, s:s + 1])
                    ins.then_inc(S["h"], 1)

                for t in range(NTOK):
                    act.wait_ge(S["centred"], t + 1)
                    nc.scalar.activation(m.hT[:, :, cols[t]], m.xT[:, :, cols[t]], ACT.Square).then_inc(S["squared"], 1)
                for t in range(NTOK):
                    act.wait_ge(S["inv"], t + 1)
                    nc.scalar.activation(rs[:, cols[t]], rs[:, cols[t]], ACT.Sqrt).then_inc(S["root"], 1)
                act.wait_ge(S["summed"], NTOK)
                for k in range(KT):
                    act.wait_ge(S["scaled"], k + 1)
                    nc.scalar.activation(m.xT[:, k], m.xT[:, k], ACT.Identity,
                                         bias=m.lnp[:, layer, 2 * part + 1, k:k + 1]).then_inc(S["shifted"], 1)
                    if not final and k:
                        modulate_tile(k - 1)
                if not final:
                    modulate_tile(KT - 1)

            @block.vector
            def _(dve):
                chain = Chain(dve, S["chain"])
                for t in range(NTOK):
                    dve.wait_ge(S["mean"], t + 1)
                    x = m.xT[:, :, cols[t]]
                    nc.vector.tensor_tensor(x, x, spread(ps[:, t, 0:NT], KT), ALU.subtract).then_inc(S["centred"], 1)
                for t in range(NTOK):
                    dve.wait_ge(S["summed"], t + 1)
                    chain.link(nc.vector.tensor_scalar(rs[:, cols[t]], ps[:, NTOK + t, 0:NT], LN_EPS, None, ALU.add))
                    nc.vector.reciprocal(rs[:, cols[t]], rs[:, cols[t]]).then_inc(S["inv"], 1)
                dve.wait_ge(S["centred"], NTOK)
                dve.wait_ge(S["root"], NTOK)
                for k in range(KT):
                    nc.vector.scalar_tensor_tensor(m.xT[:, k], m.xT[:, k], m.lnp[:, layer, 2 * part, k:k + 1], rs[:],
                                                   ALU.mult, ALU.mult).then_inc(S["scaled"], 1)
                if split:
                    hi, lo = split
                    for k in range(KT):
                        dve.wait_ge(S["h"], k + 1)
                        chain.link(nc.vector.tensor_copy(hi[:, k], m.hT[:, k]))
                        nc.vector.tensor_tensor(lo[:, k], m.hT[:, k], hi[:, k].bitcast(F32), ALU.subtract)

            if final:
                @block.sync
                def _(sp):
                    for k in range(KT):
                        sp.wait_ge(S["shifted"], k + 1)
                        sp.dma_start(m.d["yT"][:, k], m.xT[:, k]).then_inc(S["stored"], 16)
                    sp.wait_ge(S["stored"], 16 * KT)


def wait(eng, sem, value):
    if not isinstance(value, int) or value > 0:
        eng.wait_ge(sem, value)


def row(tile, at):
    if isinstance(at, int):
        return tile[:, at]
    return tile[:, bass.ds(at, 1)].rearrange("p a n -> p (a n)")


class FfnPlan:
    PARTS = (6, 6, 5, 5)

    def __init__(self):
        self.items = []
        j = 0
        starts = [sum(self.PARTS[:f]) for f in range(4)]
        for f, n in enumerate(self.PARTS):
            if f == 0:
                self.items.append(("up", 0, n, 0))
            else:
                self.items.append(("up", starts[f] + 1, n - 1, f))
            if f < 3:
                self.items.append(("up", starts[f + 1], 1, f + 1))
            self.items.append(("down", starts[f], n, f))
        self.starts = starts

    def slot(self, j):
        f = max(f for f in range(4) if self.starts[f] <= j)
        r = j - self.starts[f]
        return r if r else 6 * (f % 2)

    def walk(self):
        tiles = downs = 0
        for kind, j, n, f in self.items:
            yield kind, j, n, f, tiles, downs
            tiles += 2 * n if kind == "up" else KT
            downs += kind == "down"


def ffn_stage(m, layer, hh, hl, ctx):
    nc, ps, d = m.nc, m.ps, m.d
    PAD = 2
    UW = N + 2 * PAD
    S0 = TP + 2 * PAD
    YW = UW - PAD
    UNITS = 2 * NTOK
    gate = 48 * layer + 24 + 16
    plan = FfnPlan()
    sh = m.sb(f"sh{layer}", [P, 7, N], ctx, F32R)
    sl = m.sb(f"sl{layer}", [P, 7, N], ctx, F32R)
    raw = m.sb(f"wraw{layer}", [P, 2, KT, P], ctx)
    wh = m.sb(f"wh{layer}", [P, 2, KT, P], ctx, F32R)
    wlo = m.sb(f"wlo{layer}", [P, 2, KT, P], ctx, F32R)
    u_ = m.sb(f"u{layer}", [P, 2, UW], ctx)
    y = m.sb(f"y{layer}", [P, 2, YW], ctx)
    cp = m.sb(f"cp{layer}", [P, 8], ctx)
    loaded = [m.sem(f"w{layer}_loaded{b}") for b in range(2)]
    names = ("w_hi", "w_lo", "u_ready", "u_moved", "down_ready", "added", "staged", "tap0", "tap2", "silu",
             "convolved", "gated", "kept", "zeroed", "scaled", "turns", "chain")
    S = {n: m.sem(f"ffn{layer}_{n}") for n in names}

    def rounds(eng, kind, n, body, uniform):
        count = n if kind == "up" else KT // 2
        first = 0 if uniform else 1
        if first:
            body(0)
        if count - first == 1:
            body(first)
        elif count > first:
            with eng.Fori(first, count) as r:
                body(r)

    with nc.Block() as block:
        @block.sync
        def _(sp):
            for kind, j, n, f, tiles, downs in plan.walk():
                def body(r):
                    for b in range(2):
                        i = tiles + 2 * r + b
                        wait(sp, S["w_lo"], i - 1)
                        if kind == "up":
                            src = row(d["wfi"][layer].rearrange("j p h k m -> p j h k m"), j + r)[:, b] \
                                if isinstance(r, int) else \
                                d["wfi"][layer, bass.ds(r + j, 1)].rearrange("a p h k m -> (a p) h k m")[:, b]
                            to = raw[:, b]
                        else:
                            at = r * 2 + b
                            src = d["wfo"][layer, at] if isinstance(r, int) else \
                                d["wfo"][layer, bass.ds(at, 1)].rearrange("a p k m -> (a p) k m")
                            src, to = src[:, j:j + n], raw[:, b, 0:n]
                        sp.dma_start(to, src).then_inc(loaded[b], 16)
                rounds(sp, kind, n, body, tiles > 0)

        @block.gpsimd
        def _(pool):
            def used(item, r, b):
                kind, j, n, f, tiles, downs = item
                if kind == "up":
                    pool.wait_ge(S["u_ready"], r * UNITS + (j * UNITS + (b + 1) * NTOK))
                else:
                    pool.wait_ge(S["down_ready"], r * UNITS + (downs * KT * NTOK + (b + 1) * NTOK))

            before = None
            nc.gpsimd.memset(u_[:, :, 0:PAD], 0.0).then_inc(S["zeroed"], 1)
            for item in plan.walk():
                kind, j, n, f, tiles, downs = item

                def body(r):
                    for b in range(2):
                        i = tiles + 2 * r + b
                        k = KT if kind == "up" else n
                        pool.wait_ge(loaded[b], r * 16 + (8 * tiles + 16))
                        if not (isinstance(r, int) and r == 0):
                            used(item, r - 1, b)
                        elif before:
                            used(before, (before[2] if before[0] == "up" else KT // 2) - 1, b)
                        pool.sem_inc(S["turns"], 1)
                        nc.gpsimd.tensor_copy(wh[:, b, 0:k], raw[:, b, 0:k]).then_inc(S["w_hi"], 1)
                    if kind == "up":
                        at = j + r
                        if isinstance(r, int):
                            pick = lambda t: t[:, layer, at]
                        else:
                            pick = lambda t: t[:, layer, bass.ds(at, 1)].rearrange("p a n -> p (a n)")
                        wait(pool, S["convolved"], at)
                        wait(pool, S["kept"], at)
                        pool.sem_inc(S["turns"], 1)
                        nc.gpsimd.tensor_copy(cp[:], pick(m.convp))
                        nc.gpsimd.tensor_copy(u_[:, :, TP + PAD:S0], pick(m.convs).rearrange("p (h c) -> p h c", h=2)) \
                            .then_inc(S["staged"], 1)
                rounds(pool, kind, n, body, False)
                before = item

        @block.tensor
        def _(pe):
            def product(bank, k_tiles, b, hi, lo, cols, slots):
                last = 3 * k_tiles - 1
                n = 0
                for k in range(k_tiles):
                    for w, x in ((wh, hi), (wh, lo), (wlo, hi)):
                        mm = nc.tensor.matmul(ps[:, bank, 0:NT], w[:, b, k], x[:, slots[k], cols],
                                              start=n == 0, stop=n == last)
                        n += 1
                return mm

            for kind, j, n, f, tiles, downs in plan.walk():
                def body(r):
                    for b in range(2):
                        i = tiles + 2 * r + b
                        pe.wait_ge(S["w_lo"], i + 1)
                        for t in range(NTOK):
                            bank = b * NTOK + t
                            cols = slice(t * NT, (t + 1) * NT)
                            first = isinstance(r, int) and r == 0
                            if kind == "up":
                                if first and downs and n > 1:
                                    wait(pe, S["added"], downs * KT * NTOK - UNITS + bank + 1)
                                else:
                                    wait(pe, S["u_moved"], (j + r) * UNITS + (bank + 1 - UNITS))
                                mm = product(bank, KT, b, hh, hl, cols, range(KT))
                                mm.then_inc(S["u_ready"], 1)
                            else:
                                ups = plan.starts[f + 1] + 1 if f < 3 else FT
                                if first:
                                    if b == 0 and t == 0:
                                        pe.wait_ge(S["gated"], j + n)
                                    wait(pe, S["u_moved"], (ups - 1) * UNITS + bank + 1)
                                else:
                                    pe.wait_ge(S["added"], downs * (KT * NTOK) + r * UNITS + (bank + 1 - UNITS))
                                mm = product(bank, n, b, sh, sl, cols, [plan.slot(j + k) for k in range(n)])
                                mm.then_inc(S["down_ready"], 1)
                rounds(pe, kind, n, body, False)

        @block.scalar
        def _(act):
            for k in range(KT):
                nc.scalar.activation(m.xT[:, k], m.xT[:, k], ACT.Copy, scale=ALPHA).then_inc(S["scaled"], 1)
            act.wait_ge(S["zeroed"], 1)
            for kind, j, n, f, tiles, downs in plan.walk():
                if kind == "down":
                    continue

                def body(r):
                    at = j + r
                    act.wait_ge(S["staged"], at + 1)
                    for q in range(UNITS):
                        half, t = divmod(q, NTOK)
                        act.wait_ge(S["u_ready"], at * UNITS + (q + 1))
                        for s, c0, cn in segments(t):
                            to = t * NT + c0 + PAD * (s + 1)
                            ins = nc.scalar.activation(u_[:, half, to:to + cn], ps[:, q, c0:c0 + cn], ACT.Copy)
                        ins.then_inc(S["u_moved"], 1)
                    act.wait_ge(S["u_moved"], (at + 1) * UNITS)
                    wait(act, S["gated"], at)
                    for half in range(2):
                        nc.scalar.activation(y[:, half], u_[:, half, 0:YW], ACT.Identity,
                                             bias=cp[:, 4 * half + 3:4 * half + 4],
                                             scale=cp[:, 4 * half:4 * half + 1]).then_inc(S["tap0"], 1)
                    act.wait_ge(S["tap2"], at + 1)
                    nc.scalar.activation(y[:, 1], y[:, 1], ACT.Silu).then_inc(S["silu"], 1)
                rounds(act, kind, n, body, tiles > 0)

        @block.vector
        def _(dve):
            chain = Chain(dve, S["chain"])

            def split_lo(kind, n, i, b):
                k = KT if kind == "up" else n
                dve.wait_ge(S["w_hi"], i + 1)
                nc.vector.tensor_tensor(wlo[:, b, 0:k], raw[:, b, 0:k], wh[:, b, 0:k].bitcast(F32), ALU.subtract) \
                    .then_inc(S["w_lo"], 1)

            items = list(plan.walk())
            for b in range(2):
                split_lo("up", 1, b, b)
            for at_item, (kind, j, n, f, tiles, downs) in enumerate(items):
                count = n if kind == "up" else KT // 2
                nxt = items[at_item + 1] if at_item + 1 < len(items) else None

                def following(r, b):
                    if isinstance(r, int) and r == count - 1:
                        if nxt:
                            split_lo(nxt[0], nxt[2], nxt[4] + b, b)
                    else:
                        split_lo(kind, n, tiles + 2 * (r + 1) + b, b)

                def up(r):
                    at = j + r
                    following(r, 0)
                    following(r, 1)
                    dve.wait_ge(S["tap0"], at * 2 + 2)
                    for tap in (1, 2):
                        for half in (1, 0):
                            ins = nc.vector.scalar_tensor_tensor(
                                y[:, half], u_[:, half, tap:tap + YW], cp[:, 4 * half + tap:4 * half + tap + 1],
                                y[:, half], ALU.mult, ALU.add)
                            if (tap, half) == (2, 1):
                                ins.then_inc(S["tap2"], 1)
                            elif (tap, half) == (2, 0):
                                ins.then_inc(S["convolved"], 1)
                            else:
                                chain.link(ins)
                    for s, c0 in enumerate((TP, UW - PAD)):
                        to = m.convo[:, layer, at, 4 * s:4 * s + 4] if isinstance(r, int) else \
                            m.convo[:, layer, bass.ds(at, 1), 4 * s:4 * s + 4].rearrange("p a n -> p (a n)")
                        ins = nc.vector.tensor_copy(to.rearrange("p (h c) -> p h c", h=2), u_[:, :, c0:c0 + PAD])
                    ins.then_inc(S["kept"], 1)
                    dve.wait_ge(S["convolved"], at + 1)
                    dve.wait_ge(S["silu"], at + 1)
                    chain.link(nc.vector.tensor_tensor(y[:, 0], y[:, 0], y[:, 1], ALU.mult))
                    if downs:
                        dve.wait_ge(S["down_ready"], downs * (KT * NTOK))
                    slot = plan.slot(j + r) if isinstance(r, int) else r + plan.slot(j + 1) - 1
                    pick = lambda t, a, e: t[:, slot, a:e] if isinstance(r, int) else \
                        t[:, bass.ds(slot, 1), a:e].rearrange("p a n -> p (a n)")
                    for s, (a, e) in enumerate(SEQS):
                        ins = nc.vector.tensor_copy(pick(sh, a, e), y[:, 0, a + PAD * s:e + PAD * s])
                    chain.link(ins)
                    for s, (a, e) in enumerate(SEQS):
                        ins = nc.vector.tensor_tensor(pick(sl, a, e), y[:, 0, a + PAD * s:e + PAD * s],
                                                      pick(sh, a, e).bitcast(F32), ALU.subtract)
                    ins.then_inc(S["gated"], 1)

                def down(r):
                    for b in range(2):
                        following(r, b)
                        for t in range(NTOK):
                            bank = b * NTOK + t
                            dve.wait_ge(S["down_ready"], downs * (KT * NTOK) + r * UNITS + (bank + 1))
                            for s, c0, cn in segments(t):
                                cols = slice(t * NT + c0, t * NT + c0 + cn)
                                tile = r * 2 + b
                                if isinstance(r, int):
                                    x, g = m.xT[:, tile, cols], m.mods[:, gate + tile, s:s + 1]
                                else:
                                    x = m.xT[:, bass.ds(tile, 1), cols].rearrange("p a n -> p (a n)")
                                    g = m.mods[:, bass.ds(tile + gate, 1), s:s + 1].rearrange("p a n -> p (a n)")
                                ins = nc.vector.scalar_tensor_tensor(x, ps[:, bank, c0:c0 + cn], g, x, ALU.mult, ALU.add)
                            ins.then_inc(S["added"], 1)

                if kind == "down" and downs == 0:
                    dve.wait_ge(S["scaled"], KT)
                if kind == "down" and downs:
                    dve.wait_ge(S["added"], downs * KT * NTOK)
                body = up if kind == "up" else down
                per = 4 if kind == "up" else 0
                lo, hi = (1 if kind == "up" and f == 0 else 0), count - 1
                for r in range(lo):
                    body(r)
                if hi > lo:
                    if hi - lo == 1:
                        body(lo)
                    else:
                        with chain.loop(hi, per, lo) as r:
                            body(r)
                if hi >= lo:
                    body(hi)


class Keys:

    def __init__(self, q0, nq, key_tiles, sample=False, wide=False):
        self.q0, self.nq, self.tiles = q0, nq, key_tiles
        self.nk = sum(t[1] for t in key_tiles)
        self.sample, self.wide = sample, wide
        self.s_bank = (0, 3) if wide else (0, 2)
        self.t_banks = (6,) if wide else (4, 5)
        self.o_banks = (7, 7) if wide else (6, 7)
        self.per = 16 if wide else 4
        self.groups = -(-len(key_tiles) // self.per)
        at, self.offsets = 0, []
        for col, size, v in key_tiles:
            self.offsets.append((at, size, v))
            at += size

    def bank(self, ps, u):
        b = self.s_bank[u]
        return ps[0:self.nq, b:b + 3 if self.wide else b + 2, :].rearrange("p a b -> p (a b)")[:, 0:self.nk]


IDX_CHUNK = 384
SEL_ROUNDS = 5


class Selection:

    def __init__(self, n, kb, buffers, units0):
        self.n, self.kb, self.score = n, kb, buffers[n % 2]
        self.units0 = units0
        self.chunks = [(a, min(kb.nk, a + IDX_CHUNK)) for a in range(0, kb.nk, IDX_CHUNK)]


def attention_stage(m, tag, blocks, kind, q_of, k_of, v_of, dv, rows, out_tile, bias_w=0, bias_of=None,
                    sink=False, index=None, sels=None, out=None, osb=None):
    nc, ps = m.nc, m.ps
    out = m.hT if out is None else out
    sels = sels or {}
    names = ("q_staged", "s_ready", "max_ready", "p_ready", "t_ready", "t_moved", "o_ready", "o_moved",
             "inv_ready", "chain") + ("pchain", "turns", "pool_turns") * bool(bias_w) + \
        ("mask_ready", "relu_free") * bool(index)
    S = {n: m.sem(f"{tag}_{n}") for n in names}
    s_free = S["max_ready"] if bias_w else S["p_ready"]
    c = ExitStack()
    with c:
        qst = m.sb(tag + "qst", [P, 2, P], c)
        prob = m.sb(tag + "prob", [P, 2, max(kb.nk for kb in blocks)], c)
        probT = m.sb(tag + "probT", [P, 2, max(len(kb.tiles) * kb.nq for kb in blocks)], c)
        if osb is None:
            osb = m.sb(tag + "osb", [P, min(2, len(blocks)), HEADS * dv], c)
        stat = m.sb(tag + "stat", [P, 2, 8], c)
        bm = m.sb(tag + "bm", [P, 2, bias_w], c) if bias_w else None
        if index:
            relu = m.sb(tag + "relu", [P, 2, IDX_CHUNK], c)
            best = m.sb(tag + "best", [P, 8], c)
        OT = HEADS * dv // P
        OG = -(-OT // 4)

        plan = []
        for n, kb in enumerate(blocks):
            G = kb.groups
            p = dict(kb=kb, n=n, pair=8 * n, G=G, prev=plan[-1] if plan else None)
            p["T"] = (plan[-1]["end"] if plan else 0)
            at = p["T"] + 7 * G
            p["O_prev"] = at
            at += OG if plan else 0
            p["select"] = sels.get(n + 1) if index else None
            p["index"] = sels.get(n + 2) if index else None
            p["I"] = at
            at += 8 * len(p["index"].chunks) if p["index"] else 0
            p["T7"] = at
            p["end"] = at + G
            if plan:
                plan[-1]["next"] = p
            p["next"] = None
            plan.append(p)
        last = plan[-1]

        def t_group(p, t, u):
            if isinstance(t, int) and 2 * t + u == 7:
                return p["T7"]
            return p["T"] + t * (2 * p["G"]) + u * p["G"]

        def t_bank(p, t, u, g):
            first = t_group(p, t if isinstance(t, int) else 0, u)
            return p["kb"].t_banks[(first + g) % len(p["kb"].t_banks)]

        def slots(eng, p, slot, chain=None, per=0, peel=False):
            first = 1 if p["n"] == 0 or peel else 0
            if p["kb"].sample:
                first = 3
            for t in range(first):
                slot(t, 0)
                slot(t, 1)
            if first < 3:
                with chain.loop(3, per, first) if chain else eng.Fori(first, 3) as t:
                    slot(t, 0)
                    slot(t, 1)

        def after(p, t, u, k):
            j = u + k
            t, u = t + j // 2, j % 2
            if isinstance(t, int) and t > 3:
                return (p["next"], t - 4, u) if p["next"] else None
            if isinstance(t, int) and t < 0:
                return (p["prev"], t + 4, u) if p["prev"] else None
            return p, t, u

        def count(p, t, u):
            return p["pair"] + t * 2 + u

        with nc.Block() as block:
            @block.gpsimd
            def _(pool):
                chain = Chain(pool, S["pchain"]) if bias_w else None
                for p in plan:
                    kb, nq = p["kb"], p["kb"].nq
                    sel = sels.get(p["n"])
                    masked = not kb.sample and not sel
                    banded = kind == "swa" and not kb.sample and p["n"] > 0

                    def body(t):
                        for u in range(2):
                            n = count(p, t, u)
                            wait(pool, S["s_ready"], n - 1)
                            if bias_w:
                                wait(pool, s_free, n - 1)
                                bt = bias_of(t + 4 * u, kb)
                                to = bm[0:nq, u, 0:kb.nk]
                                standing = S["pool_turns"]
                                if sel:
                                    if u == 0 and index:
                                        pool.wait_ge(S["mask_ready"], sel.n + 1)
                                    chain.link(nc.gpsimd.tensor_tensor(to, bt, sel.score[0:nq, 0:kb.nk], ALU.add))
                                else:
                                    chain.link(nc.gpsimd.tensor_copy(to, bt), standing)
                                if masked:
                                    chain.link(nc.gpsimd.memset(bm[0:CHUNK, u, kb.nk - CHUNK:kb.nk], NEG), standing)
                                if banded:
                                    chain.link(nc.gpsimd.memset(bm[CHUNK:P, u, 0:CHUNK], NEG))
                            nc.gpsimd.tensor_copy(qst[rows(u), u, 0:nq], q_of(t, u, kb)).then_inc(S["q_staged"], 1)
                            if kind == "swa":
                                pool.wait_ge(S["q_staged"], n + 1)
                    per = 2 * (1 + masked + banded) if bias_w else 0
                    first = 4 if kb.sample else p["n"] == 0
                    for t in range(first):
                        body(t)
                    if first < 4:
                        with chain.loop(4, per, int(first)) if chain else pool.Fori(int(first), 4) as t:
                            body(t)

            @block.tensor
            def _(pe):
                def scores(p, t, u):
                    kb, n = p["kb"], count(p, t, u)
                    pe.wait_ge(S["q_staged"], n + 1)
                    wait(pe, s_free, n - 1)
                    s = kb.bank(ps, u)
                    for n0 in range(0, kb.nk, 512):
                        n1 = min(kb.nk, n0 + 512)
                        mm = nc.tensor.matmul(s[:, n0:n1], qst[rows(u), u, 0:kb.nq], k_of(t, u, kb, n0, n1),
                                              start=True, stop=True)
                    mm.then_inc(S["s_ready"], 1)

                def transposes(p, t, u):
                    kb, nq = p["kb"], p["kb"].nq
                    pe.wait_ge(S["p_ready"], count(p, t, u) + 1)
                    for g in range(p["G"]):
                        wait(pe, S["t_moved"], t_group(p, t, u) + (g - len(kb.t_banks) + 1))
                        for j, (at, size, _) in enumerate(kb.offsets[g * kb.per:(g + 1) * kb.per]):
                            mm = nc.tensor.transpose(ps[0:size, t_bank(p, t, u, g), j * nq:(j + 1) * nq],
                                                     prob[0:nq, u, at:at + size], m.ident[0:nq, 0:nq])
                        mm.then_inc(S["t_ready"], 1)

                def values(p, t, u):
                    kb, nq, n = p["kb"], p["kb"].nq, count(p, t, u)
                    pe.wait_ge(S["t_moved"], t_group(p, t, u) + p["G"])
                    wait(pe, S["o_moved"], n if kb.wide else n - 1)
                    for j, (at, size, v) in enumerate(kb.offsets):
                        mm = nc.tensor.matmul(ps[0:nq, kb.o_banks[u], 0:dv], probT[0:size, u, j * nq:(j + 1) * nq],
                                              v_of(t, u, v, size), start=j == 0, stop=j == len(kb.offsets) - 1)
                    mm.then_inc(S["o_ready"], 1)

                def outputs(p, first):
                    kb, nq = p["kb"], p["kb"].nq
                    pe.wait_ge(S["o_moved"], p["pair"] + 8)
                    for g in range(OG):
                        wait(pe, S["t_moved"], first + g - len(kb.t_banks) + 1)
                        bank = kb.t_banks[(first + g) % len(kb.t_banks)]
                        for j in range(min(4, OT - 4 * g)):
                            cols = slice((4 * g + j) * P, (4 * g + j + 1) * P)
                            mm = nc.tensor.transpose(ps[:, bank, j * nq:(j + 1) * nq], osb[0:nq, p["n"] % 2, cols],
                                                     m.ident[0:nq, 0:nq])
                        mm.then_inc(S["t_ready"], 1)

                def index_scores(p, s):
                    kb, nq, g = s.kb, s.kb.nq, p["I"]
                    for h in range(8):
                        r = slice(64 * (h % 2), 64 * (h % 2) + 64)
                        for a, b in s.chunks:
                            wait(pe, S["t_moved"], g - 1)
                            k0 = kb.tiles[0][0]
                            nc.tensor.matmul(ps[0:nq, 4 + g % 2, 0:b - a], index["q"][r, h // 2, kb.q0:kb.q0 + nq],
                                             index["k"][r, k0 + a:k0 + b], start=True, stop=True).then_inc(S["t_ready"], 1)
                            g += 1

                def slot(p, t, u):
                    for k, do in ((2, scores), (1, transposes), (0, values)):
                        at = after(p, t, u, k)
                        if at:
                            do(*at)
                scores(plan[0], 0, 0)
                scores(plan[0], 0, 1)
                transposes(plan[0], 0, 0)
                for p in plan:
                    slots(pe, p, lambda t, u: slot(p, t, u))
                    if p["prev"]:
                        outputs(p["prev"], p["O_prev"])
                    if p["index"]:
                        index_scores(p, p["index"])
                    slot(p, 3, 0)
                    slot(p, 3, 1)
                outputs(last, last["end"])

            @block.scalar
            def _(act):
                def exps(p, t, u):
                    kb, nq, n = p["kb"], p["kb"].nq, count(p, t, u)
                    act.wait_ge(S["max_ready"], n + 1)
                    wait(act, S["inv_ready"], n - 1)
                    if not bias_w:
                        prev = after(p, t, u, -2)
                        if prev:
                            wait(act, S["t_ready"], t_group(*prev) + prev[0]["G"])
                    src = prob[0:nq, u, 0:kb.nk] if bias_w else kb.bank(ps, u)
                    ins = nc.scalar.activation(prob[0:nq, u, 0:kb.nk], src, ACT.Exp, bias=stat[0:nq, u, 1:2],
                                               accum_out=stat[0:nq, u, 2:3])
                    if sink:
                        ins = nc.scalar.activation(stat[0:nq, u, 4:5], stat[0:nq, u, 5:6], ACT.Exp,
                                                   bias=stat[0:nq, u, 1:2])
                    ins.then_inc(S["p_ready"], 1)

                def move(p, t, u):
                    kb, nq = p["kb"], p["kb"].nq
                    for g in range(p["G"]):
                        act.wait_ge(S["t_ready"], t_group(p, t, u) + (g + 1))
                        bank = t_bank(p, t, u, g)
                        part = kb.offsets[g * kb.per:(g + 1) * kb.per]
                        at, full = g * kb.per * nq, sum(size == P for _, size, _ in part)
                        ins = nc.scalar.activation(probT[:, u, at:at + full * nq], ps[:, bank, 0:full * nq], ACT.Copy)
                        if full < len(part):
                            ins = nc.scalar.activation(probT[0:TS, u, at + full * nq:at + (full + 1) * nq],
                                                       ps[0:TS, bank, full * nq:(full + 1) * nq], ACT.Copy)
                        ins.then_inc(S["t_moved"], 1)

                def normed(p, t, u):
                    kb, nq, n = p["kb"], p["kb"].nq, count(p, t, u)
                    act.wait_ge(S["o_ready"], n + 1)
                    act.wait_ge(S["inv_ready"], n + 1)
                    cols = bass.ds((t + 4 * u) * dv, dv)
                    nc.scalar.activation(osb[0:nq, p["n"] % 2, cols], ps[0:nq, kb.o_banks[u], 0:dv], ACT.Copy,
                                         scale=stat[0:nq, u, 3:4]).then_inc(S["o_moved"], 1)

                def outputs(p, first):
                    kb, nq = p["kb"], p["kb"].nq
                    for g in range(OG):
                        act.wait_ge(S["t_ready"], first + g + 1)
                        bank = kb.t_banks[(first + g) % len(kb.t_banks)]
                        k = min(4, OT - 4 * g)
                        nc.scalar.activation(out[:, out_tile + 4 * g:out_tile + 4 * g + k, kb.q0:kb.q0 + nq],
                                             ps[:, bank, 0:k * nq].rearrange("p (a n) -> p a n", a=k),
                                             ACT.Copy).then_inc(S["t_moved"], 1)

                def index_relu(p, s):
                    nq, g = s.kb.nq, p["I"]
                    for n in range(8 * len(s.chunks)):
                        a, b = s.chunks[n % len(s.chunks)]
                        act.wait_ge(S["t_ready"], g + 1)
                        wait(act, S["relu_free"], s.units0 + n - 1)
                        nc.scalar.activation(relu[0:nq, n % 2, 0:b - a], ps[0:nq, 4 + g % 2, 0:b - a], ACT.Relu) \
                            .then_inc(S["t_moved"], 1)
                        g += 1

                def slot(p, t, u, skip_move=False):
                    for k, do in ((0, move), (1, exps), (-1, normed)):
                        at = after(p, t, u, k)
                        if at and not (skip_move and do is move):
                            do(*at)
                exps(plan[0], 0, 0)
                for p in plan:
                    slots(act, p, lambda t, u: slot(p, t, u), peel=True)
                    move(p, 3, 0)
                    if p["prev"]:
                        outputs(p["prev"], p["O_prev"])
                    if p["index"]:
                        index_relu(p, p["index"])
                    slot(p, 3, 0, skip_move=True)
                    slot(p, 3, 1)
                normed(last, 3, 1)
                outputs(last, last["end"])

            @block.vector
            def _(dve):
                chain = Chain(dve, S["chain"])

                def maxima(p, t, u):
                    kb, nq, nk, n = p["kb"], p["kb"].nq, p["kb"].nk, count(p, t, u)
                    dve.wait_ge(S["s_ready"], n + 1)
                    s = kb.bank(ps, u)
                    wait(dve, S["p_ready"], n - 1)
                    if sink:
                        chain.link(nc.vector.tensor_copy(stat[0:nq, u, 5:6], m.sinks[0:nq, bass.ds(t + 4 * u, 1)]))
                    if bias_w:
                        prev = after(p, t, u, -2)
                        if prev:
                            wait(dve, S["t_ready"], t_group(*prev) + prev[0]["G"])
                        dve.sem_inc(S["turns"], 1)
                        chain.link(nc.vector.tensor_tensor_reduce(
                            out=prob[0:nq, u, 0:nk], in0=s, in1=bm[0:nq, u, 0:nk], scale=1.0,
                            scalar=stat[0:nq, u, 5:6] if sink else m.negs[0:nq],
                            op0=ALU.add, op1=ALU.max, accum_out=stat[0:nq, u, 0:1]))
                        nc.vector.tensor_scalar(stat[0:nq, u, 1:2], stat[0:nq, u, 0:1], -1.0, None, ALU.mult) \
                            .then_inc(S["max_ready"], 1)
                    else:
                        if not kb.sample:
                            chain.link(nc.vector.memset(s[0:CHUNK, nk - CHUNK:nk], NEG))
                        nc.vector.tensor_reduce(stat[0:nq, u, 1:2], s, AX.X, ALU.max, negate=True) \
                            .then_inc(S["max_ready"], 1)

                def inverse(p, t, u):
                    nq, n = p["kb"].nq, count(p, t, u)
                    dve.wait_ge(S["p_ready"], n + 1)
                    wait(dve, S["o_moved"], n - 1)
                    if sink:
                        chain.link(nc.vector.tensor_tensor(stat[0:nq, u, 2:3], stat[0:nq, u, 2:3],
                                                           stat[0:nq, u, 4:5], ALU.add))
                    nc.vector.reciprocal(stat[0:nq, u, 3:4], stat[0:nq, u, 2:3]).then_inc(S["inv_ready"], 1)

                def select(s, k):
                    sc = s.score[0:s.kb.nq, 0:s.kb.nk]
                    for _ in range(k):
                        chain.link(nc.vector.max(best[0:s.kb.nq], sc), S["turns"])
                        chain.link(nc.vector.match_replace(sc, best[0:s.kb.nq], sc, TAKEN), S["turns"])

                def mask(s):
                    sc = s.score[0:s.kb.nq, 0:s.kb.nk]
                    ins = nc.vector.tensor_scalar(sc, sc, TAKEN / 2, NEG, ALU.is_gt, ALU.mult)
                    if not s.kb.sample:
                        chain.link(ins)
                        ins = nc.vector.memset(s.score[0:CHUNK, s.kb.nk - CHUNK:s.kb.nk], NEG)
                    ins.then_inc(S["mask_ready"], 1)

                def index_sums(p, s):
                    kb, nq = s.kb, s.kb.nq
                    dve.wait_ge(S["q_staged"], p["pair"] + 8)
                    for n in range(8 * len(s.chunks)):
                        h, (a, b) = n // len(s.chunks), s.chunks[n % len(s.chunks)]
                        dve.wait_ge(S["t_moved"], p["I"] + n + 1)
                        wi = index["w"][0:nq, kb.q0 // P, h:h + 1]
                        sc, src = s.score[0:nq, a:b], relu[0:nq, n % 2, 0:b - a]
                        if h == 0:
                            ins = nc.vector.tensor_scalar(sc, src, wi, None, ALU.mult)
                        else:
                            dve.wait_ge(S["relu_free"], s.units0 + n + 1 - len(s.chunks))
                            ins = nc.vector.scalar_tensor_tensor(sc, src, wi, sc, ALU.mult, ALU.add)
                        ins.then_inc(S["relu_free"], 1)
                    dve.wait_ge(S["relu_free"], s.units0 + 8 * len(s.chunks))
                    if not kb.sample:
                        chain.link(nc.vector.memset(s.score[0:CHUNK, kb.nk - CHUNK:kb.nk], NEG))

                def slot(p, t, u):
                    at = after(p, t, u, 1)
                    if at:
                        maxima(*at)
                    inverse(p, t, u)
                    if p["select"] and not (isinstance(t, int) and t == 3):
                        select(p["select"], SEL_ROUNDS)
                maxima(plan[0], 0, 0)
                for p in plan:
                    per = (1 + 2 * sink) if bias_w else int(not p["kb"].sample)
                    per = 2 * (per + (2 * SEL_ROUNDS if p["select"] else 0))
                    slots(dve, p, lambda t, u: slot(p, t, u), chain, per)
                    if p["select"]:
                        select(p["select"], TOPK // 8 - 6 * SEL_ROUNDS)
                        mask(p["select"])
                    if p["index"]:
                        index_sums(p, p["index"])
                    slot(p, 3, 0)
                    slot(p, 3, 1)


def even_mixer(m):
    nc, ps, d = m.nc, m.ps, m.d
    with ExitStack() as outer:
        lat = m.sb("lat", [P, NKEYS], outer)
        kpe = m.sb("kpe", [P, NKEYS], outer)
        cq = m.sb("cq", [P, 2, N], outer)
        rope = m.sb("rope", [P, 2, N], outer)
        R = slice(64, 96)
        with ExitStack() as mid:
            qs = m.sb("qs", [P, 4, N], mid)
            ks = m.sb("ks", [P, SWA_COLS], mid)
            vs = m.sb("vs", [P, 10, P], mid)
            with ExitStack() as c:
                w = m.sb("we", [P, KT, EVEN_W], c)
                sq = m.sb("sqe", [P, 3, N], c)
                rs = m.sb("rse", [P, 2, N], c)
                rot = m.sb("rot", [P, N], c)
                names = ("we_loaded", "ec_loaded", "e_ready", "e_moved", "e_roped", "e_squared", "e_summed", "e_chain",
                         "e_inv", "e_root", "e_normed", "e_out", "e_kpe")
                S = {n: m.sem(n) for n in names}
                units = [("cq", 0, 0), ("cq", 1, 128), ("lat", 0, 256), ("ks", 0, 384)] + \
                        [("qs", t, 512 + P * t) for t in range(4)]
                flat = [(n, i, c0, t) for n, i, c0 in units for t in range(NTOK)]
                vbase = len(flat)
                rbase = vbase + 9
                with nc.Block() as block:
                    @block.sync
                    def _(sp):
                        for k in range(KT):
                            sp.dma_start(w[:, k], d["we"][:, k]).then_inc(S["we_loaded"], 16)
                        sp.wait_ge(S["e_kpe"], 1)
                        sp.wait_ge(S["e_normed"], 1)
                        sp.wait_ge(S["e_moved"], rbase)
                        outs = [(d["latT"][:, 0:TP], lat[:, 0:TP]), (d["latT"][:, TP:N], lat[:, TP + PAST:NKEYS]),
                                (d["kpeT"][:, 0:TP], kpe[R, 0:TP]), (d["kpeT"][:, TP:N], kpe[R, TP + PAST:NKEYS]),
                                (d["swakT"][:, 0:P], ks[:, TP - P:TP]),
                                (d["swakT"][:, P:2 * P], ks[:, TP + TS:SWA_COLS]),
                                (d["swav"][0], vs[:, 7]), (d["swav"][1, 0:P - TS], vs[TS:P, 8]),
                                (d["swav"][1, P - TS:P], vs[0:TS, 9])]
                        for to, src in outs:
                            sp.dma_start(to, src).then_inc(S["e_out"], 16)
                        sp.wait_ge(S["e_out"], 16 * len(outs))

                    @block.scalar
                    def _(act):
                        ins = [(lat[:, TP:TP + PAST], "c_lat"), (kpe[R, TP:TP + PAST], "c_kpe"),
                               (ks[:, TP:TP + P], "c_swak"), (vs[:, 8], "c_swav"), (rope[R], "rope")]
                        for tile, name in ins:
                            act.dma_start(tile, d[name]).then_inc(S["ec_loaded"], 16)
                        dest = {"cq": lambda i, t: [(cq[:, i, t * NT:(t + 1) * NT], 0, NT)],
                                "qs": lambda i, t: [(qs[:, i, t * NT:(t + 1) * NT], 0, NT)]}
                        for q, (name, i, _, t) in enumerate(flat):
                            act.wait_ge(S["e_ready"], q + 1)
                            bank = q % 8
                            if name in dest:
                                pieces = dest[name](i, t)
                            else:
                                tile, start = (lat, TP + PAST) if name == "lat" else (ks, TP + P)
                                pieces = [(tile[:, t * NT + c0:t * NT + c0 + cn] if s == 0 else tile[:, start:start + cn], c0, cn)
                                          for s, c0, cn in segments(t)]
                            for to, c0, cn in pieces:
                                ins = nc.scalar.activation(to, ps[:, bank, c0:c0 + cn], ACT.Copy,
                                                           scale=SWA_SCALE if name == "qs" else 1.0)
                            ins.then_inc(S["e_moved"], 1)
                        for i in range(9):
                            q = vbase + i
                            act.wait_ge(S["e_ready"], q + 1)
                            rows = P if i < 8 else TS
                            nc.scalar.activation(vs[0:rows, i if i < 8 else 9], ps[0:rows, q % 8, 0:P], ACT.Copy) \
                                .then_inc(S["e_moved"], 1)
                        act.wait_ge(S["e_moved"], vbase)
                        for i in range(2):
                            nc.scalar.activation(sq[:, i], cq[:, i], ACT.Square).then_inc(S["e_squared"], 1)
                        nc.scalar.activation(sq[:, 2, 0:TP], lat[:, 0:TP], ACT.Square)
                        nc.scalar.activation(sq[:, 2, TP:N], lat[:, TP + PAST:NKEYS], ACT.Square).then_inc(S["e_squared"], 1)
                        for i in range(2):
                            act.wait_ge(S["e_inv"], i + 1)
                            nc.scalar.activation(rs[:, i], rs[:, i], ACT.Sqrt).then_inc(S["e_root"], 1)

                    @block.tensor
                    def _(pe):
                        pe.wait_ge(S["we_loaded"], 16 * KT)
                        for q, (name, i, c0, t) in enumerate(flat):
                            if q >= 8:
                                pe.wait_ge(S["e_moved"], q - 7)
                            for k in range(KT):
                                mm = nc.tensor.matmul(ps[:, q % 8, 0:NT], w[:, k, c0:c0 + P],
                                                      m.hT[:, k, t * NT:(t + 1) * NT], start=k == 0, stop=k == KT - 1)
                            mm.then_inc(S["e_ready"], 1)
                        for i in range(9):
                            q = vbase + i
                            pe.wait_ge(S["e_moved"], q - 7)
                            rows = P if i < 8 else TS
                            for k in range(KT):
                                mm = nc.tensor.matmul(ps[0:rows, q % 8, 0:P], m.hT[:, k, i * P:i * P + rows],
                                                      w[:, k, 1024:1024 + P], start=k == 0, stop=k == KT - 1)
                            mm.then_inc(S["e_ready"], 1)
                        for j in range(2):
                            for t in range(NTOK):
                                q = rbase + j * NTOK + t
                                pe.wait_ge(S["e_moved"], q - 7)
                                for k in range(KT):
                                    mm = nc.tensor.matmul(ps[R, q % 8, 0:NT], w[:, k, 1152 + 32 * j:1184 + 32 * j],
                                                          m.hT[:, k, t * NT:(t + 1) * NT], start=k == 0, stop=k == KT - 1)
                                mm.then_inc(S["e_ready"], 1)
                        pe.wait_ge(S["e_moved"], rbase)
                        pe.wait_ge(S["e_roped"], 6)
                        pe.wait_ge(S["e_squared"], 3)
                        for t in range(NTOK):
                            for i in range(2):
                                nc.tensor.matmul(ps[:, t, 0:NT], m.ones[:], sq[:, i, t * NT:(t + 1) * NT],
                                                 start=i == 0, stop=i == 1)
                            mm = nc.tensor.matmul(ps[:, NTOK + t, 0:NT], m.ones[:], sq[:, 2, t * NT:(t + 1) * NT],
                                                  start=True, stop=True)
                        mm.then_inc(S["e_summed"], 1)

                    @block.vector
                    def _(dve):
                        chain = Chain(dve, S["e_chain"])
                        dve.wait_ge(S["ec_loaded"], 16 * 5)
                        for j in range(2):
                            for t in range(NTOK):
                                q = rbase + j * NTOK + t
                                dve.wait_ge(S["e_ready"], q + 1)
                                if j == 0:
                                    for s, c0, cn in segments(t):
                                        to = t * NT + c0 if s == 0 else TP + PAST
                                        src = slice(t * NT + c0, t * NT + c0 + cn)
                                        ins = nc.vector.tensor_tensor(kpe[R, to:to + cn], ps[R, q % 8, c0:c0 + cn],
                                                                      rope[R, 0, src], ALU.mult)
                                else:
                                    src = slice(t * NT, (t + 1) * NT)
                                    ins = nc.vector.tensor_tensor(rot[R, src], ps[R, q % 8, 0:NT], rope[R, 1, src], ALU.mult)
                                ins.then_inc(S["e_roped"], 1)
                        dve.wait_ge(S["e_roped"], 6)
                        nc.vector.tensor_tensor(kpe[R, 0:TP], kpe[R, 0:TP], rot[R, 0:TP], ALU.add)
                        new = kpe[R, TP + PAST:NKEYS]
                        nc.vector.tensor_tensor(new, new, rot[R, TP:N], ALU.add).then_inc(S["e_kpe"], 1)
                        dve.wait_ge(S["e_summed"], 1)
                        for i, factor in enumerate((D / 256, D / 128)):
                            for t in range(NTOK):
                                ins = nc.vector.tensor_scalar(rs[:, i, t * NT:(t + 1) * NT], ps[:, i * NTOK + t, 0:NT],
                                                              factor, RMS_EPS, ALU.mult, ALU.add)
                            chain.link(ins)
                            nc.vector.reciprocal(rs[:, i], rs[:, i]).then_inc(S["e_inv"], 1)
                        chain.link(nc.vector.tensor_scalar(m.gq[:, 0:2], m.gq[:, 0:2], MLA_SCALE, None, ALU.mult))
                        dve.wait_ge(S["e_root"], 2)
                        for i in range(2):
                            nc.vector.scalar_tensor_tensor(cq[:, i], cq[:, i], m.gq[:, i:i + 1], rs[:, 0], ALU.mult, ALU.mult)
                        for a, b, r0 in ((0, TP, 0), (TP + PAST, NKEYS, TP)):
                            ins = nc.vector.scalar_tensor_tensor(lat[:, a:b], lat[:, a:b], m.gq[:, 2:3],
                                                                 rs[:, 1, r0:r0 + b - a], ALU.mult, ALU.mult)
                        ins.then_inc(S["e_normed"], 1)

            with ExitStack() as c:
                btile = m.sb("bswa", [P, HEADS, 256], c)
                bl = m.sem("bswa_loaded")
                with nc.Block() as block:
                    @block.sync
                    def _(sp):
                        src = toeplitz(m, TP - P, 256)
                        sp.dma_start(btile[:], src).then_inc(bl, 16)
                        sp.wait_ge(bl, 16)
                blocks = [Keys(b * P, P, [(c0 * P, P, c0) for c0 in range(max(0, b - 1), b + 1)]) for b in range(8)]
                blocks.append(Keys(TP, TS, [(TP, P, 8), (TP + P, TS, 9)], sample=True))

                def rows(u):
                    return slice(64 * u, 64 * u + 64)

                def q_of(t, u, kb):
                    return row(qs[rows(u)], t)[:, kb.q0:kb.q0 + kb.nq]

                def bias_of(h, kb):
                    j0 = 0 if kb.sample or kb.nk == 256 else P
                    return row(btile[0:kb.nq], h)[:, j0:j0 + kb.nk]
                attention_stage(m, "swa", blocks, "swa", q_of,
                                lambda t, u, kb, n0, n1: ks[rows(u), kb.tiles[0][0] + n0:kb.tiles[0][0] + n1],
                                lambda t, u, v, size: vs[0:size, v, 64 * u:64 * u + 64],
                                64, rows, 4, bias_w=256, bias_of=bias_of, sink=True)

        with ExitStack() as c:
            q = m.sb("qmla", [96, HEADS, N], c)
            kT = m.sb("kmla", [96, HEADS, N], c)
            v = m.sb("vmla", [P, 9, 512], c)
            for part in range(2):
                with ExitStack() as cc:
                    rot = m.sb(f"rotq{part}", [P, 2, NT], cc)
                    wq = m.sb("wuq", [P, 2, HEADS, P], cc) if part == 0 else None
                    wkv = m.sb(f"wukv{part}", [P, 2, 512], cc)
                    mla_up(m, part, q, kT, v, wq, wkv, cq, lat, kpe, rope, rot, R)
                nk0 = 0 if part == 0 else TP
                if part == 0:
                    blocks = [Keys(b * P, P, [(i * P, P, i) for i in range(b + 1)]) for b in range(8)]
                else:
                    blocks = [Keys(TP, TS, [(i * P, P, i) for i in range(8)] + [(TP, TS, 8)], sample=True, wide=True)]
                attention_stage(m, f"mla{part}", blocks, "mla",
                                lambda t, u, kb: row(q[:], t + 4 * u)[:, kb.q0:kb.q0 + kb.nq],
                                lambda t, u, kb, n0, n1: row(kT[:], t + 4 * u)[:, n0:n1],
                                lambda t, u, i, size: v[0:size, i, bass.ds((t + 4 * u) * 64, 64)],
                                64, lambda u: slice(0, 96), 0, osb=cq)
    with ExitStack() as c:
        down_stage(m, "e", d["woe"], m.hT, KT, 0, 0, c)


def mla_up(m, part, q, kT, v, wq, wkv, cq, lat, kpe, rope, rot, R):
    nc, ps, d = m.nc, m.ps, m.d
    names = ("w_loaded", "q_ready", "q_moved", "q_rot", "chain", "k_ready", "k_moved")
    S = {n: m.sem(f"up{part}_{n}") for n in names}
    l0, nk = (0, TP) if part == 0 else (TP, N)
    chunks = [(a, min(nk, a + 512)) for a in range(0, nk, 512)]
    vt = 8 if part == 0 else 9
    nunits = HEADS * NTOK if part == 0 else 0
    kunits = HEADS * len(chunks)
    with nc.Block() as block:
        @block.sync
        def _(sp):
            sp.dma_start(wkv[:], d["wukv"]).then_inc(S["w_loaded"], 16)
            if part == 0:
                sp.dma_start(wq[:], d["wuq"]).then_inc(S["w_loaded"], 16)

        @block.tensor
        def _(pe):
            pe.wait_ge(S["w_loaded"], 32 if part == 0 else 16)
            for n in range(nunits):
                h, t = divmod(n, NTOK)
                cols = slice(t * NT, (t + 1) * NT)
                if n >= 2:
                    pe.wait_ge(S["q_moved"], n - 1)
                    pe.wait_ge(S["q_rot"], n - 1)
                for j, (r, w0, w1) in enumerate(((slice(0, 96), 0, 96), (R, 96, 128))):
                    for k in range(2):
                        mm = nc.tensor.matmul(ps[r, 2 * (n % 2) + j, 0:NT], wq[:, k, h, w0:w1], cq[:, k, cols],
                                              start=k == 0, stop=k == 1)
                mm.then_inc(S["q_ready"], 1)
            for n in range(kunits + vt):
                if n >= 4:
                    pe.wait_ge(S["k_moved"], n - 3)
                bank = 4 + n % 4
                if n < kunits:
                    h, ci = divmod(n, len(chunks))
                    a, b = chunks[ci]
                    mm = nc.tensor.matmul(ps[0:64, bank, 0:b - a], wkv[:, 0, 64 * h:64 * h + 64],
                                          lat[:, l0 + a:l0 + b], start=True, stop=True)
                else:
                    i = n - kunits
                    rows = min(P, nk - i * P)
                    mm = nc.tensor.matmul(ps[0:rows, bank, :], lat[:, l0 + i * P:l0 + i * P + rows], wkv[:, 1],
                                          start=True, stop=True)
                mm.then_inc(S["k_ready"], 1)

        @block.scalar
        def _(act):
            for n in range(nunits):
                h, t = divmod(n, NTOK)
                act.wait_ge(S["q_ready"], n + 1)
                act.wait_ge(S["q_rot"], n + 1)
                nc.scalar.activation(q[0:64, h, t * NT:(t + 1) * NT], ps[0:64, 2 * (n % 2), 0:NT], ACT.Copy) \
                    .then_inc(S["q_moved"], 1)
            for n in range(kunits + vt):
                act.wait_ge(S["k_ready"], n + 1)
                bank = 4 + n % 4
                if n < kunits:
                    h, ci = divmod(n, len(chunks))
                    a, b = chunks[ci]
                    ins = nc.scalar.activation(kT[0:64, h, a:b], ps[0:64, bank, 0:b - a], ACT.Copy)
                else:
                    i = n - kunits
                    rows = min(P, nk - i * P)
                    ins = nc.scalar.activation(v[0:rows, i], ps[0:rows, bank, :], ACT.Copy)
                ins.then_inc(S["k_moved"], 1)

        @block.gpsimd
        def _(pool):
            nc.gpsimd.tensor_copy(kT[R, :, 0:nk], spread(kpe[R, l0:l0 + nk], HEADS))

        @block.vector
        def _(dve):
            chain = Chain(dve, S["chain"])
            for n in range(nunits):
                h, t = divmod(n, NTOK)
                cols = slice(t * NT, (t + 1) * NT)
                dve.wait_ge(S["q_ready"], n + 1)
                nc.vector.tensor_tensor(rot[R, 0], ps[R, 2 * (n % 2), 0:NT], rope[R, 0, cols], ALU.mult)
                chain.link(nc.vector.tensor_tensor(rot[R, 1], ps[R, 2 * (n % 2) + 1, 0:NT], rope[R, 1, cols], ALU.mult))
                nc.vector.tensor_tensor(q[R, h, cols], rot[R, 0], rot[R, 1], ALU.add).then_inc(S["q_rot"], 1)
                dve.wait_ge(S["q_rot"], n + 1)


def odd_mixer(m):
    nc, ps, d = m.nc, m.ps, m.d
    with ExitStack() as outer:
        qd = m.sb("qd", [P, HEADS, N], outer)
        kd = m.sb("kd", [P, 2, NKEYS], outer)
        ki = m.sb("ki", [P, NKEYS], outer)
        qi = m.sb("qi", [P, 4, N], outer)
        v = m.sb("vd", [P, 17, 256], outer)
        wi = m.sb("wi", [P, 9, HEADS], outer)
        with ExitStack() as c:
            w = m.sb("wo", [P, 3, KT, P], c)
            wv = m.sb("wov", [P, KT, VW], c)
            names = ("ready", "moved", "v_loaded", "c_loaded", "out", "v_ready", "v_moved", "w_chain")
            S = {n: m.sem("o_" + n) for n in names}
            wl = [m.sem(f"wo_loaded{u}") for u in range(3)]
            with nc.Block() as block:
                @block.sync
                def _(sp):
                    for j in range(ODD_TILES):
                        if j >= 3:
                            sp.wait_ge(S["ready"], 3 * (j - 2))
                        sp.dma_start(w[:, j % 3], d["wo"][j]).then_inc(wl[j % 3], 16)
                        if j == 2:
                            sp.dma_start(wv[:], d["wov"]).then_inc(S["v_loaded"], 16)
                    sp.wait_ge(S["moved"], 3 * ODD_TILES)
                    sp.wait_ge(S["v_moved"], 18)
                    outs = [(d["dsakT"][:, :, 0:TP], kd[:, :, 0:TP]), (d["dsakT"][:, :, TP:N], kd[:, :, TP + PAST:NKEYS]),
                            (d["idxT"][:, 0:TP], ki[0:64, 0:TP]), (d["idxT"][:, TP:N], ki[0:64, TP + PAST:NKEYS]),
                            (d["dsav"][:, 0:8], v[:, 0:8]), (d["dsav"][0:TS, 8], v[0:TS, 16])]
                    for to, src in outs:
                        sp.dma_start(to, src).then_inc(S["out"], 16)
                    sp.wait_ge(S["out"], 16 * len(outs))

                @block.tensor
                def _(pe):
                    for j in range(ODD_TILES):
                        pe.wait_ge(wl[j % 3], 16 * (j // 3 + 1))
                        for t in range(NTOK):
                            n = NTOK * j + t
                            if n >= 6:
                                pe.wait_ge(S["moved"], n - 5)
                            for k in range(KT):
                                mm = nc.tensor.matmul(ps[:, n % 6, 0:NT], w[:, j % 3, k], m.hT[:, k, t * NT:(t + 1) * NT],
                                                      start=k == 0, stop=k == KT - 1)
                            mm.then_inc(S["ready"], 1)
                    pe.wait_ge(S["v_loaded"], 16)
                    for i in range(9):
                        if i >= 2:
                            pe.wait_ge(S["v_moved"], 2 * (i - 1))
                        rows = P if i < 8 else TS
                        for k in range(KT):
                            mm = nc.tensor.matmul(ps[0:rows, 6 + i % 2, 0:VW], m.hT[:, k, i * P:i * P + rows], wv[:, k],
                                                  start=k == 0, stop=k == KT - 1)
                        mm.then_inc(S["v_ready"], 1)

                @block.scalar
                def _(act):
                    for to, name in ((kd[:, :, TP:TP + PAST], "c_dsak"), (v[:, 8:16], "c_dsav"),
                                     (ki[0:64, TP:TP + PAST], "c_idx"), (ki[64:P, TP:TP + PAST], "c_idx")):
                        act.dma_start(to, d[name]).then_inc(S["c_loaded"], 16)
                    for j in range(ODD_TILES):
                        for t in range(NTOK):
                            n = NTOK * j + t
                            act.wait_ge(S["ready"], n + 1)
                            cols = slice(t * NT, (t + 1) * NT)
                            if j < 8 or j > 10:
                                to = qd[:, j, cols] if j < 8 else qi[:, j - 11, cols]
                                pieces = [(to, 0, NT)]
                            else:
                                tile = kd[:, j - 8] if j < 10 else ki[:]
                                pieces = [(tile[:, t * NT + c0:t * NT + c0 + cn] if s == 0 else tile[:, TP + PAST:NKEYS], c0, cn)
                                          for s, c0, cn in segments(t)]
                            for to, c0, cn in pieces:
                                ins = nc.scalar.activation(to, ps[:, n % 6, c0:c0 + cn], ACT.Copy,
                                                           scale=DSA_SCALE if j < 8 else 1.0)
                            ins.then_inc(S["moved"], 1)
                    for i in range(9):
                        rows = P if i < 8 else TS
                        act.wait_ge(S["v_ready"], i + 1)
                        nc.scalar.activation(v[0:rows, i if i < 8 else 16], ps[0:rows, 6 + i % 2, 0:256], ACT.Copy) \
                            .then_inc(S["v_moved"], 1)
                        nc.scalar.activation(wi[0:rows, i], ps[0:rows, 6 + i % 2, 256:VW], ACT.Copy, scale=IDX_W_SCALE) \
                            .then_inc(S["v_moved"], 1)
                    act.wait_ge(S["c_loaded"], 64)

        btile = m.hT
        prompt = [Keys(b * P, P, [(i * P, P, i) for i in range(b + 1)]) for b in range(8)]
        sample = Keys(TP, TS, [(TP + i * P, P, 8 + i) for i in range(8)] + [(TP + PAST, TS, 16)],
                      sample=True, wide=True)
        scores = [m.sb(f"score{i}", [P, N], outer) for i in range(2)]
        sels, units = {}, 0
        for b, kb in enumerate(prompt + [sample]):
            if kb.nk > TOPK:
                sels[b] = Selection(len(sels), kb, scores, units)
                units += 8 * len(sels[b].chunks)
        for part in range(2):
            bl = m.sem(f"bdsa_loaded{part}")
            width, j0 = (TP, P) if part == 0 else (N, 0)
            with nc.Block() as block:
                @block.sync
                def _(sp):
                    src = toeplitz(m, j0, width)
                    sp.dma_start(btile[:, :, 0:width], src).then_inc(bl, 16)
                    sp.wait_ge(bl, 16)
            attention_stage(m, f"dsa{part}", prompt if part == 0 else [sample], "dsa",
                            lambda t, u, kb: row(qd[:], t + 4 * u)[:, kb.q0:kb.q0 + kb.nq],
                            lambda t, u, kb, n0, n1: kd[:, u, kb.tiles[0][0] + n0:kb.tiles[0][0] + n1],
                            lambda t, u, i, size: v[0:size, i, P * u:P * u + P],
                            P, lambda u: slice(0, P), 0, bias_w=TP if part == 0 else N,
                            bias_of=lambda h, kb: row(btile[0:kb.nq], h)[:, (0 if kb.sample else 7 * P - kb.q0):][:, 0:kb.nk],
                            index=dict(q=qi, k=ki, w=wi) if part == 0 else None,
                            sels=sels if part == 0 else {0: sels[8]}, out=qd)
        down_stage(m, "o", d["woo"], qd, KT, 1, 0, outer)


def ffn_with_norms(m, layer):
    with ExitStack() as c:
        hh = m.sb(f"hh{layer}", [P, KT, N], c, F32R)
        hl = m.sb(f"hl{layer}", [P, KT, N], c, F32R)
        with ExitStack() as scratch:
            m.hT = m.sb(f"h_ffn{layer}", [P, KT, N], scratch)
            norm_stage(m, layer, 0, split=(hh, hl))
        m.recycle()
        ffn_stage(m, layer, hh, hl, c)


def build_program(nc, dram):
    with ExitStack() as ctx:
        m = Machine(nc, ctx, dram)
        with ExitStack() as c:
            m.hT = m.sb("h_even", [P, KT, N], c)
            start_stage(m)
            even_mixer(m)
        ffn_with_norms(m, 0)
        with ExitStack() as c:
            m.hT = m.sb("h_odd", [P, KT, N], c)
            norm_stage(m, 0, 1)
            m.recycle()
            odd_mixer(m)
        ffn_with_norms(m, 1)
        with ExitStack() as c:
            m.hT = m.sb("squares", [P, KT, N], c)
            norm_stage(m, 1, 1, final=True)
        stored = m.sem("conv_stored")
        with nc.Block() as block:
            @block.sync
            def _(sp):
                sp.dma_start(dram["convo"], m.convo[:]).then_inc(stored, 16)
                sp.wait_ge(stored, 16)


def shape_constants():
    pos = np.arange(N, dtype=np.float32)
    half = np.arange(16, dtype=np.float32)
    inv = np.power(np.float64(10000.0), -(half / np.float32(16)).astype(np.float64)).astype(np.float32)
    ang = (pos[None, :] * inv[:, None]).astype(np.float32).astype(np.float64)
    cos, sin = np.cos(ang).astype(np.float32), np.sin(ang).astype(np.float32)
    rope = np.stack([np.concatenate([cos, cos]), np.concatenate([-sin, sin])], axis=1)
    rel = np.arange(REL_LEN) - REL_BASE
    n = np.abs(rel)
    large = 8 + (np.log(np.maximum(n, 1).astype(np.float32) / np.float32(8)) / np.float32(np.log(128.0))
                 * np.float32(8)).astype(np.int32)
    bucket = np.where(rel > 0, 16, 0) + np.where(n < 8, n, np.minimum(large, 15))
    onehot = (np.arange(32)[:, None] == bucket[None, :]).astype(np.float32)
    return dict(rope=rope, onehot=onehot, ident=np.eye(P, dtype=np.float32),
                ones=np.full((P, P), 1.0 / D, np.float32))


def tiles_of(w, columns):
    w = w[:, columns]
    rows, cols = w.shape
    return np.ascontiguousarray(w.reshape(rows // P, P, cols // P, P).transpose(2, 1, 0, 3))


def by_partition(a):
    return np.moveaxis(a.reshape(a.shape[:-1] + (-1, P)), -1, 0)


def kernel(**inputs):
    import concourse.bacc as bacc
    from concourse.bass_utils import run_bass_kernel_spmd

    i = {k: np.asarray(v) for k, v in inputs.items()}
    a = dict(shape_constants())
    a["xT"] = np.concatenate([i["x_prompt"][0], i["x_sample"][0]]).T.reshape(KT, P, N).transpose(1, 0, 2)
    a["cT"] = np.stack([i["c_prompt"][0], i["c_sample"][0]]).T.reshape(KT, P, 2).transpose(1, 0, 2)
    wada = i["w_ada"].reshape(2, KT, P, 12, 512)
    a["wada"] = wada.transpose(0, 3, 2, 1, 4).reshape(24, P, KT, 512)
    a["bada"] = np.repeat(by_partition(i["b_ada"]).reshape(P, 96, 1), 2, axis=2)
    a["lnp"] = np.stack([by_partition(i[n]) for n in ("ln_mix_g", "ln_mix_b", "ln_ffn_g", "ln_ffn_b")], axis=2)
    a["rel_bias"] = i["rel_bias"]
    a["sinks"] = np.broadcast_to(i["swa_sinks"][0], (P, HEADS))
    a["gq"] = np.concatenate([i["g_q_lora"][0].reshape(2, P), i["g_kv_lora"][0].reshape(1, P)]).T

    kr = np.arange(384, 416)
    qs = 416 + np.concatenate([np.r_[t * 64:t * 64 + 64, (t + 4) * 64:(t + 4) * 64 + 64] for t in range(4)])
    cols = np.concatenate([np.arange(384), np.arange(928, 1056), qs, np.arange(1056, 1184), kr, np.roll(kr, 16)])
    a["we"] = i["w_in_even"][0][:, cols].reshape(KT, P, EVEN_W).transpose(1, 0, 2)
    uq = i["w_uq"][0].reshape(2, P, HEADS, 96)
    a["wuq"] = np.concatenate([uq, np.roll(uq[..., 64:], 16, axis=-1)], axis=-1).transpose(1, 0, 2, 3)
    ukv = i["w_ukv"][0].reshape(P, HEADS, 2, 64)
    a["wukv"] = ukv.transpose(0, 2, 1, 3).reshape(P, 2, 512)
    a["woe"] = tiles_of(i["w_out_even"][0], slice(None))

    cols = np.concatenate([np.arange(1280), np.arange(2048, 2112), np.arange(2048, 2112), np.arange(1536, 2048)])
    a["wo"] = tiles_of(i["w_in_odd"][0], cols)
    a["wov"] = i["w_in_odd"][0][:, np.r_[1280:1536, 2112:2120]].reshape(KT, P, VW).transpose(1, 0, 2)
    a["woo"] = tiles_of(i["w_out_odd"][0], slice(None))

    wfi = np.stack([tiles_of(i["ffn_w_in"][l], slice(None)) for l in range(2)])
    a["wfi"] = wfi.reshape(2, 2, FT, P, KT, P).transpose(0, 2, 3, 1, 4, 5)
    a["wfo"] = np.stack([tiles_of(i["ffn_w_out"][l], slice(None)) for l in range(2)])
    taps = np.concatenate([i["ffn_conv_w"], i["ffn_conv_b"][:, None]], axis=1)
    a["convp"] = taps.reshape(2, 4, 2, FT, P).transpose(4, 0, 3, 2, 1).reshape(P, 2, FT, 8)
    state = i["state_ffn_conv"][:, 0]
    a["convs"] = state.reshape(2, 2, 2, FT, P).transpose(4, 0, 3, 2, 1).reshape(P, 2, FT, 4)

    a["c_lat"] = i["cache_mla_latent"][0, 0].T
    a["c_kpe"] = i["cache_mla_kpe"][0, 0].T
    a["c_swak"] = i["cache_swa_k"][0, 0].reshape(P, P).T
    a["c_swav"] = i["cache_swa_v"][0, 0].reshape(P, P)
    a["c_dsak"] = i["cache_dsa_k"][0, 0].transpose(2, 1, 0)
    a["c_dsav"] = i["cache_dsa_v"][0, 0].reshape(8, P, 256).transpose(1, 0, 2)
    a["c_idx"] = i["cache_dsa_idx_k"][0, 0].T
    a = {k: np.ascontiguousarray(v) for k, v in a.items()}

    outs = dict(yT=(P, KT, N), latT=(P, N), kpeT=(32, N), swakT=(P, 2 * P), swav=(2, P, P), dsakT=(P, 2, N),
                dsav=(P, 9, 256), idxT=(64, N), convo=(P, 2, FT, 8))
    nc = bacc.Bacc("TRN2", target_bir_lowering=False, num_devices=1)
    dram = {k: nc.dram_tensor(f"in_{k}", v.shape, F32, kind="ExternalInput").ap() for k, v in a.items()}
    for k, shape in outs.items():
        dram[k] = nc.dram_tensor(f"out_{k}", shape, F32, kind="ExternalOutput").ap()
    build_program(nc, dram)
    r = run_bass_kernel_spmd(nc, [{f"in_{k}": v for k, v in a.items()}], core_ids=[0]).results[0]
    o = {k: np.asarray(r[f"out_{k}"]) for k in outs}

    y = o["yT"].transpose(2, 1, 0).reshape(N, D)
    lat, kpe = o["latT"].T, o["kpeT"].T
    swak = o["swakT"].T.reshape(2, 1, 1, P, 2, 64)
    swav = o["swav"].reshape(2, 1, 1, P, 2, 64)
    dk = o["dsakT"].transpose(2, 1, 0)
    dv = o["dsav"].transpose(1, 0, 2).reshape(9 * P, 2, P)[:N]
    di = o["idxT"].T
    cv = o["convo"].reshape(P, 2, FT, 2, 2, 2).transpose(3, 1, 5, 4, 2, 0).reshape(2, 2, 1, 2, 2 * FF)
    both = [slice(0, TP), slice(TP, N)]
    group = [[lat[s][None, None], kpe[s][None, None], swak[n], swav[n], dk[s][None, None], dv[s][None, None],
              di[s][None, None], cv[n]] for n, s in enumerate(both)]
    return tuple(np.ascontiguousarray(x) for x in [y[both[0]][None], y[both[1]][None], *group[0], *group[1]])
```

```python
from contextlib import ExitStack, contextmanager

import numpy as np

import concourse.bass as bass
from concourse import mybir

F32 = mybir.dt.float32
F32R = mybir.dt.float32r
ALU = mybir.AluOpType
ACT = mybir.ActivationFunctionType
AX = mybir.AxisListType

P = 128
D = 1024
KT = D // P
TP, TS = 1024, 32
N = TP + TS
NTOK = 3
NT = N // NTOK
PAST = 1024
CHUNK = 64
NEG = -1e30
TAKEN = -3e38
LN_EPS, RMS_EPS = 1e-5, 1e-6
ALPHA = float(np.float32(4.0 ** 0.25))
FF = 2816
FT = FF // P
HEADS = 8
MLA_SCALE = 96 ** -0.5
SWA_SCALE = 64 ** -0.5
DSA_SCALE = 128 ** -0.5
IDX_W_SCALE = (8 * 64) ** -0.5
TOPK = 256
NKEYS = TP + PAST + TS
SWA_COLS = TP + P + TS
REL_LEN = 1281
REL_BASE = 1151
EVEN_W = 1216
ODD_TILES = 15
VW = 256 + 8
SEQS = ((0, TP), (TP, N))


class Chain:

    def __init__(self, eng, sem):
        self.eng, self.sem, self.n, self.extra = eng, sem, 0, 0

    def link(self, ins, standing=None):
        self.issue(ins)
        self.wait(standing)

    def issue(self, ins):
        ins.then_inc(self.sem, 1)
        self.n += 1

    def wait(self, standing=None):
        self.eng.wait_ge(self.sem, self.extra + self.n)
        if standing:
            self.eng.sem_inc(standing, 1)

    @contextmanager
    def loop(self, rounds, per, first=0):
        with self.eng.Fori(first, rounds) as i:
            start = self.n
            self.extra = (i - first) * per if first else i * per
            yield i
            assert self.n == start + per, (self.n - start, per)
            self.extra = 0
        self.n = start + per * (rounds - first)


class Machine:

    def __init__(self, nc, ctx, dram):
        self.nc, self.ctx, self.d, self.held = nc, ctx, dram, []
        sb = self.sb
        self.xT = sb("xT", [P, KT, N])
        self.hT = None
        self.mods = sb("mods", [P, 96, 2])
        self.lnp = sb("lnp", [P, 2, 4, KT])
        self.ones = sb("ones", [P, P])
        self.ident = sb("ident", [P, P])
        self.convp = sb("convp", [P, 2, FT, 8])
        self.convs = sb("convs", [P, 2, FT, 4])
        self.convo = sb("convo", [P, 2, FT, 8])
        self.sinks = sb("sinks", [P, HEADS])
        self.gq = sb("gq", [P, 3])
        self.negs = sb("negs", [P, 1])
        self.ps = ctx.enter_context(nc.psum_tensor("ps", [P, 8, 512], F32))
        self.biasd = nc.dram_tensor("rel_scratch", [HEADS, P, REL_LEN], F32, kind="Internal").ap()

    def sb(self, name, shape, ctx=None, dtype=F32):
        return (ctx or self.ctx).enter_context(self.nc.sbuf_tensor("t_" + name, shape, dtype))

    def sem(self, name):
        self.held.append(self.nc.alloc_semaphore(name=name))
        return self.held[-1]

    def recycle(self):
        self.nc.clear_and_free_semaphores(self.held)
        self.nc.all_engine_barrier()
        self.held = []


def spread(ap, k):
    return ap.unsqueeze(1).broadcast_to([ap.shape[0], k, ap.shape[1]])


def segments(t):
    out = []
    for s, (a, b) in enumerate(SEQS):
        lo, hi = max(a, t * NT), min(b, (t + 1) * NT)
        if lo < hi:
            out.append((s, lo - t * NT, hi - lo))
    return out


def toeplitz(m, j0, width, rows=P):
    return bass.AP(m.biasd.tensor, REL_BASE - TP + j0,
                   [[REL_LEN - 1, rows], [P * REL_LEN, HEADS], [1, width]])


def down_stage(m, tag, wd, rhs, layer, part, ctx):
    nc, ps = m.nc, m.ps
    raw = m.sb("wdraw" + tag, [P, 2, KT, P], ctx)
    wh = m.sb("wdh" + tag, [P, 2, KT, P], ctx, F32R)
    wlo = m.sb("wdl" + tag, [P, 2, KT, P], ctx, F32R)
    xh = m.sb("dh" + tag, [P, KT, N], ctx, F32R)
    xl = m.sb("dl" + tag, [P, KT, N], ctx, F32R)
    loaded = [m.sem(f"wd{tag}_loaded{u}") for u in range(2)]
    names = ("w_hi", "w_lo", "x_hi", "x_lo", "ready", "added", "scaled", "turns")
    S = {n: m.sem(f"down{tag}_{n}") for n in names}
    gate = 48 * layer + 24 * part + 16
    BANKS = 2 * NTOK
    ROUNDS = KT // 2
    with nc.Block() as block:
        @block.sync
        def _(sp):
            for u in range(2):
                sp.dma_start(raw[:, u], wd[u]).then_inc(loaded[u], 16)
            with sp.Fori(1, ROUNDS) as i:
                for u in range(2):
                    sp.wait_ge(S["w_lo"], i * 2 + (u - 1))
                    sp.dma_start(raw[:, u], wd[bass.ds(i * 2 + u, 1)]
                                 .rearrange("a p k m -> (a p) k m")).then_inc(loaded[u], 16)

        @block.gpsimd
        def _(pool):
            def high(i, u):
                pool.wait_ge(loaded[u], i * 16 + 16)
                if not isinstance(i, int):
                    pool.wait_ge(S["ready"], i * BANKS + (u - 1) * NTOK)
                    pool.sem_inc(S["turns"], 1)
                nc.gpsimd.tensor_copy(wh[:, u], raw[:, u]).then_inc(S["w_hi"], 1)
            for u in range(2):
                high(0, u)
            with pool.Fori(1, ROUNDS) as i:
                for u in range(2):
                    high(i, u)

        @block.scalar
        def _(act):
            for k in range(KT):
                nc.scalar.activation(xh[:, k], rhs[:, k], ACT.Copy).then_inc(S["x_hi"], 1)
            for k in range(KT):
                nc.scalar.activation(m.xT[:, k], m.xT[:, k], ACT.Copy, scale=ALPHA).then_inc(S["scaled"], 1)

        @block.tensor
        def _(pe):
            def tiles(i, first):
                for u in range(2):
                    pe.wait_ge(S["w_lo"], i * 2 + (u + 1))
                    for t in range(NTOK):
                        bank, n = u * NTOK + t, 0
                        if not first:
                            pe.wait_ge(S["added"], i * BANKS + (bank - BANKS + 1))
                        for k in range(KT):
                            if first and u == t == 0:
                                pe.wait_ge(S["x_lo"], k + 1)
                            for w, x in ((wh, xh), (wh, xl), (wlo, xh)):
                                mm = nc.tensor.matmul(ps[:, bank, 0:NT], w[:, u, k], x[:, k, t * NT:(t + 1) * NT],
                                                      start=n == 0, stop=n == 3 * KT - 1)
                                n += 1
                        mm.then_inc(S["ready"], 1)
            tiles(0, True)
            with pe.Fori(1, ROUNDS) as i:
                tiles(i, False)

        @block.vector
        def _(dve):
            def low(i, u):
                dve.wait_ge(S["w_hi"], i * 2 + (u + 1))
                nc.vector.tensor_tensor(wlo[:, u], raw[:, u], wh[:, u].bitcast(F32), ALU.subtract).then_inc(S["w_lo"], 1)

            def tiles(i, last):
                for u in range(2):
                    for t in range(NTOK):
                        bank = u * NTOK + t
                        dve.wait_ge(S["ready"], i * BANKS + (bank + 1))
                        for s, c0, cn in segments(t):
                            x = m.xT[:, bass.ds(i * 2 + u, 1), t * NT + c0:t * NT + c0 + cn] \
                                .rearrange("p a n -> p (a n)")
                            g = m.mods[:, bass.ds(i * 2 + (gate + u), 1), s:s + 1].rearrange("p a n -> p (a n)")
                            ins = nc.vector.scalar_tensor_tensor(x, ps[:, bank, c0:c0 + cn], g, x, ALU.mult, ALU.add)
                        ins.then_inc(S["added"], 1)
                    if not last:
                        low(i + 1, u)
            for k in range(KT):
                if k in (1, 4):
                    low(0, k // 4)
                dve.wait_ge(S["x_hi"], k + 1)
                nc.vector.tensor_tensor(xl[:, k], rhs[:, k], xh[:, k].bitcast(F32), ALU.subtract).then_inc(S["x_lo"], 1)
            dve.wait_ge(S["scaled"], KT)
            with dve.Fori(0, ROUNDS - 1) as i:
                tiles(i, False)
            tiles(ROUNDS - 1, True)


def norm_stage(m, layer, part, split=None, final=False, ahead=()):
    nc, ps = m.nc, m.ps
    tag = f"{layer}{part}"
    names = ("centred", "squared", "summed", "mean", "inv", "root", "chain", "scaled", "shifted", "h_act", "h_dve",
             "hi", "stored")
    S = {n: m.sem(f"ln{tag}_{n}") for n in names}
    base = 48 * (layer + part) + 24 * (1 - part)
    SHARE = 4
    with ExitStack() as c:
        rs = m.sb("rs" + tag, [P, N], c)
        cols = [slice(t * NT, (t + 1) * NT) for t in range(NTOK)]
        with nc.Block() as block:
            @block.tensor
            def _(pe):
                for t in range(NTOK):
                    for k in range(KT):
                        mm = nc.tensor.matmul(ps[:, t, 0:NT], m.ones[:], m.xT[:, k, cols[t]],
                                              start=k == 0, stop=k == KT - 1)
                    mm.then_inc(S["mean"], 1)
                for t in range(NTOK):
                    pe.wait_ge(S["squared"], t + 1)
                    for k in range(KT):
                        mm = nc.tensor.matmul(ps[:, NTOK + t, 0:NT], m.ones[:], m.hT[:, k, cols[t]],
                                              start=k == 0, stop=k == KT - 1)
                    mm.then_inc(S["summed"], 1)

            @block.scalar
            def _(act):
                for t in range(NTOK):
                    act.wait_ge(S["centred"], t + 1)
                    nc.scalar.activation(m.hT[:, :, cols[t]], m.xT[:, :, cols[t]], ACT.Square).then_inc(S["squared"], 1)

                def root(t):
                    act.wait_ge(S["inv"], t + 1)
                    nc.scalar.activation(rs[:, cols[t]], rs[:, cols[t]], ACT.Sqrt).then_inc(S["root"], 1)
                root(0)
                for t in range(NTOK):
                    for k in range(KT):
                        act.wait_ge(S["scaled"], t * KT + k + 1)
                        nc.scalar.activation(m.xT[:, k, cols[t]], m.xT[:, k, cols[t]], ACT.Identity,
                                             bias=m.lnp[:, layer, 2 * part + 1, k:k + 1]).then_inc(S["shifted"], 1)
                    if t + 1 < NTOK:
                        root(t + 1)
                    if final:
                        continue
                    act.wait_ge(S["shifted"], t * KT + SHARE)
                    for k in range(SHARE):
                        for s, c0, cn in segments(t):
                            at = slice(t * NT + c0, t * NT + c0 + cn)
                            ins = nc.scalar.activation(m.hT[:, k, at], m.xT[:, k, at], ACT.Identity,
                                                       bias=m.mods[:, base + k, s:s + 1],
                                                       scale=m.mods[:, base + 8 + k, s:s + 1])
                    ins.then_inc(S["h_act"], 1)
                    if split:
                        act.wait_ge(S["h_act"], t + 1)
                        act.wait_ge(S["h_dve"], t + 1)
                        nc.scalar.activation(split[0][:, :, cols[t]], m.hT[:, :, cols[t]], ACT.Copy).then_inc(S["hi"], 1)

            def low(eng, t):
                eng.wait_ge(S["hi"], t + 1)
                eng.tensor_tensor(split[1][:, :, cols[t]], m.hT[:, :, cols[t]], split[0][:, :, cols[t]].bitcast(F32),
                                  ALU.subtract)

            if split:
                @block.gpsimd
                def _(pool):
                    for tile, _, loaded, high, split_done in ahead:
                        if high is not None:
                            pool.wait_ge(loaded, 16)
                            nc.gpsimd.tensor_copy(high, tile).then_inc(split_done, 1)
                    for t in range(NTOK - 1):
                        low(pool, t)

            if ahead:
                @block.sync
                def _(sp):
                    for tile, source, loaded, _, _ in ahead:
                        sp.dma_start(tile, source).then_inc(loaded, 16)

            @block.vector
            def _(dve):
                chain = Chain(dve, S["chain"])
                for t in range(NTOK):
                    dve.wait_ge(S["mean"], t + 1)
                    x = m.xT[:, :, cols[t]]
                    nc.vector.tensor_tensor(x, x, spread(ps[:, t, 0:NT], KT), ALU.subtract).then_inc(S["centred"], 1)

                def inverse(t):
                    dve.wait_ge(S["summed"], t + 1)
                    chain.link(nc.vector.tensor_scalar(rs[:, cols[t]], ps[:, NTOK + t, 0:NT], LN_EPS, None, ALU.add))
                    nc.vector.reciprocal(rs[:, cols[t]], rs[:, cols[t]]).then_inc(S["inv"], 1)

                dve.wait_ge(S["centred"], NTOK)
                inverse(0)
                for t in range(NTOK):
                    dve.wait_ge(S["root"], t + 1)
                    for k in range(KT):
                        x = m.xT[:, k, cols[t]]
                        nc.vector.scalar_tensor_tensor(x, x, m.lnp[:, layer, 2 * part, k:k + 1], rs[:, cols[t]],
                                                       ALU.mult, ALU.mult).then_inc(S["scaled"], 1)
                    if t + 1 < NTOK:
                        inverse(t + 1)
                    if final:
                        continue
                    for k in range(SHARE, KT):
                        dve.wait_ge(S["shifted"], t * KT + k + 1)
                        for s, c0, cn in segments(t):
                            at = slice(t * NT + c0, t * NT + c0 + cn)
                            ins = nc.vector.tensor_scalar(m.hT[:, k, at], m.xT[:, k, at],
                                                          m.mods[:, base + 8 + k, s:s + 1], m.mods[:, base + k, s:s + 1],
                                                          ALU.mult, ALU.add)
                    ins.then_inc(S["h_dve"], 1)
                if split:
                    dve.wait_ge(S["h_dve"], NTOK)
                    low(dve, NTOK - 1)

            if final:
                @block.sync
                def _(sp):
                    for t in range(NTOK):
                        sp.wait_ge(S["shifted"], (t + 1) * KT)
                        sp.dma_start(m.d["yT"][:, :, cols[t]], m.xT[:, :, cols[t]]).then_inc(S["stored"], 16)
                    sp.wait_ge(S["stored"], 16 * NTOK)


def wait(eng, sem, value):
    if not isinstance(value, int) or value > 0:
        eng.wait_ge(sem, value)


def row(tile, at):
    if isinstance(at, int):
        return tile[:, at]
    return tile[:, bass.ds(at, 1)].rearrange("p a n -> p (a n)")


class FfnPlan:
    PARTS = (6, 6, 5, 5)

    def __init__(self):
        self.items = []
        j = 0
        starts = [sum(self.PARTS[:f]) for f in range(4)]
        for f, n in enumerate(self.PARTS):
            if f == 0:
                self.items.append(("up", 0, n, 0))
            else:
                self.items.append(("up", starts[f] + 1, n - 1, f))
            if f < 3:
                self.items.append(("up", starts[f + 1], 1, f + 1))
            self.items.append(("down", starts[f], n, f))
        self.starts = starts

    def slot(self, j):
        f = max(f for f in range(4) if self.starts[f] <= j)
        r = j - self.starts[f]
        return r if r else 6 * (f % 2)

    def walk(self):
        tiles = downs = 0
        for kind, j, n, f in self.items:
            yield kind, j, n, f, tiles, downs
            tiles += 2 * n if kind == "up" else KT
            downs += kind == "down"


def ffn_stage(m, layer, hh, hl, ring, ctx):
    nc, ps, d = m.nc, m.ps, m.d
    PAD = 2
    UW = N + 2 * PAD
    S0 = TP + 2 * PAD
    YW = UW - PAD
    UNITS = 2 * NTOK
    gate = 48 * layer + 24 + 16
    plan = FfnPlan()
    sh = m.sb(f"sh{layer}", [P, 7, N], ctx, F32R)
    sl = m.sb(f"sl{layer}", [P, 7, N], ctx, F32R)
    raw, wh, wlo, loaded, w_hi = ring
    u_ = m.sb(f"u{layer}", [P, 2, UW], ctx)
    y = m.sb(f"y{layer}", [P, 2, YW], ctx)
    cp = m.sb(f"cp{layer}", [P, 8], ctx)
    names = ("w_lo", "u_ready", "u_moved", "down_ready", "added", "staged", "tap0", "tap2", "silu",
             "convolved", "gated", "kept", "zeroed", "scaled", "turns", "chain")
    S = {n: m.sem(f"ffn{layer}_{n}") for n in names}
    S["w_hi"] = w_hi

    def rounds(eng, kind, n, body, uniform):
        count = n if kind == "up" else KT // 2
        first = 0 if uniform else 1
        if first:
            body(0)
        if count - first == 1:
            body(first)
        elif count > first:
            with eng.Fori(first, count) as r:
                body(r)

    with nc.Block() as block:
        @block.sync
        def _(sp):
            for kind, j, n, f, tiles, downs in plan.walk():
                def body(r):
                    for b in range(2):
                        i = tiles + 2 * r + b
                        if isinstance(i, int) and i < 2:
                            continue
                        wait(sp, S["w_lo"], i - 1)
                        if kind == "up":
                            src = row(d["wfi"][layer].rearrange("j p h k m -> p j h k m"), j + r)[:, b] \
                                if isinstance(r, int) else \
                                d["wfi"][layer, bass.ds(r + j, 1)].rearrange("a p h k m -> (a p) h k m")[:, b]
                            to = raw[:, b]
                        else:
                            at = r * 2 + b
                            src = d["wfo"][layer, at] if isinstance(r, int) else \
                                d["wfo"][layer, bass.ds(at, 1)].rearrange("a p k m -> (a p) k m")
                            src, to = src[:, j:j + n], raw[:, b, 0:n]
                        sp.dma_start(to, src).then_inc(loaded[b], 16)
                rounds(sp, kind, n, body, tiles > 0)

        @block.gpsimd
        def _(pool):
            def used(item, r, b):
                kind, j, n, f, tiles, downs = item
                if kind == "up":
                    pool.wait_ge(S["u_ready"], r * UNITS + (j * UNITS + (b + 1) * NTOK))
                else:
                    pool.wait_ge(S["down_ready"], r * UNITS + (downs * KT * NTOK + (b + 1) * NTOK))

            before = None
            nc.gpsimd.memset(u_[:, :, 0:PAD], 0.0).then_inc(S["zeroed"], 1)
            for item in plan.walk():
                kind, j, n, f, tiles, downs = item

                def body(r):
                    for b in range(2):
                        i = tiles + 2 * r + b
                        if isinstance(i, int) and i < 2:
                            continue
                        k = KT if kind == "up" else n
                        pool.wait_ge(loaded[b], r * 16 + (8 * tiles + 16))
                        if not (isinstance(r, int) and r == 0):
                            used(item, r - 1, b)
                        elif before:
                            used(before, (before[2] if before[0] == "up" else KT // 2) - 1, b)
                        pool.sem_inc(S["turns"], 1)
                        nc.gpsimd.tensor_copy(wh[:, b, 0:k], raw[:, b, 0:k]).then_inc(S["w_hi"], 1)
                    if kind == "up":
                        at = j + r
                        if isinstance(r, int):
                            pick = lambda t: t[:, layer, at]
                        else:
                            pick = lambda t: t[:, layer, bass.ds(at, 1)].rearrange("p a n -> p (a n)")
                        wait(pool, S["convolved"], at)
                        wait(pool, S["kept"], at)
                        pool.sem_inc(S["turns"], 1)
                        nc.gpsimd.tensor_copy(cp[:], pick(m.convp))
                        nc.gpsimd.tensor_copy(u_[:, :, TP + PAD:S0], pick(m.convs).rearrange("p (h c) -> p h c", h=2)) \
                            .then_inc(S["staged"], 1)
                rounds(pool, kind, n, body, False)
                before = item

        @block.tensor
        def _(pe):
            def product(bank, b, hi, lo, cols, slots, ks, total):
                for k in ks:
                    for n, (w, x) in enumerate(((wh, hi), (wh, lo), (wlo, hi))):
                        mm = nc.tensor.matmul(ps[:, bank, 0:NT], w[:, b, k], x[:, slots[k], cols],
                                              start=k == n == 0, stop=k == total - 1 and n == 2)
                return mm

            def last_part_start(j, n, tiles, slots):
                pe.wait_ge(S["gated"], j + n - 1)
                for share in (range(n - 1), range(n - 1, n)):
                    for b in range(2):
                        for t in range(NTOK):
                            bank = b * NTOK + t
                            if share[0] == 0:
                                pe.wait_ge(S["w_lo"], tiles + b + 1)
                                pe.wait_ge(S["u_moved"], (FT - 1) * UNITS + bank + 1)
                            else:
                                pe.wait_ge(S["gated"], j + n)
                            mm = product(bank, b, sh, sl, slice(t * NT, (t + 1) * NT), slots, share, n)
                            if share[0]:
                                mm.then_inc(S["down_ready"], 1)

            for kind, j, n, f, tiles, downs in plan.walk():
                def body(r):
                    slots = [plan.slot(j + k) for k in range(n)]
                    if kind == "down" and f == 3 and isinstance(r, int) and r == 0:
                        return last_part_start(j, n, tiles, slots)
                    for b in range(2):
                        i = tiles + 2 * r + b
                        pe.wait_ge(S["w_lo"], i + 1)
                        for t in range(NTOK):
                            bank = b * NTOK + t
                            cols = slice(t * NT, (t + 1) * NT)
                            first = isinstance(r, int) and r == 0
                            if kind == "up":
                                if first and downs and n > 1:
                                    wait(pe, S["added"], downs * KT * NTOK - UNITS + bank + 1)
                                else:
                                    wait(pe, S["u_moved"], (j + r) * UNITS + (bank + 1 - UNITS))
                                mm = product(bank, b, hh, hl, cols, range(KT), range(KT), KT)
                                mm.then_inc(S["u_ready"], 1)
                            else:
                                ups = plan.starts[f + 1] + 1 if f < 3 else FT
                                if first:
                                    if b == 0 and t == 0:
                                        pe.wait_ge(S["gated"], j + n)
                                    wait(pe, S["u_moved"], (ups - 1) * UNITS + bank + 1)
                                else:
                                    pe.wait_ge(S["added"], downs * (KT * NTOK) + r * UNITS + (bank + 1 - UNITS))
                                mm = product(bank, b, sh, sl, cols, slots, range(n), n)
                                mm.then_inc(S["down_ready"], 1)
                rounds(pe, kind, n, body, False)

        @block.scalar
        def _(act):
            for k in range(KT):
                nc.scalar.activation(m.xT[:, k], m.xT[:, k], ACT.Copy, scale=ALPHA).then_inc(S["scaled"], 1)
            act.wait_ge(S["zeroed"], 1)
            for kind, j, n, f, tiles, downs in plan.walk():
                if kind == "down":
                    continue

                def body(r):
                    at = j + r
                    act.wait_ge(S["staged"], at + 1)
                    for q in range(UNITS):
                        half, t = divmod(q, NTOK)
                        act.wait_ge(S["u_ready"], at * UNITS + (q + 1))
                        for s, c0, cn in segments(t):
                            to = t * NT + c0 + PAD * (s + 1)
                            ins = nc.scalar.activation(u_[:, half, to:to + cn], ps[:, q, c0:c0 + cn], ACT.Copy)
                        ins.then_inc(S["u_moved"], 1)
                    act.wait_ge(S["u_moved"], (at + 1) * UNITS)
                    wait(act, S["gated"], at)
                    for half in range(2):
                        nc.scalar.activation(y[:, half], u_[:, half, 0:YW], ACT.Identity,
                                             bias=cp[:, 4 * half + 3:4 * half + 4],
                                             scale=cp[:, 4 * half:4 * half + 1]).then_inc(S["tap0"], 1)
                    act.wait_ge(S["tap2"], at + 1)
                    nc.scalar.activation(y[:, 1], y[:, 1], ACT.Silu).then_inc(S["silu"], 1)
                rounds(act, kind, n, body, tiles > 0)

        @block.vector
        def _(dve):
            chain = Chain(dve, S["chain"])

            def split_lo(kind, n, i, b):
                k = KT if kind == "up" else n
                dve.wait_ge(S["w_hi"], i + 1)
                nc.vector.tensor_tensor(wlo[:, b, 0:k], raw[:, b, 0:k], wh[:, b, 0:k].bitcast(F32), ALU.subtract) \
                    .then_inc(S["w_lo"], 1)

            items = list(plan.walk())
            for b in range(2):
                split_lo("up", 1, b, b)
            for at_item, (kind, j, n, f, tiles, downs) in enumerate(items):
                count = n if kind == "up" else KT // 2
                nxt = items[at_item + 1] if at_item + 1 < len(items) else None

                def following(r, b):
                    if isinstance(r, int) and r == count - 1:
                        if nxt:
                            split_lo(nxt[0], nxt[2], nxt[4] + b, b)
                    else:
                        split_lo(kind, n, tiles + 2 * (r + 1) + b, b)

                def up(r):
                    at = j + r
                    following(r, 0)
                    following(r, 1)
                    dve.wait_ge(S["tap0"], at * 2 + 2)
                    for tap in (1, 2):
                        for half in (1, 0):
                            ins = nc.vector.scalar_tensor_tensor(
                                y[:, half], u_[:, half, tap:tap + YW], cp[:, 4 * half + tap:4 * half + tap + 1],
                                y[:, half], ALU.mult, ALU.add)
                            if (tap, half) == (2, 1):
                                ins.then_inc(S["tap2"], 1)
                            elif (tap, half) == (2, 0):
                                ins.then_inc(S["convolved"], 1)
                            else:
                                chain.link(ins)
                    for s, c0 in enumerate((TP, UW - PAD)):
                        to = m.convo[:, layer, at, 4 * s:4 * s + 4] if isinstance(r, int) else \
                            m.convo[:, layer, bass.ds(at, 1), 4 * s:4 * s + 4].rearrange("p a n -> p (a n)")
                        ins = nc.vector.tensor_copy(to.rearrange("p (h c) -> p h c", h=2), u_[:, :, c0:c0 + PAD])
                    ins.then_inc(S["kept"], 1)
                    dve.wait_ge(S["convolved"], at + 1)
                    dve.wait_ge(S["silu"], at + 1)
                    chain.link(nc.vector.tensor_tensor(y[:, 0], y[:, 0], y[:, 1], ALU.mult))
                    if downs:
                        dve.wait_ge(S["down_ready"], downs * (KT * NTOK))
                    slot = plan.slot(j + r) if isinstance(r, int) else r + plan.slot(j + 1) - 1
                    pick = lambda t, a, e: t[:, slot, a:e] if isinstance(r, int) else \
                        t[:, bass.ds(slot, 1), a:e].rearrange("p a n -> p (a n)")
                    for s, (a, e) in enumerate(SEQS):
                        ins = nc.vector.tensor_copy(pick(sh, a, e), y[:, 0, a + PAD * s:e + PAD * s])
                    chain.link(ins)
                    for s, (a, e) in enumerate(SEQS):
                        ins = nc.vector.tensor_tensor(pick(sl, a, e), y[:, 0, a + PAD * s:e + PAD * s],
                                                      pick(sh, a, e).bitcast(F32), ALU.subtract)
                    ins.then_inc(S["gated"], 1)

                def down(r):
                    for b in range(2):
                        following(r, b)
                        for t in range(NTOK):
                            bank = b * NTOK + t
                            dve.wait_ge(S["down_ready"], downs * (KT * NTOK) + r * UNITS + (bank + 1))
                            for s, c0, cn in segments(t):
                                cols = slice(t * NT + c0, t * NT + c0 + cn)
                                tile = r * 2 + b
                                if isinstance(r, int):
                                    x, g = m.xT[:, tile, cols], m.mods[:, gate + tile, s:s + 1]
                                else:
                                    x = m.xT[:, bass.ds(tile, 1), cols].rearrange("p a n -> p (a n)")
                                    g = m.mods[:, bass.ds(tile + gate, 1), s:s + 1].rearrange("p a n -> p (a n)")
                                ins = nc.vector.scalar_tensor_tensor(x, ps[:, bank, c0:c0 + cn], g, x, ALU.mult, ALU.add)
                            ins.then_inc(S["added"], 1)

                if kind == "down" and downs == 0:
                    dve.wait_ge(S["scaled"], KT)
                if kind == "down" and downs:
                    dve.wait_ge(S["added"], downs * KT * NTOK)
                body = up if kind == "up" else down
                per = 4 if kind == "up" else 0
                lo, hi = (1 if kind == "up" and f == 0 else 0), count - 1
                for r in range(lo):
                    body(r)
                if hi > lo:
                    if hi - lo == 1:
                        body(lo)
                    else:
                        with chain.loop(hi, per, lo) as r:
                            body(r)
                if hi >= lo:
                    body(hi)


class Keys:

    def __init__(self, q0, nq, key_tiles, sample=False, wide=False):
        self.q0, self.nq, self.tiles = q0, nq, key_tiles
        self.nk = sum(t[1] for t in key_tiles)
        self.sample, self.wide = sample, wide
        self.s_bank = (0, 3) if wide else (0, 2)
        self.t_banks = (6,) if wide else (4, 5)
        self.o_banks = (7, 7) if wide else (6, 7)
        self.per = 16 if wide else 4
        self.groups = -(-len(key_tiles) // self.per)
        at, self.offsets = 0, []
        for col, size, v in key_tiles:
            self.offsets.append((at, size, v))
            at += size

    def bank(self, ps, u):
        b = self.s_bank[u]
        return ps[0:self.nq, b:b + 3 if self.wide else b + 2, :].rearrange("p a b -> p (a b)")[:, 0:self.nk]


IDX_CHUNK = 512
SEL_ROUNDS = (4, 3, 3, 3, 3, 4)
SEL_AHEAD = (TOPK // 8 - sum(SEL_ROUNDS)) // 2


class Selection:

    def __init__(self, n, kb, buffers, units0):
        self.n, self.kb, self.score = n, kb, buffers[n % len(buffers)]
        self.units0 = units0
        width = -(-kb.nk // -(-kb.nk // IDX_CHUNK))
        self.chunks = [(a, min(kb.nk, a + width)) for a in range(0, kb.nk, width)]
        self.C = len(self.chunks)


def attention_stage(m, tag, blocks, kind, q_of, k_of, v_of, dv, rows, out_tile, bias_w=0, bias_of=None,
                    bias_added=None, sink=False, index=None, sels=None, out=None, osb=None):
    nc, ps = m.nc, m.ps
    out = m.hT if out is None else out
    sels = sels or {}
    names = ("q_staged", "s_ready", "max_ready", "p_ready", "t_ready", "t_moved", "o_ready", "o_moved",
             "inv_ready", "chain", "turns") + ("pchain", "pool_turns") * bool(bias_w) + \
        ("mask_ready", "relu_free", "qi_staged") * bool(index)
    S = {n: m.sem(f"{tag}_{n}") for n in names}
    s_free = S["max_ready"] if bias_w else S["p_ready"]
    vector_moves = not bias_w
    c = ExitStack()
    with c:
        qst = m.sb(tag + "qst", [P, 2, P], c)
        prob = m.sb(tag + "prob", [P, 2, max(kb.nk for kb in blocks)], c)
        probT = m.sb(tag + "probT", [P, 2, max(len(kb.tiles) * kb.nq for kb in blocks)], c)
        if osb is None:
            osb = m.sb(tag + "osb", [P, min(2, len(blocks)), HEADS * dv], c)
        stat = m.sb(tag + "stat", [P, 2, 8], c)
        bm = m.sb(tag + "bm", [P, 2, bias_w], c) if bias_w else None
        if index:
            relu = m.sb(tag + "relu", [P, 2, N], c)
            qist = m.sb(tag + "qist", [P, 2, P], c)
            best = m.sb(tag + "best", [P, 8], c)
        OT = HEADS * dv // P
        OG = -(-OT // 4)

        plan = []
        for n, kb in enumerate(blocks):
            prev = plan[-1] if plan else None
            p = dict(kb=kb, n=n, pair=8 * n, G=kb.groups, prev=prev, next=None)
            p["select"] = sels.get(n + 1) if index else None
            p["index"] = sels.get(n + 2) if index else None
            p["C"] = p["index"].C if p["index"] else 0
            p["T"] = prev["end"] if prev else 0
            p["O_prev"] = p["T"] + 7 * p["G"] + 8 * p["C"]
            p["T7"] = p["O_prev"] + (OG if prev else 0)
            p["end"] = p["T7"] + p["G"]
            if prev:
                prev["next"] = p
            plan.append(p)
        last = plan[-1]

        def t_group(p, t, u):
            if isinstance(t, int):
                k = 2 * t + u
                return p["T7"] if k == 7 else p["T"] + k * p["G"] + 2 * p["C"] * max(0, min(k - 1, 4))
            return t * (2 * p["G"]) + (p["T"] + u * p["G"])

        def i_group(p, h):
            return t_group(p, (h // 2 + 1) // 2, (h // 2 + 1) % 2) + p["G"] + h % 2 * p["C"]

        def index_heads(p, k):
            return (2 * k, 2 * k + 1) if p["index"] and 0 <= k < 4 else ()

        def t_bank(p, t, u, g):
            first = t_group(p, t if isinstance(t, int) else 0, u)
            return p["kb"].t_banks[(first + g) % len(p["kb"].t_banks)]

        def slots(eng, p, slot, chain=None, per=0, peel=False):
            first = 1 if p["n"] == 0 or peel else 0
            if p["kb"].sample or index:
                first = 3
            for t in range(first):
                slot(t, 0)
                slot(t, 1)
            if first < 3:
                with chain.loop(3, per, first) if chain else eng.Fori(first, 3) as t:
                    slot(t, 0)
                    slot(t, 1)

        def after(p, t, u, k):
            j = u + k
            t, u = t + j // 2, j % 2
            if isinstance(t, int) and t > 3:
                return (p["next"], t - 4, u) if p["next"] else None
            if isinstance(t, int) and t < 0:
                return (p["prev"], t + 4, u) if p["prev"] else None
            return p, t, u

        def count(p, t, u):
            return p["pair"] + t * 2 + u

        def moved(eng, out, src):
            return nc.vector.tensor_copy(out, src) if vector_moves else nc.scalar.activation(out, src, ACT.Copy)

        def move(eng, p, t, u):
            kb, nq = p["kb"], p["kb"].nq
            if vector_moves:
                wait(eng, S["o_ready"], count(p, t, u) - 1)
            for g in range(p["G"]):
                eng.wait_ge(S["t_ready"], t_group(p, t, u) + (g + 1))
                if vector_moves:
                    eng.sem_inc(S["turns"], 1)
                bank = t_bank(p, t, u, g)
                part = kb.offsets[g * kb.per:(g + 1) * kb.per]
                at, full = g * kb.per * nq, sum(size == P for _, size, _ in part)
                ins = moved(eng, probT[:, u, at:at + full * nq], ps[:, bank, 0:full * nq])
                if full < len(part):
                    ins = moved(eng, probT[0:TS, u, at + full * nq:at + (full + 1) * nq],
                                ps[0:TS, bank, full * nq:(full + 1) * nq])
                ins.then_inc(S["t_moved"], 1)

        def outputs_moved(eng, p, first):
            kb, nq = p["kb"], p["kb"].nq
            for g in range(OG):
                eng.wait_ge(S["t_ready"], first + g + 1)
                bank = kb.t_banks[(first + g) % len(kb.t_banks)]
                k = min(4, OT - 4 * g)
                moved(eng, out[:, out_tile + 4 * g:out_tile + 4 * g + k, kb.q0:kb.q0 + nq],
                      ps[:, bank, 0:k * nq].rearrange("p (a n) -> p a n", a=k)).then_inc(S["t_moved"], 1)

        with nc.Block() as block:
            @block.gpsimd
            def _(pool):
                chain = Chain(pool, S["pchain"]) if bias_w else None

                def index_queries(p, k):
                    pool.wait_ge(S["q_staged"], p["pair"] + k + 1)
                    for h in index_heads(p, k - 1):
                        s = p["index"]
                        if h >= 4:
                            pool.wait_ge(S["t_ready"], i_group(p, h - 4) + p["C"])
                        elif p["prev"] and p["prev"]["index"]:
                            pool.wait_ge(S["t_ready"], i_group(p["prev"], h + 4) + p["prev"]["C"])
                        r = slice(64 * (h % 2), 64 * (h % 2) + 64)
                        nc.gpsimd.tensor_copy(qist[r, h // 2 % 2, 0:s.kb.nq], index["q"][r, h // 2, s.kb.q0:s.kb.q0 + s.kb.nq]) \
                            .then_inc(S["qi_staged"], 1)
                        pool.wait_ge(S["qi_staged"], 8 * s.n + h + 1)

                for p in plan:
                    kb, nq = p["kb"], p["kb"].nq
                    sel = sels.get(p["n"])
                    masked = not kb.sample and not sel

                    def body(t):
                        for u in range(2):
                            n = count(p, t, u)
                            wait(pool, S["s_ready"], n - 1)
                            if bias_w:
                                wait(pool, s_free, n - 1)
                                bt = bias_of(t + 4 * u, kb)
                                to = bm[0:nq, u, 0:kb.nk]
                                standing = S["pool_turns"]
                                if sel:
                                    if u == 0 and index:
                                        pool.wait_ge(S["mask_ready"], sel.n + 1)
                                    chain.link(nc.gpsimd.tensor_tensor(to, bt, sel.score[0:nq, 0:kb.nk], ALU.add))
                                else:
                                    chain.link(nc.gpsimd.tensor_copy(to, bt), standing)
                                if masked:
                                    chain.link(nc.gpsimd.memset(bm[0:CHUNK, u, kb.nk - CHUNK:kb.nk], NEG), standing)
                            nc.gpsimd.tensor_copy(qst[rows(u), u, 0:nq], q_of(t, u, kb)).then_inc(S["q_staged"], 1)
                            if index:
                                index_queries(p, 2 * t + u)
                            if kind == "swa":
                                pool.wait_ge(S["q_staged"], n + 1)
                    per = 2 * (1 + masked) if bias_w else 0
                    first = 4 if kb.sample or index else p["n"] == 0
                    for t in range(first):
                        body(t)
                    if first < 4:
                        with chain.loop(4, per, int(first)) if chain else pool.Fori(int(first), 4) as t:
                            body(t)

            @block.tensor
            def _(pe):
                def scores(p, t, u):
                    kb, n = p["kb"], count(p, t, u)
                    pe.wait_ge(S["q_staged"], n + 1)
                    wait(pe, s_free, n - 1)
                    s = kb.bank(ps, u)
                    for n0 in range(0, kb.nk, 512):
                        n1 = min(kb.nk, n0 + 512)
                        mm = nc.tensor.matmul(s[:, n0:n1], qst[rows(u), u, 0:kb.nq], k_of(t, u, kb, n0, n1),
                                              start=True, stop=not bias_added)
                        if bias_added:
                            mm = nc.tensor.matmul(s[:, n0:n1], m.ident[0:kb.nq, 0:kb.nq],
                                                  bias_added(t + 4 * u, kb)[:, n0:n1], start=False, stop=True)
                    mm.then_inc(S["s_ready"], 1)

                def transposes(p, t, u):
                    kb, nq = p["kb"], p["kb"].nq
                    pe.wait_ge(S["p_ready"], count(p, t, u) + 1)
                    for g in range(p["G"]):
                        wait(pe, S["t_moved"], t_group(p, t, u) + (g - len(kb.t_banks) + 1))
                        for j, (at, size, _) in enumerate(kb.offsets[g * kb.per:(g + 1) * kb.per]):
                            mm = nc.tensor.transpose(ps[0:size, t_bank(p, t, u, g), j * nq:(j + 1) * nq],
                                                     prob[0:nq, u, at:at + size], m.ident[0:nq, 0:nq])
                        mm.then_inc(S["t_ready"], 1)

                def values(p, t, u):
                    kb, nq, n = p["kb"], p["kb"].nq, count(p, t, u)
                    pe.wait_ge(S["t_moved"], t_group(p, t, u) + p["G"])
                    wait(pe, S["o_moved"], n if kb.wide else n - 1)
                    for j, (at, size, v) in enumerate(kb.offsets):
                        mm = nc.tensor.matmul(ps[0:nq, kb.o_banks[u], 0:dv], probT[0:size, u, j * nq:(j + 1) * nq],
                                              v_of(t, u, v, size), start=j == 0, stop=j == len(kb.offsets) - 1)
                    mm.then_inc(S["o_ready"], 1)

                def outputs(p, first):
                    kb, nq = p["kb"], p["kb"].nq
                    pe.wait_ge(S["o_moved"], p["pair"] + 8)
                    for g in range(OG):
                        wait(pe, S["t_moved"], first + g - len(kb.t_banks) + 1)
                        bank = kb.t_banks[(first + g) % len(kb.t_banks)]
                        for j in range(min(4, OT - 4 * g)):
                            cols = slice((4 * g + j) * P, (4 * g + j + 1) * P)
                            mm = nc.tensor.transpose(ps[:, bank, j * nq:(j + 1) * nq], osb[0:nq, p["n"] % 2, cols],
                                                     m.ident[0:nq, 0:nq])
                        mm.then_inc(S["t_ready"], 1)

                def index_scores(p, h):
                    s, g = p["index"], i_group(p, h)
                    nq, r, k0 = s.kb.nq, slice(64 * (h % 2), 64 * (h % 2) + 64), s.kb.tiles[0][0]
                    pe.wait_ge(S["qi_staged"], 8 * s.n + h + 1)
                    for j, (a, b) in enumerate(s.chunks):
                        wait(pe, S["t_moved"], g + j - 1)
                        nc.tensor.matmul(ps[0:nq, 4 + (g + j) % 2, 0:b - a], qist[r, h // 2 % 2, 0:nq],
                                         index["k"][r, k0 + a:k0 + b], start=True, stop=True).then_inc(S["t_ready"], 1)

                def slot(p, t, u):
                    for k, do in ((2, scores), (1, transposes), (0, values)):
                        at = after(p, t, u, k)
                        if at:
                            do(*at)
                    if index:
                        for h in index_heads(p, 2 * t + u):
                            index_scores(p, h)
                scores(plan[0], 0, 0)
                scores(plan[0], 0, 1)
                transposes(plan[0], 0, 0)
                for p in plan:
                    slots(pe, p, lambda t, u: slot(p, t, u))
                    if p["prev"]:
                        outputs(p["prev"], p["O_prev"])
                    slot(p, 3, 0)
                    slot(p, 3, 1)
                outputs(last, last["end"])

            @block.scalar
            def _(act):
                def exps(p, t, u):
                    kb, nq, n = p["kb"], p["kb"].nq, count(p, t, u)
                    act.wait_ge(S["max_ready"], n + 1)
                    wait(act, S["inv_ready"], n - 1)
                    if not bias_w:
                        prev = after(p, t, u, -2)
                        if prev:
                            wait(act, S["t_ready"], t_group(*prev) + prev[0]["G"])
                    src = prob[0:nq, u, 0:kb.nk] if bias_w else kb.bank(ps, u)
                    ins = nc.scalar.activation(prob[0:nq, u, 0:kb.nk], src, ACT.Exp, bias=stat[0:nq, u, 1:2],
                                               accum_out=stat[0:nq, u, 2:3])
                    if sink:
                        ins = nc.scalar.activation(stat[0:nq, u, 4:5], stat[0:nq, u, 5:6], ACT.Exp,
                                                   bias=stat[0:nq, u, 1:2])
                    ins.then_inc(S["p_ready"], 1)

                def normed(p, t, u):
                    kb, nq, n = p["kb"], p["kb"].nq, count(p, t, u)
                    act.wait_ge(S["o_ready"], n + 1)
                    act.wait_ge(S["inv_ready"], n + 1)
                    cols = bass.ds((t + 4 * u) * dv, dv)
                    nc.scalar.activation(osb[0:nq, p["n"] % 2, cols], ps[0:nq, kb.o_banks[u], 0:dv], ACT.Copy,
                                         scale=stat[0:nq, u, 3:4]).then_inc(S["o_moved"], 1)

                def index_relu(p, k):
                    for h in index_heads(p, k - 1):
                        s, g = p["index"], i_group(p, h)
                        nq = s.kb.nq
                        wait(act, S["relu_free"], s.units0 + max(0, h - 1) * s.C)
                        for j, (a, b) in enumerate(s.chunks):
                            act.wait_ge(S["t_ready"], g + j + 1)
                            nc.scalar.activation(relu[0:nq, h % 2, a:b], ps[0:nq, 4 + (g + j) % 2, 0:b - a], ACT.Relu) \
                                .then_inc(S["t_moved"], 1)

                def slot(p, t, u, skip_move=False):
                    if not (vector_moves or skip_move):
                        move(act, p, t, u)
                        if index:
                            index_relu(p, 2 * t + u)
                    for k, do in ((1, exps), (-1, normed)):
                        at = after(p, t, u, k)
                        if at:
                            do(*at)
                exps(plan[0], 0, 0)
                for p in plan:
                    slots(act, p, lambda t, u: slot(p, t, u), peel=True)
                    if not vector_moves:
                        move(act, p, 3, 0)
                        if p["prev"]:
                            outputs_moved(act, p["prev"], p["O_prev"])
                    slot(p, 3, 0, skip_move=True)
                    slot(p, 3, 1)
                normed(last, 3, 1)
                if not vector_moves:
                    outputs_moved(act, last, last["end"])

            @block.vector
            def _(dve):
                chain = Chain(dve, S["chain"])

                def maxima(p, t, u, meanwhile=None):
                    kb, nq, nk, n = p["kb"], p["kb"].nq, p["kb"].nk, count(p, t, u)
                    dve.wait_ge(S["s_ready"], n + 1)
                    s = kb.bank(ps, u)
                    wait(dve, S["p_ready"], n - 1)
                    if sink:
                        chain.issue(nc.vector.tensor_copy(stat[0:nq, u, 5:6], m.sinks[0:nq, bass.ds(t + 4 * u, 1)]))
                    if bias_w:
                        prev = after(p, t, u, -2)
                        if prev:
                            wait(dve, S["t_ready"], t_group(*prev) + prev[0]["G"])
                        dve.sem_inc(S["turns"], 1)
                        chain.issue(nc.vector.tensor_tensor_reduce(
                            out=prob[0:nq, u, 0:nk], in0=s, in1=bm[0:nq, u, 0:nk], scale=1.0,
                            scalar=stat[0:nq, u, 5:6] if sink else m.negs[0:nq],
                            op0=ALU.add, op1=ALU.max, accum_out=stat[0:nq, u, 0:1]))
                        if meanwhile:
                            inverse(*meanwhile)
                        chain.wait()
                        nc.vector.tensor_scalar(stat[0:nq, u, 1:2], stat[0:nq, u, 0:1], -1.0, None, ALU.mult) \
                            .then_inc(S["max_ready"], 1)
                    else:
                        if not kb.sample and not bias_added:
                            chain.link(nc.vector.memset(s[0:CHUNK, nk - CHUNK:nk], NEG))
                        ins = nc.vector.tensor_reduce(stat[0:nq, u, 1:2], s, AX.X, ALU.max, negate=True)
                        if sink:
                            chain.link(ins)
                            ins = nc.vector.scalar_tensor_tensor(stat[0:nq, u, 1:2], stat[0:nq, u, 5:6], -1.0,
                                                                 stat[0:nq, u, 1:2], ALU.mult, ALU.min)
                        ins.then_inc(S["max_ready"], 1)

                def inverse(p, t, u):
                    nq, n = p["kb"].nq, count(p, t, u)
                    dve.wait_ge(S["p_ready"], n + 1)
                    wait(dve, S["o_moved"], n - 1)
                    if sink:
                        chain.link(nc.vector.tensor_tensor(stat[0:nq, u, 2:3], stat[0:nq, u, 2:3],
                                                           stat[0:nq, u, 4:5], ALU.add))
                    nc.vector.reciprocal(stat[0:nq, u, 3:4], stat[0:nq, u, 2:3]).then_inc(S["inv_ready"], 1)

                def select(s, k):
                    sc = s.score[0:s.kb.nq, 0:s.kb.nk]
                    for n in range(2 * k):
                        chain.issue(nc.vector.match_replace(sc, best[0:s.kb.nq], sc, TAKEN) if n % 2 else
                                    nc.vector.max(best[0:s.kb.nq], sc))
                        yield n
                        chain.wait(S["turns"])

                def mask(s):
                    sc = s.score[0:s.kb.nq, 0:s.kb.nk]
                    ins = nc.vector.tensor_scalar(sc, sc, TAKEN / 2, NEG, ALU.is_gt, ALU.mult)
                    if not s.kb.sample:
                        chain.link(ins)
                        ins = nc.vector.memset(s.score[0:CHUNK, s.kb.nk - CHUNK:s.kb.nk], NEG)
                    ins.then_inc(S["mask_ready"], 1)

                def index_sum(p, k, i):
                    s = p["index"]
                    h, j = index_heads(p, k - 1)[i // s.C], i % s.C
                    g, kb, nq, (a, b) = i_group(p, h), s.kb, s.kb.nq, s.chunks[j]
                    if h == j == 0:
                        wait(dve, S["q_staged"], p["pair"])
                    dve.wait_ge(S["t_moved"], g + j + 1)
                    wi = index["w"][0:nq, kb.q0 // P, h:h + 1]
                    sc, src = s.score[0:nq, a:b], relu[0:nq, h % 2, a:b]
                    if h == 0:
                        ins = nc.vector.tensor_scalar(sc, src, wi, None, ALU.mult)
                    else:
                        dve.wait_ge(S["relu_free"], s.units0 + (h - 1) * s.C + j + 1)
                        ins = nc.vector.scalar_tensor_tensor(sc, src, wi, sc, ALU.mult, ALU.add)
                    ins.then_inc(S["relu_free"], 1)

                def summed(s):
                    dve.wait_ge(S["relu_free"], s.units0 + 8 * s.C)
                    if not s.kb.sample:
                        chain.link(nc.vector.memset(s.score[0:CHUNK, s.kb.nk - CHUNK:s.kb.nk], NEG))

                def slot(p, t, u):
                    at = after(p, t, u, 1)
                    if at:
                        maxima(*at, meanwhile=(p, t, u) if bias_w else None)
                    if vector_moves:
                        move(dve, p, t, u)
                        if p["prev"] and isinstance(t, int) and (t, u) == (3, 0):
                            outputs_moved(dve, p["prev"], p["O_prev"])
                    if not (at and bias_w):
                        inverse(p, t, u)
                    if index:
                        k = 2 * t + u
                        pieces = len(index_heads(p, k - 1)) * p["C"]
                        rounds = SEL_ROUNDS[k] if p["select"] and k < 6 else 0
                        early = max(0, pieces - 2 * rounds)
                        for i in range(early):
                            index_sum(p, k, i)
                        if rounds:
                            for n in select(p["select"], rounds):
                                if n >= 2 * rounds - (pieces - early):
                                    index_sum(p, k, pieces - 2 * rounds + n)
                        if p["index"] and k == 5:
                            summed(p["index"])
                        if p["index"] and k >= 6:
                            for _ in select(p["index"], SEL_AHEAD):
                                pass
                maxima(plan[0], 0, 0)
                for p in plan:
                    per = 3 if sink else 1 if bias_w else int(not p["kb"].sample)
                    slots(dve, p, lambda t, u: slot(p, t, u), chain, 2 * per)
                    if p["select"]:
                        mask(p["select"])
                    slot(p, 3, 0)
                    slot(p, 3, 1)
                if vector_moves:
                    outputs_moved(dve, last, last["end"])


def entry_stage(m, lat, kpe, cq, rope, qs, ks, vs, R):
    nc, d, ps = m.nc, m.d, m.ps
    with ExitStack() as c:
        CW = 512
        CHUNKS = 96 * P // CW
        TILES = CW // P
        NB = 3
        HK = KT // 2
        WE_PARTS = ((0, 512), (512, 1024), (1024, EVEN_W))
        UB = 5
        we = m.sb("we", [P, KT, EVEN_W], c)
        wada = m.sb("wada", [P, NB, HK, CW], c)
        rows = m.sb("modrows", [P, 2, CW], c)
        rot = m.sb("rot", [P, N], c)
        bada = m.sb("bada", [P, 96, 2], c)
        cT = m.sb("cT", [P, KT, 2], c)
        csT = m.sb("csT", [P, KT, 2], c)
        rel = m.sb("rel", [32, HEADS], c)
        onehot = rope[0:32].rearrange("p a n -> p (a n)")[:, 0:REL_LEN]
        relrow = kpe[0:HEADS, 0:REL_LEN]
        loaded = [m.sem(f"wada_loaded{i}") for i in range(NB)]
        we_loaded = [m.sem(f"we_loaded{i}") for i in range(len(WE_PARTS))]
        names = ("par_loaded", "c_loaded", "rel_loaded", "x_loaded", "caches_loaded", "later_loaded", "c_silu", "half_done",
                 "rowed", "turned", "mods_out", "rows_zeroed", "rel_mm", "rel_ev", "rel_stored", "h_ready",
                 "e_ready", "e_moved", "e_roped")
        S = {n: m.sem(n) for n in names}
        params = [(m.ident, "ident"), (bada, "bada")]
        later = [(m.lnp, "lnp"), (m.convp, "convp"), (m.convs, "convs"), (m.sinks, "sinks"), (m.gq, "gq"), (m.ones, "ones")]
        caches = [(lat[:, TP:TP + PAST], "c_lat"), (kpe[R, TP:TP + PAST], "c_kpe"),
                  (ks[:, TP:TP + P], "c_swak"), (vs[:, 8], "c_swav"), (rope[R], "rope")]

        tiles = [("cq", 0, 0), ("cq", 1, 128), ("lat", 0, 256), ("ks", 0, 384)] + \
                [("qs", t, 512 + P * t) for t in range(4)]
        units = [(n, i, c0, t) for n, i, c0 in tiles for t in range(NTOK)]
        units += [("v", i, 1024, 0) for i in range(9)]
        rbase = len(units)
        units += [("kr", j, 1152 + 32 * j, t) for j in range(2) for t in range(NTOK)]

        order = [("chunk", 0), ("chunk", 1), ("turn", 0), ("chunk", 2), ("chunk", 3), ("turn", 1)]
        chunks, turns = 4, 2
        for q in range(len(units)):
            order.append(("unit", q))
            if 2 * turns + 2 <= chunks:
                order.append(("turn", turns))
                turns += 1
            if (q % 2 or q == 0) and chunks < CHUNKS:
                order.append(("chunk", chunks))
                chunks += 1
        order += [("turn", g) for g in range(turns, CHUNKS // 2)]
        assert chunks == CHUNKS

        with nc.Block() as block:
            @block.sync
            def _(sp):
                sp.wait_ge(S["c_loaded"], 16)
                sp.wait_ge(S["rel_loaded"], 32)
                sp.dma_start(m.xT[:], d["xT"]).then_inc(S["x_loaded"], 16)
                for u in range(NB):
                    sp.dma_start(wada[:, u], d["wada"][u]).then_inc(loaded[u], 16)
                for n in range(NB, 3 * NB):
                    if n == 8:
                        for (c0, c1), part_loaded in zip(WE_PARTS, we_loaded):
                            sp.dma_start(we[:, :, c0:c1], d["we"][:, :, c0:c1]).then_inc(part_loaded, 16)
                    sp.wait_ge(S["half_done"], n - NB + 1)
                    sp.dma_start(wada[:, n % NB], d["wada"][n]).then_inc(loaded[n % NB], 16)
                with sp.Fori(3, 2 * CHUNKS // NB) as i:
                    for u in range(NB):
                        sp.wait_ge(S["half_done"], i * NB + (u - NB + 1))
                        sp.dma_start(wada[:, u], d["wada"][bass.ds(i * NB + u, 1)]
                                     .rearrange("a p k m -> (a p) k m")).then_inc(loaded[u], 16)

            @block.scalar
            def _(act):
                act.dma_start(cT[:], d["cT"]).then_inc(S["c_loaded"], 16)
                act.dma_start(onehot, d["onehot"]).then_inc(S["rel_loaded"], 16)
                act.dma_start(rel[:], d["rel_bias"]).then_inc(S["rel_loaded"], 16)
                for tile, name in params:
                    act.dma_start(tile[:], d[name]).then_inc(S["par_loaded"], 16)
                act.wait_ge(S["c_loaded"], 16)
                nc.scalar.activation(csT[:], cT[:], ACT.Silu).then_inc(S["c_silu"], 1)
                act.wait_ge(S["rel_ev"], 1)
                act.dma_start(m.biasd, spread(relrow, P)).then_inc(S["rel_stored"], 16)
                act.wait_ge(S["rows_zeroed"], 1)

                def chunk(n):
                    g, at = n // 2, slice(32 * (n % 2), 32 * (n % 2) + 2)
                    if g >= 2:
                        act.wait_ge(S["turned"], g - 1)
                    act.wait_ge(S["half_done"], 2 * n + 2)
                    nc.scalar.activation(rows[at, g % 2], ps[at, UB + n % 2], ACT.Copy).then_inc(S["rowed"], 1)

                def unit(q):
                    name, i, _, t = units[q]
                    if name == "kr":
                        return
                    act.wait_ge(S["e_ready"], q + 1)
                    bank = q % UB
                    if name == "v":
                        rows_ = P if i < 8 else TS
                        pieces = [(vs[0:rows_, i if i < 8 else 9], ps[0:rows_, bank, 0:P])]
                    elif name in ("cq", "qs"):
                        pieces = [((cq if name == "cq" else qs)[:, i, t * NT:(t + 1) * NT], ps[:, bank, 0:NT])]
                    else:
                        tile, start = (lat, TP + PAST) if name == "lat" else (ks, TP + P)
                        pieces = [(tile[:, t * NT + c0:t * NT + c0 + cn] if s == 0 else tile[:, start:start + cn],
                                   ps[:, bank, c0:c0 + cn]) for s, c0, cn in segments(t)]
                    for to, src in pieces:
                        ins = nc.scalar.activation(to, src, ACT.Copy, scale=SWA_SCALE if name == "qs" else 1.0)
                    ins.then_inc(S["e_moved"], 1)

                for kind, n in order:
                    if kind == "chunk":
                        chunk(n)
                        if n == 4:
                            for tile, name in caches:
                                act.dma_start(tile, d[name]).then_inc(S["caches_loaded"], 16)
                            for tile, name in later:
                                act.dma_start(tile[:], d[name]).then_inc(S["later_loaded"], 16)
                    elif kind == "unit":
                        unit(n)
                act.wait_ge(S["rel_stored"], 16)
                act.wait_ge(S["later_loaded"], 16 * len(later))

            @block.tensor
            def _(pe):
                pe.wait_ge(S["rel_loaded"], 32)
                for q in range(3):
                    n0, n1 = q * 512, min(REL_LEN, (q + 1) * 512)
                    mm = nc.tensor.matmul(ps[0:HEADS, q, 0:n1 - n0], rel[:], onehot[:, n0:n1],
                                          start=True, stop=True)
                mm.then_inc(S["rel_mm"], 1)
                pe.wait_ge(S["c_silu"], 1)

                def chunk(n):
                    if n >= 2:
                        pe.wait_ge(S["rowed"], n - 1)
                    at = slice(32 * (n % 2), 32 * (n % 2) + 2)
                    for f in range(2):
                        u = (2 * n + f) % NB
                        pe.wait_ge(loaded[u], 16 * ((2 * n + f) // NB + 1))
                        for k in range(HK):
                            mm = nc.tensor.matmul(ps[at, UB + n % 2], csT[:, f * HK + k], wada[:, u, k],
                                                  start=f == k == 0, stop=f == 1 and k == HK - 1)
                        mm.then_inc(S["half_done"], 1)

                def turn(g):
                    if g == 0:
                        pe.wait_ge(S["par_loaded"], 16 * len(params))
                    else:
                        pe.wait_ge(S["mods_out"], g)
                    pe.wait_ge(S["rowed"], 2 * g + 2)
                    for j in range(TILES):
                        mm = nc.tensor.matmul(ps[:, 7, P * j:P * (j + 1)], rows[:, g % 2, P * j:P * (j + 1)], m.ident[:],
                                              start=True, stop=True)
                    mm.then_inc(S["turned"], 1)

                def unit(q):
                    name, i, c0, t = units[q]
                    if q == 0:
                        pe.wait_ge(S["rel_ev"], 1)
                    if q == 0 or units[q - 1][2] // 512 != c0 // 512:
                        pe.wait_ge(we_loaded[c0 // 512], 16)
                    if q >= UB + rbase:
                        pe.wait_ge(S["e_roped"], q - UB - rbase + 1)
                    elif q >= UB:
                        pe.wait_ge(S["e_moved"], q - UB + 1)
                    bank = q % UB
                    for k in range(KT):
                        if q == 0:
                            pe.wait_ge(S["h_ready"], k + 1)
                        if name == "v":
                            n = P if i < 8 else TS
                            to, w, x = ps[0:n, bank, 0:P], m.hT[:, k, i * P:i * P + n], we[:, k, c0:c0 + P]
                        else:
                            x = m.hT[:, k, t * NT:(t + 1) * NT]
                            to, w = (ps[R, bank, 0:NT], we[:, k, c0:c0 + 32]) if name == "kr" else \
                                (ps[:, bank, 0:NT], we[:, k, c0:c0 + P])
                        mm = nc.tensor.matmul(to, w, x, start=k == 0, stop=k == KT - 1)
                    mm.then_inc(S["e_ready"], 1)

                for kind, n in order:
                    if kind == "chunk":
                        chunk(n)
                    elif kind == "turn":
                        turn(n)
                    else:
                        unit(n)

            @block.vector
            def _(dve):
                nc.vector.memset(rows[:], 0.0).then_inc(S["rows_zeroed"], 1)
                nc.vector.memset(m.negs[:], TAKEN)
                dve.wait_ge(S["rel_mm"], 1)
                flat = ps[0:HEADS, 0:3, :].rearrange("p a b -> p (a b)")
                nc.vector.tensor_copy(relrow, flat[:, 0:REL_LEN]).then_inc(S["rel_ev"], 1)
                dve.wait_ge(S["par_loaded"], 16 * len(params))

                def turn(g):
                    dve.wait_ge(S["turned"], g + 1)
                    pick = lambda t: t[:, 8 * g:8 * g + 8].rearrange("p (q j) s -> p q j s", q=2)
                    src = ps[:, 7].rearrange("p (j q s) -> p q j s", j=TILES, q=4)[:, 0:2, :, 0:2]
                    for q in range(2):
                        if g % 3 == 1:
                            ins = nc.vector.scalar_tensor_tensor(pick(m.mods)[:, q], src[:, q], 1.0, pick(bada)[:, q],
                                                                 ALU.add, ALU.add)
                        else:
                            ins = nc.vector.tensor_tensor(pick(m.mods)[:, q], src[:, q], pick(bada)[:, q], ALU.add)
                    ins.then_inc(S["mods_out"], 1)
                    if g == 1:
                        dve.wait_ge(S["mods_out"], 2)
                        dve.wait_ge(S["x_loaded"], 16)
                        for k in range(KT):
                            for s, (a, b) in enumerate(SEQS):
                                ins = nc.vector.tensor_scalar(m.hT[:, k, a:b], m.xT[:, k, a:b], m.mods[:, 8 + k, s:s + 1],
                                                              m.mods[:, k, s:s + 1], ALU.mult, ALU.add)
                            ins.then_inc(S["h_ready"], 1)

                def unit(q):
                    name, j, _, t = units[q]
                    if name != "kr":
                        return
                    if q == rbase:
                        dve.wait_ge(S["caches_loaded"], 16 * len(caches))
                    dve.wait_ge(S["e_ready"], q + 1)
                    bank = q % UB
                    if j == 0:
                        for s, c0, cn in segments(t):
                            to = t * NT + c0 if s == 0 else TP + PAST
                            src = slice(t * NT + c0, t * NT + c0 + cn)
                            ins = nc.vector.tensor_tensor(kpe[R, to:to + cn], ps[R, bank, c0:c0 + cn],
                                                          rope[R, 0, src], ALU.mult)
                    else:
                        src = slice(t * NT, (t + 1) * NT)
                        ins = nc.vector.tensor_tensor(rot[R, src], ps[R, bank, 0:NT], rope[R, 1, src], ALU.mult)
                    ins.then_inc(S["e_roped"], 1)

                for kind, n in order:
                    if kind == "turn":
                        turn(n)
                    elif kind == "unit":
                        unit(n)
                dve.wait_ge(S["e_roped"], 2 * NTOK)
                nc.vector.tensor_tensor(kpe[R, 0:TP], kpe[R, 0:TP], rot[R, 0:TP], ALU.add)
                new = kpe[R, TP + PAST:NKEYS]
                nc.vector.tensor_tensor(new, new, rot[R, TP:N], ALU.add)


def latent_norms(m, lat, kpe, cq, ks, vs, btile, R):
    nc, d, ps = m.nc, m.d, m.ps
    with ExitStack() as c:
        sq = m.sb("sqe", [P, 3, N], c)
        rs = m.sb("rse", [P, 2, N], c)
        S = {n: m.sem("ln_e_" + n) for n in ("squared", "summed", "chain", "inv", "root", "normed", "out", "bias_loaded")}
        with nc.Block() as block:
            @block.sync
            def _(sp):
                sp.dma_start(btile[:], toeplitz(m, TP - P, 256)).then_inc(S["bias_loaded"], 16)
                outs = [(d["kpeT"][:, 0:TP], kpe[R, 0:TP]), (d["kpeT"][:, TP:N], kpe[R, TP + PAST:NKEYS]),
                        (d["swakT"][:, 0:P], ks[:, TP - P:TP]),
                        (d["swakT"][:, P:2 * P], ks[:, TP + TS:SWA_COLS]),
                        (d["swav"][0], vs[:, 7]), (d["swav"][1, 0:P - TS], vs[TS:P, 8]),
                        (d["swav"][1, P - TS:P], vs[0:TS, 9]),
                        (d["latT"][:, 0:TP], lat[:, 0:TP]), (d["latT"][:, TP:N], lat[:, TP + PAST:NKEYS])]
                for i, (to, src) in enumerate(outs):
                    if i == len(outs) - 2:
                        sp.wait_ge(S["normed"], 1)
                    sp.dma_start(to, src).then_inc(S["out"], 16)
                sp.wait_ge(S["out"], 16 * len(outs))

            @block.scalar
            def _(act):
                nc.scalar.activation(sq[:, 2, 0:TP], lat[:, 0:TP], ACT.Square)
                nc.scalar.activation(sq[:, 2, TP:N], lat[:, TP + PAST:NKEYS], ACT.Square).then_inc(S["squared"], 1)
                nc.scalar.activation(sq[:, 0:2], cq[:], ACT.Square).then_inc(S["squared"], 1)
                for i in (1, 0):
                    act.wait_ge(S["inv"], 2 - i)
                    nc.scalar.activation(rs[:, i], rs[:, i], ACT.Sqrt).then_inc(S["root"], 1)

            @block.tensor
            def _(pe):
                for i, srcs in ((1, (2,)), (0, (0, 1))):
                    pe.wait_ge(S["squared"], 2 - i)
                    for t in range(NTOK):
                        for n, j in enumerate(srcs):
                            mm = nc.tensor.matmul(ps[:, i * NTOK + t, 0:NT], m.ones[:], sq[:, j, t * NT:(t + 1) * NT],
                                                  start=n == 0, stop=n == len(srcs) - 1)
                    mm.then_inc(S["summed"], 1)

            @block.vector
            def _(dve):
                chain = Chain(dve, S["chain"])
                chain.link(nc.vector.tensor_scalar(m.gq[:, 0:2], m.gq[:, 0:2], MLA_SCALE, None, ALU.mult))
                for i, factor in ((1, D / 128), (0, D / 256)):
                    dve.wait_ge(S["summed"], 2 - i)
                    for t in range(NTOK):
                        ins = nc.vector.tensor_scalar(rs[:, i, t * NT:(t + 1) * NT], ps[:, i * NTOK + t, 0:NT],
                                                      factor, RMS_EPS, ALU.mult, ALU.add)
                    chain.link(ins)
                    nc.vector.reciprocal(rs[:, i], rs[:, i]).then_inc(S["inv"], 1)
                dve.wait_ge(S["root"], 1)
                for a, b, r0 in ((0, TP, 0), (TP + PAST, NKEYS, TP)):
                    ins = nc.vector.scalar_tensor_tensor(lat[:, a:b], lat[:, a:b], m.gq[:, 2:3],
                                                         rs[:, 1, r0:r0 + b - a], ALU.mult, ALU.mult)
                ins.then_inc(S["normed"], 1)
                dve.wait_ge(S["root"], 2)
                for i in range(2):
                    nc.vector.scalar_tensor_tensor(cq[:, i], cq[:, i], m.gq[:, i:i + 1], rs[:, 0], ALU.mult, ALU.mult)
                dve.wait_ge(S["bias_loaded"], 16)
                nc.vector.memset(btile[0:CHUNK, :, 256 - CHUNK:256], NEG)
                nc.vector.memset(btile[CHUNK:P, :, 0:CHUNK], NEG)


def even_mixer(m):
    d = m.d
    with ExitStack() as outer:
        lat = m.sb("lat", [P, NKEYS], outer)
        kpe = m.sb("kpe", [P, NKEYS], outer)
        cq = m.sb("cq", [P, 2, N], outer)
        rope = m.sb("rope", [P, 2, N], outer)
        R = slice(64, 96)
        with ExitStack() as mid:
            qs = m.sb("qs", [P, 4, N], mid)
            ks = m.sb("ks", [P, SWA_COLS], mid)
            vs = m.sb("vs", [P, 10, P], mid)
            entry_stage(m, lat, kpe, cq, rope, qs, ks, vs, R)

            with ExitStack() as c:
                btile = m.sb("bswa", [P, HEADS, 256], c)
                latent_norms(m, lat, kpe, cq, ks, vs, btile, R)
                blocks = [Keys(b * P, P, [(c0 * P, P, c0) for c0 in range(max(0, b - 1), b + 1)]) for b in range(8)]
                blocks.append(Keys(TP, TS, [(TP, P, 8), (TP + P, TS, 9)], sample=True))

                def rows(u):
                    return slice(64 * u, 64 * u + 64)

                def q_of(t, u, kb):
                    return row(qs[rows(u)], t)[:, kb.q0:kb.q0 + kb.nq]

                def bias_of(h, kb):
                    j0 = 0 if kb.sample or kb.nk == 256 else P
                    return row(btile[0:kb.nq], h)[:, j0:j0 + kb.nk]
                attention_stage(m, "swa", blocks, "swa", q_of,
                                lambda t, u, kb, n0, n1: ks[rows(u), kb.tiles[0][0] + n0:kb.tiles[0][0] + n1],
                                lambda t, u, v, size: vs[0:size, v, 64 * u:64 * u + 64],
                                64, rows, 4, bias_added=bias_of, sink=True)

        with ExitStack() as c:
            q = m.sb("qmla", [96, HEADS, N], c)
            kT = m.sb("kmla", [96, HEADS, N], c)
            v = m.sb("vmla", [P, 9, 512], c)
            for part in range(2):
                with ExitStack() as cc:
                    rot = m.sb(f"rotq{part}", [P, 2, NT], cc)
                    wq = m.sb("wuq", [P, 2, HEADS, P], cc) if part == 0 else None
                    wkv = m.sb(f"wukv{part}", [P, 2, 512], cc)
                    mla_up(m, part, q, kT, v, wq, wkv, cq, lat, kpe, rope, rot, R)
                if part == 0:
                    blocks = [Keys(b * P, P, [(i * P, P, i) for i in range(b + 1)]) for b in range(8)]
                else:
                    blocks = [Keys(TP, TS, [(i * P, P, i) for i in range(8)] + [(TP, TS, 8)], sample=True, wide=True)]
                attention_stage(m, f"mla{part}", blocks, "mla",
                                lambda t, u, kb: row(q[:], t + 4 * u)[:, kb.q0:kb.q0 + kb.nq],
                                lambda t, u, kb, n0, n1: row(kT[:], t + 4 * u)[:, n0:n1],
                                lambda t, u, i, size: v[0:size, i, bass.ds((t + 4 * u) * 64, 64)],
                                64, lambda u: slice(0, 96), 0, osb=cq)
    with ExitStack() as c:
        down_stage(m, "e", d["woe"], m.hT, 0, 0, c)


def mla_up(m, part, q, kT, v, wq, wkv, cq, lat, kpe, rope, rot, R):
    nc, ps, d = m.nc, m.ps, m.d
    names = ("w_loaded", "q_ready", "q_moved", "q_rot", "chain", "k_ready", "k_moved")
    S = {n: m.sem(f"up{part}_{n}") for n in names}
    l0, nk = (0, TP) if part == 0 else (TP, N)
    chunks = [(a, min(nk, a + 512)) for a in range(0, nk, 512)]
    vt = 8 if part == 0 else 9
    nunits = HEADS * NTOK if part == 0 else 0
    kunits = HEADS * len(chunks)
    with nc.Block() as block:
        @block.sync
        def _(sp):
            sp.dma_start(wkv[:], d["wukv"]).then_inc(S["w_loaded"], 16)
            if part == 0:
                sp.dma_start(wq[:], d["wuq"]).then_inc(S["w_loaded"], 16)

        @block.tensor
        def _(pe):
            pe.wait_ge(S["w_loaded"], 32 if part == 0 else 16)
            def query(n):
                h, t = divmod(n, NTOK)
                cols = slice(t * NT, (t + 1) * NT)
                if n >= 2:
                    pe.wait_ge(S["q_moved"], n - 1)
                    pe.wait_ge(S["q_rot"], n - 1)
                for j, (r, w0, w1) in enumerate(((slice(0, 96), 0, 96), (R, 96, 128))):
                    for k in range(2):
                        mm = nc.tensor.matmul(ps[r, 2 * (n % 2) + j, 0:NT], wq[:, k, h, w0:w1], cq[:, k, cols],
                                              start=k == 0, stop=k == 1)
                mm.then_inc(S["q_ready"], 1)

            def key(n):
                if n >= 4:
                    pe.wait_ge(S["k_moved"], n - 3)
                bank = 4 + n % 4
                if n < kunits:
                    h, ci = divmod(n, len(chunks))
                    a, b = chunks[ci]
                    mm = nc.tensor.matmul(ps[0:64, bank, 0:b - a], wkv[:, 0, 64 * h:64 * h + 64],
                                          lat[:, l0 + a:l0 + b], start=True, stop=True)
                else:
                    i = n - kunits
                    rows = min(P, nk - i * P)
                    mm = nc.tensor.matmul(ps[0:rows, bank, :], lat[:, l0 + i * P:l0 + i * P + rows], wkv[:, 1],
                                          start=True, stop=True)
                mm.then_inc(S["k_ready"], 1)

            for n in range(max(nunits, kunits + vt)):
                if n < nunits:
                    query(n)
                if n < kunits + vt:
                    key(n)

        @block.scalar
        def _(act):
            def query(n):
                h, t = divmod(n, NTOK)
                act.wait_ge(S["q_ready"], n + 1)
                act.wait_ge(S["q_rot"], n + 1)
                nc.scalar.activation(q[0:64, h, t * NT:(t + 1) * NT], ps[0:64, 2 * (n % 2), 0:NT], ACT.Copy) \
                    .then_inc(S["q_moved"], 1)

            def key(n):
                act.wait_ge(S["k_ready"], n + 1)
                bank = 4 + n % 4
                if n < kunits:
                    h, ci = divmod(n, len(chunks))
                    a, b = chunks[ci]
                    ins = nc.scalar.activation(kT[0:64, h, a:b], ps[0:64, bank, 0:b - a], ACT.Copy)
                else:
                    i = n - kunits
                    rows = min(P, nk - i * P)
                    ins = nc.scalar.activation(v[0:rows, i], ps[0:rows, bank, :], ACT.Copy)
                ins.then_inc(S["k_moved"], 1)

            for n in range(max(nunits, kunits + vt)):
                if n < kunits + vt:
                    key(n)
                if n < nunits:
                    query(n)

        @block.gpsimd
        def _(pool):
            nc.gpsimd.tensor_copy(kT[R, :, 0:nk], spread(kpe[R, l0:l0 + nk], HEADS))

        @block.vector
        def _(dve):
            chain = Chain(dve, S["chain"])
            for n in range(nunits):
                h, t = divmod(n, NTOK)
                cols = slice(t * NT, (t + 1) * NT)
                dve.wait_ge(S["q_ready"], n + 1)
                nc.vector.tensor_tensor(rot[R, 0], ps[R, 2 * (n % 2), 0:NT], rope[R, 0, cols], ALU.mult)
                chain.link(nc.vector.tensor_tensor(rot[R, 1], ps[R, 2 * (n % 2) + 1, 0:NT], rope[R, 1, cols], ALU.mult))
                nc.vector.tensor_tensor(q[R, h, cols], rot[R, 0], rot[R, 1], ALU.add).then_inc(S["q_rot"], 1)
                dve.wait_ge(S["q_rot"], n + 1)


def odd_mixer(m):
    nc, d = m.nc, m.d
    with ExitStack() as outer:
        qd = m.sb("qd", [P, HEADS, N], outer)
        with ExitStack() as inner:
            kd = m.sb("kd", [P, 2, N], inner)
            ki = m.sb("ki", [P, NKEYS], inner)
            qi = m.sb("qi", [P, 4, N], inner)
            v = m.sb("vd", [P, 9, 256], inner)
            wi = m.sb("wi", [P, 9, HEADS], inner)
            with ExitStack() as c:
                hh = m.sb("hh_odd", [P, KT, N], c, F32R)
                hl = m.sb("hl_odd", [P, KT, N], c, F32R)
                m.hT = qd
                with ExitStack() as cv:
                    wv = m.sb("wov", [P, KT, VW], cv)
                    m.recycle()
                    wv_loaded = m.sem("wov_loaded")
                    norm_stage(m, 0, 1, split=(hh, hl), ahead=[(wv[:], d["wov"], wv_loaded, None, None)])
                    odd_values(m, qd, wv, wv_loaded, v, wi)
                odd_tiles(m, hh, hl, qd, kd, ki, qi, v)

            btile = m.sb("bdsa", [P, HEADS, N], inner)
            prompt = [Keys(b * P, P, [(i * P, P, i) for i in range(b + 1)]) for b in range(8)]
            sample = Keys(TP, TS, [(TP + i * P, P, i) for i in range(8)] + [(TP + PAST, TS, 8)],
                          sample=True, wide=True)
            scores = [m.sb(f"score{i}", [P, N], inner) for i in range(3)]
            sels, units = {}, 0
            for b, kb in enumerate(prompt + [sample]):
                if kb.nk > TOPK:
                    sels[b] = Selection(len(sels), kb, scores, units)
                    units += 8 * len(sels[b].chunks)
            for part in range(2):
                with ExitStack() as c:
                    bl, cl = m.sem(f"bdsa_loaded{part}"), m.sem(f"dsa_cache_loaded{part}")
                    width, j0, rows = (TP, P, P) if part == 0 else (N, 0, TS)
                    if part == 0:
                        keys, values, at = kd, v, 0
                    else:
                        keys, values, at = m.sb("kds", [P, 2, N], c), m.sb("vds", [P, 9, 256], c), TP
                    with nc.Block() as block:
                        @block.sync
                        def _(sp):
                            sp.dma_start(btile[0:rows, :, 0:width], toeplitz(m, j0, width, rows)).then_inc(bl, 16)
                            sp.wait_ge(bl, 16)

                        if part == 1:
                            @block.scalar
                            def _(act):
                                act.dma_start(keys[:, :, 0:PAST], d["c_dsak"]).then_inc(cl, 16)
                                act.dma_start(values[:, 0:8], d["c_dsav"]).then_inc(cl, 16)
                                nc.scalar.activation(keys[:, :, PAST:N], kd[:, :, TP:N], ACT.Copy)
                                nc.scalar.activation(values[0:TS, 8], v[0:TS, 8], ACT.Copy)
                                act.wait_ge(cl, 32)
                    attention_stage(m, f"dsa{part}", prompt if part == 0 else [sample], "dsa",
                                    lambda t, u, kb: row(qd[:], t + 4 * u)[:, kb.q0:kb.q0 + kb.nq],
                                    lambda t, u, kb, n0, n1: keys[:, u, kb.tiles[0][0] - at + n0:kb.tiles[0][0] - at + n1],
                                    lambda t, u, i, size: values[0:size, i, P * u:P * u + P],
                                    P, lambda u: slice(0, P), 0, bias_w=TP if part == 0 else N,
                                    bias_of=lambda h, kb: row(btile[0:kb.nq], h)[:, (0 if kb.sample else 7 * P - kb.q0):][:, 0:kb.nk],
                                    index=dict(q=qi, k=ki, w=wi) if part == 0 else None,
                                    sels=sels if part == 0 else {0: sels[8]}, out=qd)
        down_stage(m, "o", d["woo"], qd, 1, 0, outer)


def odd_values(m, h, wv, loaded, v, wi):
    nc, ps = m.nc, m.ps
    ready, moved = m.sem("v_ready"), m.sem("v_moved")
    with nc.Block() as block:
        @block.tensor
        def _(pe):
            pe.wait_ge(loaded, 16)
            for i in range(9):
                if i >= 4:
                    pe.wait_ge(moved, 2 * (i - 3))
                rows = P if i < 8 else TS
                for k in range(KT):
                    mm = nc.tensor.matmul(ps[0:rows, i % 4, 0:VW], h[:, k, i * P:i * P + rows], wv[:, k],
                                          start=k == 0, stop=k == KT - 1)
                mm.then_inc(ready, 1)

        @block.scalar
        def _(act):
            for i in range(9):
                rows = P if i < 8 else TS
                act.wait_ge(ready, i + 1)
                nc.scalar.activation(v[0:rows, i], ps[0:rows, i % 4, 0:256], ACT.Copy).then_inc(moved, 1)
                nc.scalar.activation(wi[0:rows, i], ps[0:rows, i % 4, 256:VW], ACT.Copy, scale=IDX_W_SCALE) \
                    .then_inc(moved, 1)


def odd_tiles(m, hh, hl, qd, kd, ki, qi, v):
    nc, ps, d = m.nc, m.ps, m.d
    with ExitStack() as c:
        raw = m.sb("wo_raw", [P, 2, KT, P], c)
        wh = m.sb("wo_hi", [P, 2, KT, P], c, F32R)
        wlo = m.sb("wo_lo", [P, 2, KT, P], c, F32R)
        S = {n: m.sem("o_" + n) for n in ("w_hi", "w_lo", "ready", "moved", "c_loaded", "out")}
        loaded = [m.sem(f"wo_loaded{u}") for u in range(2)]
        with nc.Block() as block:
            @block.sync
            def _(sp):
                for j in range(ODD_TILES):
                    if j >= 2:
                        sp.wait_ge(S["w_lo"], j - 1)
                    sp.dma_start(raw[:, j % 2], d["wo"][j]).then_inc(loaded[j % 2], 16)
                sp.wait_ge(S["moved"], NTOK * ODD_TILES)
                outs = [(d["dsakT"], kd[:]), (d["idxT"][:, 0:TP], ki[0:64, 0:TP]),
                        (d["idxT"][:, TP:N], ki[0:64, TP + PAST:NKEYS]),
                        (d["dsav"][:, 0:8], v[:, 0:8]), (d["dsav"][0:TS, 8], v[0:TS, 8])]
                for to, src in outs:
                    sp.dma_start(to, src).then_inc(S["out"], 16)
                sp.wait_ge(S["out"], 16 * len(outs))

            @block.gpsimd
            def _(pool):
                for j in range(ODD_TILES):
                    pool.wait_ge(loaded[j % 2], 16 * (j // 2 + 1))
                    if j >= 2:
                        pool.wait_ge(S["ready"], NTOK * (j - 1))
                    nc.gpsimd.tensor_copy(wh[:, j % 2], raw[:, j % 2]).then_inc(S["w_hi"], 1)

            @block.vector
            def _(dve):
                for j in range(ODD_TILES):
                    dve.wait_ge(S["w_hi"], j + 1)
                    nc.vector.tensor_tensor(wlo[:, j % 2], raw[:, j % 2], wh[:, j % 2].bitcast(F32), ALU.subtract) \
                        .then_inc(S["w_lo"], 1)

            @block.tensor
            def _(pe):
                for j in range(ODD_TILES):
                    pe.wait_ge(S["w_lo"], j + 1)
                    for t in range(NTOK):
                        n = NTOK * j + t
                        if n >= 6:
                            pe.wait_ge(S["moved"], n - 5)
                        for k in range(KT):
                            for i, (w, x) in enumerate(((wh, hh), (wh, hl), (wlo, hh))):
                                mm = nc.tensor.matmul(ps[:, n % 6, 0:NT], w[:, j % 2, k], x[:, k, t * NT:(t + 1) * NT],
                                                      start=k == i == 0, stop=k == KT - 1 and i == 2)
                        mm.then_inc(S["ready"], 1)

            @block.scalar
            def _(act):
                for to in (ki[0:64, TP:TP + PAST], ki[64:P, TP:TP + PAST]):
                    act.dma_start(to, d["c_idx"]).then_inc(S["c_loaded"], 16)
                for j in range(ODD_TILES):
                    for t in range(NTOK):
                        n = NTOK * j + t
                        act.wait_ge(S["ready"], n + 1)
                        cols = slice(t * NT, (t + 1) * NT)
                        if j != 10:
                            to = qd[:, j, cols] if j < 8 else kd[:, j - 8, cols] if j < 10 else qi[:, j - 11, cols]
                            pieces = [(to, 0, NT)]
                        else:
                            pieces = [(ki[:, t * NT + c0:t * NT + c0 + cn] if s == 0 else ki[:, TP + PAST:NKEYS], c0, cn)
                                      for s, c0, cn in segments(t)]
                        for to, c0, cn in pieces:
                            ins = nc.scalar.activation(to, ps[:, n % 6, c0:c0 + cn], ACT.Copy,
                                                       scale=DSA_SCALE if j < 8 else 1.0)
                        ins.then_inc(S["moved"], 1)
                act.wait_ge(S["c_loaded"], 32)


def ffn_with_norms(m, layer):
    with ExitStack() as c:
        hh = m.sb(f"hh{layer}", [P, KT, N], c, F32R)
        hl = m.sb(f"hl{layer}", [P, KT, N], c, F32R)
        raw = m.sb(f"wraw{layer}", [P, 2, KT, P], c)
        wh = m.sb(f"wh{layer}", [P, 2, KT, P], c, F32R)
        wlo = m.sb(f"wlo{layer}", [P, 2, KT, P], c, F32R)
        m.recycle()
        loaded, w_hi = [m.sem(f"w{layer}_loaded{b}") for b in range(2)], m.sem(f"w{layer}_hi")
        with ExitStack() as scratch:
            m.hT = m.sb(f"h_ffn{layer}", [P, KT, N], scratch)
            norm_stage(m, layer, 0, split=(hh, hl),
                       ahead=[(raw[:, b], m.d["wfi"][layer, 0, :, b], loaded[b], wh[:, b], w_hi) for b in range(2)])
        ffn_stage(m, layer, hh, hl, (raw, wh, wlo, loaded, w_hi), c)


def build_program(nc, dram):
    with ExitStack() as ctx:
        m = Machine(nc, ctx, dram)
        with ExitStack() as c:
            m.hT = m.sb("h_even", [P, KT, N], c)
            even_mixer(m)
        ffn_with_norms(m, 0)
        odd_mixer(m)
        ffn_with_norms(m, 1)
        with ExitStack() as c:
            m.hT = m.sb("squares", [P, KT, N], c)
            norm_stage(m, 1, 1, final=True)
        stored = m.sem("conv_stored")
        with nc.Block() as block:
            @block.sync
            def _(sp):
                sp.dma_start(dram["convo"], m.convo[:]).then_inc(stored, 16)
                sp.wait_ge(stored, 16)


def shape_constants():
    pos = np.arange(N, dtype=np.float32)
    half = np.arange(16, dtype=np.float32)
    inv = np.power(np.float64(10000.0), -(half / np.float32(16)).astype(np.float64)).astype(np.float32)
    ang = (pos[None, :] * inv[:, None]).astype(np.float32).astype(np.float64)
    cos, sin = np.cos(ang).astype(np.float32), np.sin(ang).astype(np.float32)
    rope = np.stack([np.concatenate([cos, cos]), np.concatenate([-sin, sin])], axis=1)
    rel = np.arange(REL_LEN) - REL_BASE
    n = np.abs(rel)
    large = 8 + (np.log(np.maximum(n, 1).astype(np.float32) / np.float32(8)) / np.float32(np.log(128.0))
                 * np.float32(8)).astype(np.int32)
    bucket = np.where(rel > 0, 16, 0) + np.where(n < 8, n, np.minimum(large, 15))
    onehot = (np.arange(32)[:, None] == bucket[None, :]).astype(np.float32)
    return dict(rope=rope, onehot=onehot, ident=np.eye(P, dtype=np.float32),
                ones=np.full((P, P), 1.0 / D, np.float32))


def tiles_of(w, columns):
    w = w[:, columns]
    rows, cols = w.shape
    return np.ascontiguousarray(w.reshape(rows // P, P, cols // P, P).transpose(2, 1, 0, 3))


def by_partition(a):
    return np.moveaxis(a.reshape(a.shape[:-1] + (-1, P)), -1, 0)


def kernel(**inputs):
    import concourse.bacc as bacc
    from concourse.bass_utils import run_bass_kernel_spmd

    i = {k: np.asarray(v) for k, v in inputs.items()}
    a = dict(shape_constants())
    a["xT"] = np.concatenate([i["x_prompt"][0], i["x_sample"][0]]).T.reshape(KT, P, N).transpose(1, 0, 2)
    a["cT"] = np.stack([i["c_prompt"][0], i["c_sample"][0]]).T.reshape(KT, P, 2).transpose(1, 0, 2)
    wada = i["w_ada"].reshape(2, 2, KT // 2, P, 12, 512)
    a["wada"] = wada.transpose(0, 4, 1, 3, 2, 5).reshape(48, P, KT // 2, 512)
    a["bada"] = np.repeat(by_partition(i["b_ada"]).reshape(P, 96, 1), 2, axis=2)
    a["lnp"] = np.stack([by_partition(i[n]) for n in ("ln_mix_g", "ln_mix_b", "ln_ffn_g", "ln_ffn_b")], axis=2)
    a["rel_bias"] = i["rel_bias"]
    a["sinks"] = np.broadcast_to(i["swa_sinks"][0], (P, HEADS))
    a["gq"] = np.concatenate([i["g_q_lora"][0].reshape(2, P), i["g_kv_lora"][0].reshape(1, P)]).T

    kr = np.arange(384, 416)
    qs = 416 + np.concatenate([np.r_[t * 64:t * 64 + 64, (t + 4) * 64:(t + 4) * 64 + 64] for t in range(4)])
    cols = np.concatenate([np.arange(384), np.arange(928, 1056), qs, np.arange(1056, 1184), kr, np.roll(kr, 16)])
    a["we"] = i["w_in_even"][0][:, cols].reshape(KT, P, EVEN_W).transpose(1, 0, 2)
    uq = i["w_uq"][0].reshape(2, P, HEADS, 96)
    a["wuq"] = np.concatenate([uq, np.roll(uq[..., 64:], 16, axis=-1)], axis=-1).transpose(1, 0, 2, 3)
    ukv = i["w_ukv"][0].reshape(P, HEADS, 2, 64)
    a["wukv"] = ukv.transpose(0, 2, 1, 3).reshape(P, 2, 512)
    a["woe"] = tiles_of(i["w_out_even"][0], slice(None))

    cols = np.concatenate([np.arange(1280), np.arange(2048, 2112), np.arange(2048, 2112), np.arange(1536, 2048)])
    a["wo"] = tiles_of(i["w_in_odd"][0], cols)
    a["wov"] = i["w_in_odd"][0][:, np.r_[1280:1536, 2112:2120]].reshape(KT, P, VW).transpose(1, 0, 2)
    a["woo"] = tiles_of(i["w_out_odd"][0], slice(None))

    wfi = np.stack([tiles_of(i["ffn_w_in"][l], slice(None)) for l in range(2)])
    a["wfi"] = wfi.reshape(2, 2, FT, P, KT, P).transpose(0, 2, 3, 1, 4, 5)
    a["wfo"] = np.stack([tiles_of(i["ffn_w_out"][l], slice(None)) for l in range(2)])
    taps = np.concatenate([i["ffn_conv_w"], i["ffn_conv_b"][:, None]], axis=1)
    a["convp"] = taps.reshape(2, 4, 2, FT, P).transpose(4, 0, 3, 2, 1).reshape(P, 2, FT, 8)
    state = i["state_ffn_conv"][:, 0]
    a["convs"] = state.reshape(2, 2, 2, FT, P).transpose(4, 0, 3, 2, 1).reshape(P, 2, FT, 4)

    a["c_lat"] = i["cache_mla_latent"][0, 0].T
    a["c_kpe"] = i["cache_mla_kpe"][0, 0].T
    a["c_swak"] = i["cache_swa_k"][0, 0].reshape(P, P).T
    a["c_swav"] = i["cache_swa_v"][0, 0].reshape(P, P)
    a["c_dsak"] = i["cache_dsa_k"][0, 0].transpose(2, 1, 0)
    a["c_dsav"] = i["cache_dsa_v"][0, 0].reshape(8, P, 256).transpose(1, 0, 2)
    a["c_idx"] = i["cache_dsa_idx_k"][0, 0].T
    a = {k: np.ascontiguousarray(v) for k, v in a.items()}

    outs = dict(yT=(P, KT, N), latT=(P, N), kpeT=(32, N), swakT=(P, 2 * P), swav=(2, P, P), dsakT=(P, 2, N),
                dsav=(P, 9, 256), idxT=(64, N), convo=(P, 2, FT, 8))
    nc = bacc.Bacc("TRN2", target_bir_lowering=False, num_devices=1)
    dram = {k: nc.dram_tensor(f"in_{k}", v.shape, F32, kind="ExternalInput").ap() for k, v in a.items()}
    for k, shape in outs.items():
        dram[k] = nc.dram_tensor(f"out_{k}", shape, F32, kind="ExternalOutput").ap()
    build_program(nc, dram)
    r = run_bass_kernel_spmd(nc, [{f"in_{k}": v for k, v in a.items()}], core_ids=[0]).results[0]
    o = {k: np.asarray(r[f"out_{k}"]) for k in outs}

    y = o["yT"].transpose(2, 1, 0).reshape(N, D)
    lat, kpe = o["latT"].T, o["kpeT"].T
    swak = o["swakT"].T.reshape(2, 1, 1, P, 2, 64)
    swav = o["swav"].reshape(2, 1, 1, P, 2, 64)
    dk = o["dsakT"].transpose(2, 1, 0)
    dv = o["dsav"].transpose(1, 0, 2).reshape(9 * P, 2, P)[:N]
    di = o["idxT"].T
    cv = o["convo"].reshape(P, 2, FT, 2, 2, 2).transpose(3, 1, 5, 4, 2, 0).reshape(2, 2, 1, 2, 2 * FF)
    both = [slice(0, TP), slice(TP, N)]
    group = [[lat[s][None, None], kpe[s][None, None], swak[n], swav[n], dk[s][None, None], dv[s][None, None],
              di[s][None, None], cv[n]] for n, s in enumerate(both)]
    return tuple(np.ascontiguousarray(x) for x in [y[both[0]][None], y[both[1]][None], *group[0], *group[1]])
```
